# Optimizing a Trainium2 kernel written in Bass

```python
import numpy as np
import jax, jax.numpy as jnp
from jax import lax

D_MODEL = 1024
BATCH = 1
SEQ = 256
DEPTH = 1
DEC_BATCH = 1
DEC_SEQ = 2048
PAST_LEN = 256

GRID_W = 64
GLA_HEADS = 4
GLA_DK = 64
GLA_DV = 128
GLA_LOWRANK = 16
GLA_GATE_NORM = 16.0
GLA_CHUNK = 64
ATT_HEADS = 8
ATT_KV_HEADS = 2
HEAD_DIM = 64
ROPE_AXIS_DIM = HEAD_DIM // 2
ROPE_THETA = 10000.0
Q_BLOCK = 128
D_FF = -(-8 * D_MODEL // (3 * 256)) * 256
N_MOD = 6
EPS = 1e-6
SPLIT_SIZES = (GLA_HEADS * GLA_DK, GLA_HEADS * GLA_DK, GLA_HEADS * GLA_DV, GLA_HEADS * GLA_DV,
               2 * GLA_LOWRANK, ATT_HEADS * HEAD_DIM, ATT_KV_HEADS * HEAD_DIM, ATT_KV_HEADS * HEAD_DIM)
D_IN_PROJ = sum(SPLIT_SIZES)
D_MIX = GLA_HEADS * GLA_DV + ATT_HEADS * HEAD_DIM

kernel_name = 'hybrid_gla_gqa_prefix_dit_step'

F32 = jnp.float32

def rms_norm(x, g):
    xf = x.astype(F32)
    y = xf * lax.rsqrt(jnp.mean(xf * xf, axis=-1, keepdims=True) + EPS)
    return (y * g.astype(F32)).astype(x.dtype)

def adaln_params(cond, ada_w, ada_b):
    mod = jax.nn.silu(cond) @ ada_w + ada_b
    return jnp.split(mod, N_MOD, axis=-1)

def modulate(h, shift, scale):
    return h * (1.0 + scale[:, None, :]) + shift[:, None, :]

def axial_rope_tables(T):
    rows = T // GRID_W
    row = jnp.repeat(jnp.arange(rows, dtype=F32), GRID_W)
    col = jnp.tile(jnp.arange(GRID_W, dtype=F32), rows)
    inv = ROPE_THETA ** (-jnp.arange(0, ROPE_AXIS_DIM, 2, dtype=F32) / ROPE_AXIS_DIM)
    ang = jnp.stack([row[:, None] * inv, col[:, None] * inv], axis=1)
    return jnp.cos(ang), jnp.sin(ang)

def apply_axial_rope(x, cos, sin):
    B, T, H, Dh = x.shape
    xr = x.reshape(B, T, H, 2, 2, ROPE_AXIS_DIM // 2).astype(F32)
    x1, x2 = xr[..., 0, :], xr[..., 1, :]
    c, s = cos[None, :, None], sin[None, :, None]
    out = jnp.stack([x1 * c - x2 * s, x1 * s + x2 * c], axis=-2)
    return out.reshape(B, T, H, Dh).astype(x.dtype)

def gla_chunked(q, k, v, g, s0):
    B, T, H, DK = q.shape
    DV = v.shape[-1]
    n = T // GLA_CHUNK
    q = q.astype(F32).reshape(B, n, GLA_CHUNK, H, DK) * (DK ** -0.5)
    k = k.astype(F32).reshape(B, n, GLA_CHUNK, H, DK)
    v = v.astype(F32).reshape(B, n, GLA_CHUNK, H, DV)
    b = jnp.cumsum(g.astype(F32).reshape(B, n, GLA_CHUNK, H, DK), axis=2)
    b_last = b[:, :, -1:]
    q_t = q * jnp.exp(b)
    k_t = k * jnp.exp(-b)
    k_e = k * jnp.exp(b_last - b)
    mask = jnp.tril(jnp.ones((GLA_CHUNK, GLA_CHUNK), dtype=bool))
    a = jnp.where(mask, jnp.einsum('bnihd,bnjhd->bnhij', q_t, k_t), 0.0)
    o_intra = jnp.einsum('bnhij,bnjhv->bnihv', a, v)
    u = jnp.einsum('bnjhd,bnjhv->bnhdv', k_e, v)
    decay = jnp.exp(b_last[:, :, 0])

    def step(s, inp):
        d, uu = inp
        return d[..., None] * s + uu, s

    s_fin, s_prev = lax.scan(step, s0.astype(F32), (jnp.moveaxis(decay, 1, 0), jnp.moveaxis(u, 1, 0)))
    s_prev = jnp.moveaxis(s_prev, 0, 1)
    o_inter = jnp.einsum('bnihd,bnhdv->bnihv', q_t, s_prev)
    return (o_intra + o_inter).reshape(B, T, H, DV), s_fin

def blocked_attention(q, k, v):
    B, T, H, Dh = q.shape
    Hkv = k.shape[2]
    G = H // Hkv
    nb = T // Q_BLOCK
    qb = jnp.moveaxis(q.reshape(B, nb, Q_BLOCK, Hkv, G, Dh), 1, 0) * (Dh ** -0.5)

    def one_block(qi):
        s = jnp.einsum('bqhgd,bkhd->bhgqk', qi.astype(F32), k.astype(F32))
        p = jax.nn.softmax(s, axis=-1)
        return jnp.einsum('bhgqk,bkhd->bqhgd', p, v.astype(F32))

    o = lax.map(one_block, qb)
    return jnp.moveaxis(o, 0, 1).reshape(B, T, H * Dh).astype(q.dtype)

def mixer(h, rope, ctx_kv, s_f0, s_b0, w_in, w_gk2, b_gk2, gla_g, q_g, k_g, w_out):
    B, T, _ = h.shape
    offs = np.cumsum(SPLIT_SIZES)[:-1].tolist()
    qg, kg, vg, og, lr, qa, ka, va = jnp.split(h @ w_in, offs, axis=-1)
    qg = qg.reshape(B, T, GLA_HEADS, GLA_DK)
    kg = kg.reshape(B, T, GLA_HEADS, GLA_DK)
    vg = vg.reshape(B, T, GLA_HEADS, GLA_DV)
    gk = jnp.einsum('btrl,rlk->btrk', lr.reshape(B, T, 2, GLA_LOWRANK), w_gk2) + b_gk2
    gk = (jax.nn.log_sigmoid(gk.astype(F32)) / GLA_GATE_NORM).reshape(B, T, 2, GLA_HEADS, GLA_DK)
    o_f, s_f = gla_chunked(qg, kg, vg, gk[:, :, 0], s_f0)
    o_b, s_b = gla_chunked(qg[:, ::-1], kg[:, ::-1], vg[:, ::-1], gk[:, ::-1, 1], s_b0)
    o_gla = rms_norm(o_f + o_b[:, ::-1], gla_g).astype(h.dtype)
    o_gla = (o_gla * jax.nn.silu(og.reshape(B, T, GLA_HEADS, GLA_DV))).reshape(B, T, GLA_HEADS * GLA_DV)
    qa = rms_norm(qa.reshape(B, T, ATT_HEADS, HEAD_DIM), q_g)
    ka = rms_norm(ka.reshape(B, T, ATT_KV_HEADS, HEAD_DIM), k_g)
    va = va.reshape(B, T, ATT_KV_HEADS, HEAD_DIM)
    if rope is None:
        keys, vals = ka, va
    else:
        qa = apply_axial_rope(qa, *rope)
        ka = apply_axial_rope(ka, *rope)
        ck, cv = ctx_kv
        keys = jnp.concatenate([ka, ck.astype(ka.dtype)], axis=1)
        vals = jnp.concatenate([va, cv.astype(va.dtype)], axis=1)
    o_att = blocked_attention(qa, keys, vals)
    out = jnp.concatenate([o_gla, o_att], axis=-1) @ w_out
    return out, ka, va, s_f, s_b

def swiglu(h, w1, w3, w2):
    return (jax.nn.silu(h @ w1) * (h @ w3)) @ w2

def block(x, cond, rope, ctx_kv, s_f0, s_b0, ada_w, ada_b, n1, n2, w_in, w_gk2, b_gk2,
          gla_g, q_g, k_g, w_out, w1, w3, w2):
    sh1, sc1, g1, sh2, sc2, g2 = adaln_params(cond, ada_w, ada_b)
    h = modulate(rms_norm(x, n1), sh1, sc1)
    out, k, v, s_f, s_b = mixer(h, rope, ctx_kv, s_f0, s_b0, w_in, w_gk2, b_gk2, gla_g, q_g, k_g, w_out)
    x = x + g1[:, None, :] * out
    h = modulate(rms_norm(x, n2), sh2, sc2)
    x = x + g2[:, None, :] * swiglu(h, w1, w3, w2)
    return x, k, v, s_f, s_b

def setup_inputs(seed: int = 0) -> dict:
    key = jax.random.key(seed)
    ks = jax.random.split(key, 24)
    nrm = jax.random.normal
    D = D_MODEL
    return {
        'x_prompt': nrm(ks[0], (BATCH, SEQ, D), F32),
        'x_sample': nrm(ks[1], (DEC_BATCH, DEC_SEQ, D), F32),
        'cache_k': nrm(ks[2], (DEC_BATCH, DEPTH, PAST_LEN, ATT_KV_HEADS, HEAD_DIM), F32),
        'cache_v': nrm(ks[3], (DEC_BATCH, DEPTH, PAST_LEN, ATT_KV_HEADS, HEAD_DIM), F32),
        'state_gla_fwd': nrm(ks[4], (DEC_BATCH, DEPTH, GLA_HEADS, GLA_DK, GLA_DV), F32),
        'state_gla_bwd': nrm(ks[5], (DEC_BATCH, DEPTH, GLA_HEADS, GLA_DK, GLA_DV), F32),
        'c': nrm(ks[6], (DEC_BATCH, D), F32),
        'c_ctx': nrm(ks[7], (D,), F32),
        'ada_w': nrm(ks[8], (DEPTH, D, N_MOD * D), F32) * D ** -0.5,
        'ada_b': nrm(ks[9], (DEPTH, N_MOD * D), F32) * 0.02,
        'norm1_g': 1.0 + 0.02 * nrm(ks[10], (DEPTH, D), F32),
        'norm2_g': 1.0 + 0.02 * nrm(ks[11], (DEPTH, D), F32),
        'w_in': nrm(ks[12], (DEPTH, D, D_IN_PROJ), F32) * D ** -0.5,
        'w_gk2': nrm(ks[13], (DEPTH, 2, GLA_LOWRANK, GLA_HEADS * GLA_DK), F32) * GLA_LOWRANK ** -0.5,
        'b_gk2': nrm(ks[14], (DEPTH, 2, GLA_HEADS * GLA_DK), F32) * 0.1,
        'gla_norm_g': 1.0 + 0.02 * nrm(ks[15], (DEPTH, GLA_DV), F32),
        'q_norm_g': 1.0 + 0.02 * nrm(ks[16], (DEPTH, HEAD_DIM), F32),
        'k_norm_g': 1.0 + 0.02 * nrm(ks[17], (DEPTH, HEAD_DIM), F32),
        'w_out': nrm(ks[18], (DEPTH, D_MIX, D), F32) * D_MIX ** -0.5,
        'w_ffn1': nrm(ks[19], (DEPTH, D, D_FF), F32) * D ** -0.5,
        'w_ffn3': nrm(ks[20], (DEPTH, D, D_FF), F32) * D ** -0.5,
        'w_ffn2': nrm(ks[21], (DEPTH, D_FF, D), F32) * D_FF ** -0.5,
        'final_g': 1.0 + 0.02 * nrm(ks[22], (D,), F32),
    }

def reference(x_prompt, x_sample, cache_k, cache_v, state_gla_fwd, state_gla_bwd, c, c_ctx,
              ada_w, ada_b, norm1_g, norm2_g, w_in, w_gk2, b_gk2, gla_norm_g, q_norm_g, k_norm_g,
              w_out, w_ffn1, w_ffn3, w_ffn2, final_g):
    B = x_prompt.shape[0]
    T = x_sample.shape[1]
    rope = axial_rope_tables(T)
    zero_state = jnp.zeros((B, GLA_HEADS, GLA_DK, GLA_DV), F32)
    cond_ctx = jnp.broadcast_to(c_ctx[None, :], (B, D_MODEL))
    xc, xl = x_prompt, x_sample
    ks_new, vs_new, sf_new, sb_new = [], [], [], []
    for l in range(DEPTH):
        lw = (ada_w[l], ada_b[l], norm1_g[l], norm2_g[l], w_in[l], w_gk2[l], b_gk2[l],
              gla_norm_g[l], q_norm_g[l], k_norm_g[l], w_out[l], w_ffn1[l], w_ffn3[l], w_ffn2[l])
        xc, k_c, v_c, s_f, s_b = block(xc, cond_ctx, None, None, zero_state, zero_state, *lw)
        ks_new.append(k_c)
        vs_new.append(v_c)
        sf_new.append(s_f)
        sb_new.append(s_b)
        xl, _, _, _, _ = block(xl, c, rope, (cache_k[:, l], cache_v[:, l]),
                               state_gla_fwd[:, l], state_gla_bwd[:, l], *lw)
    y_prompt = rms_norm(xc, final_g)
    y_sample = rms_norm(xl, final_g)
    new_cache_k = jnp.stack(ks_new, axis=1)
    new_cache_v = jnp.stack(vs_new, axis=1)
    new_state_gla_fwd = jnp.stack(sf_new, axis=1)
    new_state_gla_bwd = jnp.stack(sb_new, axis=1)
    return (y_prompt, y_sample, new_cache_k, new_cache_v, new_state_gla_fwd, new_state_gla_bwd)


_drawn_inputs = setup_inputs


def setup_inputs(seed=0):
    import zlib

    import numpy as np

    out = dict(_drawn_inputs(seed))
    spreads = {}
    factors = {'cache_k': 8.0,
     'cache_v': 8.0,
     'state_gla_fwd': 42.384,
     'state_gla_bwd': 41.289,
     'norm1_g': 3.301,
     'norm2_g': 12.319,
     'gla_norm_g': 7.974,
     'q_norm_g': 8.0,
     'k_norm_g': 8.142,
     'final_g': 7.956}
    for name, (base, spread) in spreads.items():
        noise = np.random.default_rng([zlib.crc32(name.encode()), seed]).standard_normal(out[name].shape)
        drawn = base * np.exp(spread * noise) if base else spread * noise
        out[name] = __import__('jax').numpy.asarray(drawn.astype(out[name].dtype))
    for name, factor in factors.items():
        out[name] = (out[name] * factor).astype(out[name].dtype)
    return out
```

```python
from contextlib import ExitStack

import numpy as np

import concourse.bass as bass
from concourse import mybir

F32 = mybir.dt.float32
F32R = mybir.dt.float32r
U32 = mybir.dt.uint32
ALU = mybir.AluOpType
ACT = mybir.ActivationFunctionType
AX = mybir.AxisListType

P = 128
D_MODEL = 1024
KC = D_MODEL // P
T_LAT = 2048
T_CTX = 256
PAST = 256
N_LAT = T_LAT // P
N_CTX = T_CTX // P
NT = N_LAT + N_CTX
GH = 4
DK = 64
DV = 128
LR = 16
AH = 8
KVH = 2
HD = 64
D_GLA = 2 * GH * DK + 2 * GH * DV + 2 * LR
D_ATT = AH * HD + 2 * KVH * HD
D_FF = 2816
NF = D_FF // P
EPS = 1e-6
CH = 64
N_MOD = 6
GRID_W = 64
LAT_SLOTS = T_LAT // CH + 2
CTX_SLOTS = T_CTX // CH + 2
SLOTS = LAT_SLOTS + CTX_SLOTS


def wait(eng, sem, value):
    if not (isinstance(value, int) and value <= 0):
        eng.wait_ge(sem, value)


class Step:

    def __init__(self, half, par, static):
        self.half, self.par, self.static = half, par, static

    def at(self, off):
        t = 2 * self.half + self.par - off if self.static else self.half * 2 + (self.par - off)
        if self.static:
            return (t, t // 2, t % 2) if 0 <= t < NT else None
        return t, self.half + (self.par - off) // 2, (self.par - off) % 2


def steps(eng, depth, body):
    first = (depth + 2) // 2
    for u in range(2 * first):
        body(Step(u // 2, u % 2, True))
    with eng.Fori(first, N_LAT // 2) as i:
        for par in range(2):
            body(Step(i, par, False))
    for u in range(N_LAT, NT + depth):
        body(Step(u // 2, u % 2, True))


def cond_of(t):
    return 1 if isinstance(t, int) and t >= N_LAT else 0


def bc(ap, axis, n):
    a = ap.unsqueeze(axis)
    shape = list(a.shape)
    shape[axis] = n
    return a.to_broadcast(shape)


class Names:
    pass


class Phase:

    def __init__(self, nc, stack, name):
        self.nc, self.stack, self.name = nc, stack, name
        self.s = Names()
        self.handles = []
        stack.callback(self.clear)

    def semaphores(self, names):
        new = [self.nc.alloc_semaphore(name=f"{self.name}_{n}") for n in names.split()]
        self.handles += new
        return new

    def clear(self):
        self.nc.clear_and_free_semaphores(self.handles)
        self.nc.all_engine_barrier()

    def sb(self, name, shape, dt=F32):
        return self.stack.enter_context(self.nc.sbuf_tensor(f"{self.name}_{name}", shape, dt))

    def ps(self, name, cols=512):
        return self.stack.enter_context(self.nc.psum_tensor(f"{self.name}_{name}", [P, cols], F32))


def modulation(nc, g):
    NCH = N_MOD * D_MODEL // 512
    with ExitStack() as stack:
        ph = Phase(nc, stack, "mod")
        s = ph.s
        (s.rows, s.w0, s.w1, s.silu, s.tr, s.cT, s.acc, s.bias, s.out, s.back, s.mtr, s.mT, s.done) = ph.semaphores(
            "rows w0 w1 silu tr cT acc bias out back mtr mT done")
        s.w = [s.w0, s.w1]
        crow = ph.sb("crow", [2 * KC, P])
        nrow = ph.sb("nrow", [2 * KC, P])
        srow = ph.sb("srow", [2 * KC, P])
        adab = ph.sb("adab", [2, N_MOD * D_MODEL])
        mod = ph.sb("mod", [2, N_MOD * D_MODEL])
        aw = ph.sb("aw", [P, 2, KC, 512])
        cT = ph.sb("cT", [P, 2 * KC])
        nT = ph.sb("nT", [P, 2 * KC])
        modr = ph.sb("modr", [2 * N_MOD * KC, P])
        modT = ph.sb("modT", [P, 2, N_MOD, KC])
        p_tr = ph.ps("p_tr")
        p_acc = [ph.ps("p_acc0"), ph.ps("p_acc1")]
        ada_w = g.ada_w.rearrange("l (k p) n -> p (l k) n", p=P)

        with nc.Block() as block:

            @block.sync
            def _(sp):
                sp.dma_start(g.ident[:, :], g.d_ident).then_inc(s.rows, 16)
                sp.dma_start(crow[0:KC, :], g.c.rearrange("a (k p) -> (a k) p", p=P)).then_inc(s.rows, 16)
                sp.dma_start(crow[KC:2 * KC, :], g.c_ctx.rearrange("(k p) -> k p", p=P)).then_inc(s.rows, 16)
                sp.dma_start(nrow[0:KC, :], g.norm1_g.rearrange("l (k p) -> (l k) p", p=P)).then_inc(s.rows, 16)
                sp.dma_start(nrow[KC:2 * KC, :], g.norm2_g.rearrange("l (k p) -> (l k) p", p=P)).then_inc(s.rows, 16)
                for r in range(2):
                    sp.dma_start(adab[r:r + 1, :], g.ada_b).then_inc(s.rows, 16)
                for n in range(2):
                    sp.dma_start(aw[:, n], ada_w[:, :, n * 512:(n + 1) * 512]).then_inc(s.w[n], 16)
                with sp.Fori(1, NCH // 2) as i:
                    for par in range(2):
                        sp.wait_ge(s.acc, i * 2 + (par - 1))
                        sp.dma_start(aw[:, par], ada_w[:, :, bass.ds(i * 1024 + par * 512, 512)]).then_inc(s.w[par], 16)
                sp.wait_ge(s.bias, NCH)
                sp.dma_start(g.mod_d, mod[:, :]).then_inc(s.out, 16)
                sp.wait_ge(s.out, 16)
                sp.dma_start(modr[:, :], g.mod_d.rearrange("c (j p) -> (c j) p", p=P)).then_inc(s.back, 16)

            @block.scalar
            def _(act):
                act.wait_ge(s.rows, 16 * 7)
                act.activation(srow[:, :], crow[:, :], ACT.Silu).then_inc(s.silu, 1)

            @block.tensor
            def _(pe):
                pe.wait_ge(s.silu, 1)
                pe.transpose(p_tr[:, 0:2 * KC], srow[:, :], g.ident[0:2 * KC, 0:2 * KC])
                pe.transpose(p_tr[:, 2 * KC:4 * KC], nrow[:, :], g.ident[0:2 * KC, 0:2 * KC]).then_inc(s.tr, 1)
                pe.wait_ge(s.cT, 1)

                def chunk(n, half, par):
                    pe.wait_ge(s.w[par], (half + 1) * 16)
                    wait(pe, s.bias, n - 1)
                    for k in range(KC):
                        last = pe.matmul(p_acc[par][0:2, :], cT[:, k::KC], aw[:, par, k, :], start=k == 0, stop=k == KC - 1)
                    last.then_inc(s.acc, 1)

                chunk(0, 0, 0)
                chunk(1, 0, 1)
                with pe.Fori(1, NCH // 2) as i:
                    for par in range(2):
                        chunk(i * 2 + par, i, par)
                pe.wait_ge(s.back, 16)
                pe.transpose(p_tr[:, 64:64 + 2 * N_MOD * KC], modr[:, :], g.ident[0:96, 0:96]).then_inc(s.mtr, 1)

            @block.vector
            def _(dve):
                dve.memset(g.neg_half[:, :], -0.5)
                dve.wait_ge(s.tr, 1)
                dve.tensor_copy(nT[:, :], p_tr[:, 2 * KC:4 * KC])
                dve.tensor_copy(cT[:, :], p_tr[:, 0:2 * KC]).then_inc(s.cT, 1)
                with dve.Fori(0, NCH // 2) as i:
                    for par in range(2):
                        dve.wait_ge(s.acc, i * 2 + (par + 1))
                        cols = bass.ds(i * 1024 + par * 512, 512)
                        dve.tensor_tensor(mod[:, cols], p_acc[par][0:2, :], adab[:, cols], ALU.add).then_inc(s.bias, 1)
                dve.wait_ge(s.mtr, 1)
                dve.tensor_copy(modT[:, :, :, :], p_tr[:, 64:64 + 2 * N_MOD * KC].rearrange("p (c m k) -> p c m k", c=2, m=N_MOD)).then_inc(s.mT, 1)
                dve.wait_ge(s.mT, 1)
                for n in range(2):
                    for c in range(2):
                        dve.scalar_tensor_tensor(g.lnp[:, n, c, 0, :], modT[:, c, 3 * n + 1, :], 1.0,
                                                 nT[:, n * KC:(n + 1) * KC], ALU.add, ALU.mult)
                        last = dve.tensor_copy(g.lnp[:, n, c, 1, :], modT[:, c, 3 * n, :])
                last.then_inc(s.done, 1)
                dve.wait_ge(s.done, 1)


class Front:

    def __init__(self, ph, s, g, norm, used):
        self.s, self.g, self.norm, self.used = s, g, norm, used
        (s.x0, s.x1, s.sq, s.ms, s.rstd, s.xn, s.tr, s.hT, s.hi, s.split) = ph.semaphores("x0 x1 sq ms rstd xn tr hT hi split")
        self.x = ph.sb("x", [P, 2, D_MODEL])
        self.junk = ph.sb("junk", [P, D_MODEL])
        self.ss = ph.sb("ss", [P, 2, 1])
        self.ms = ph.sb("ms", [P, 2, 1])
        self.rstd = ph.sb("rstd", [P, 2, 1])
        self.hT = ph.sb("hT", [P, KC, P])
        self.hi = ph.sb("hi", [P, 2, KC, P], F32R)
        self.lo = ph.sb("lo", [P, 2, KC, P], F32R)
        self.p_tr = ph.ps("p_tr", 1024)

    def load(self, sp, T):
        t, half, par = T
        wait(sp, self.s.tr, t - 1)
        src = self.g.x_tile(t)
        sp.dma_start(self.x[:, par, :], src).then_inc([self.s.x0, self.s.x1][par], 16)

    def squares(self, act, T):
        t, half, par = T
        act.wait_ge([self.s.x0, self.s.x1][par], (half + 1) * 16)
        wait(act, self.s.sq, t)
        act.activation(self.junk[:, :], self.x[:, par, :], ACT.Square, accum_out=self.ss[:, par, :]).then_inc(self.s.sq, 1)

    def normalise(self, dve, T):
        t, half, par = T
        dve.wait_ge(self.s.sq, t + 1)
        dve.tensor_scalar(self.ms[:, par, :], self.ss[:, par, :], 1.0 / D_MODEL, EPS, ALU.mult, ALU.add).then_inc(self.s.ms, 1)
        dve.wait_ge(self.s.rstd, t + 1)
        dve.tensor_scalar(self.x[:, par, :], self.x[:, par, :], self.rstd[:, par, :], None, ALU.mult).then_inc(self.s.xn, 1)

    def root(self, pool, T):
        t, half, par = T
        pool.wait_ge(self.s.ms, t + 1)
        pool.tensor_tensor(self.rstd[:, par, :], self.ms[:, par, :], self.g.neg_half[:, 0:1], ALU.pow).then_inc(self.s.rstd, 1)

    def transpose(self, pe, T):
        t, half, par = T
        pe.wait_ge(self.s.xn, t + 1)
        wait(pe, self.s.hT, t)
        for k in range(KC):
            last = pe.transpose(self.p_tr[:, k * P:(k + 1) * P], self.x[:, par, k * P:(k + 1) * P], self.g.ident[:, :])
        last.then_inc(self.s.tr, 1)

    def modulate(self, act, T):
        t, half, par = T
        act.wait_ge(self.s.tr, t + 1)
        wait(act, self.s.split, t)
        c = cond_of(t)
        for k in range(KC):
            last = act.activation(self.hT[:, k, :], self.p_tr[:, k * P:(k + 1) * P], ACT.Identity,
                                  bias=self.g.lnp[:, self.norm, c, 1, k:k + 1], scale=self.g.lnp[:, self.norm, c, 0, k:k + 1])
        last.then_inc(self.s.hT, 1)

    def split(self, dve, T):
        t, half, par = T
        dve.wait_ge(self.s.hT, t + 1)
        wait(dve, self.used, t - 1)
        dve.tensor_copy(self.hi[:, par], self.hT[:, :, :]).then_inc(self.s.hi, 1)
        dve.wait_ge(self.s.hi, t + 1)
        dve.tensor_tensor(self.lo[:, par], self.hT[:, :, :], self.hi[:, par].bitcast(F32), ALU.subtract).then_inc(self.s.split, 1)


def load_split_weights(ph, s, w_dram, n_k, cols, w_hi, w_lo, stage):
    (s.w0, s.w1, s.w_hi, s.w_lo) = ph.semaphores("w0 w1 w_hi w_lo")

    def sp_part(sp):
        for k in range(n_k):
            wait(sp, s.w_lo, k - 1)
            sp.dma_start(stage[:, k % 2, 0:cols], w_dram[k * P:(k + 1) * P, :]).then_inc([s.w0, s.w1][k % 2], 16)

    def act_part(act):
        for k in range(n_k):
            act.wait_ge([s.w0, s.w1][k % 2], 16 * (k // 2 + 1))
            act.activation(w_hi[:, k, :], stage[:, k % 2, 0:cols], ACT.Copy).then_inc(s.w_hi, 1)

    def dve_part(dve):
        for k in range(n_k):
            dve.wait_ge(s.w_hi, k + 1)
            dve.tensor_tensor(w_lo[:, k, :], stage[:, k % 2, 0:cols], w_hi[:, k, :].bitcast(F32), ALU.subtract).then_inc(s.w_lo, 1)

    return sp_part, act_part, dve_part


def split_product(pe, out, parts, first, last):
    (ah, al), (bh, bl) = parts
    pe.matmul(out, ah, bh, start=first, stop=False)
    pe.matmul(out, ah, bl, start=False, stop=False)
    return pe.matmul(out, al, bh, start=False, stop=last)


def attention_projection(nc, g):
    NH = AH + KVH
    with ExitStack() as stack:
        ph = Phase(nc, stack, "qkv")
        s = ph.s
        (s.gain, s.gmul, s.rope0, s.rope1, s.mq, s.mkv, s.eq, s.ekv, s.psq, s.ssh, s.msh, s.rsh, s.cs, s.qn, s.m1, s.m2,
         s.rot, s.hq, s.lo_q, s.hk, s.lo_k, s.vhi, s.vlo, s.ptr, s.eptr, s.eptk, s.qout0, s.qout1, s.cache) = ph.semaphores(
            "gain gmul rope0 rope1 mq mkv eq ekv psq ssh msh rsh cs qn m1 m2 rot hq lo_q hk lo_k vhi vlo ptr eptr eptk qout0 qout1 cache")
        fr = Front(ph, s, g, 0, s.mkv)
        w_hi = ph.sb("w_hi", [P, KC, D_ATT], F32R)
        w_lo = ph.sb("w_lo", [P, KC, D_ATT], F32R)
        stage = ph.sb("stage", [P, 2, D_ATT])
        gsrc = ph.sb("gsrc", [P, 4, HD])
        gain = ph.sb("gain", [P, 2, NH, HD])
        rope = ph.sb("rope", [P, 2, 2, HD])
        qkv = ph.sb("qkv", [P, 2, D_ATT])
        psq = ph.sb("psq", [P, NH * HD])
        ssh = ph.sb("ssh", [P, NH])
        msh = ph.sb("msh", [P, NH])
        rsh = ph.sb("rsh", [P, NH])
        cs = ph.sb("cs", [P, 2, NH, HD])
        qn = ph.sb("qn", [P, NH, HD])
        m1 = ph.sb("m1", [P, NH, HD])
        m2 = ph.sb("m2", [P, NH, HD])
        rot = ph.sb("rot", [P, 2, NH, HD])
        qhl = ph.sb("qhl", [P, AH, 2, HD], F32R)
        khl = ph.sb("khl", [P, KVH, 4, HD], F32R)
        qT = ph.sb("qT", [P, 2, AH, P], F32R)
        p_q = [ph.ps("p_q0"), ph.ps("p_q1")]
        p_kv = ph.ps("p_kv")
        p_t = ph.ps("p_t", 1536)
        w_sp, w_act, w_dve = load_split_weights(ph, s, g.w_in[0, :, D_GLA:D_GLA + D_ATT], KC, D_ATT, w_hi, w_lo, stage)
        NQ = AH * HD

        def key_tile(t):
            return t + 2 if cond_of(t) else t

        with nc.Block() as block:

            @block.sync
            def _(sp):
                q_g, k_g = g.q_norm_g, g.k_norm_g
                half = HD // 4
                with nc.allow_non_contiguous_dma(reason="gains"):
                    for n, gg in enumerate((q_g, k_g)):
                        sp.dma_start(gsrc[:, 2 * n, :], gg.to_broadcast([P, HD])).then_inc(s.gain, 16)
                        for a in range(2):
                            for h in range(2):
                                src = gg[:, (2 * a + 1 - h) * half:(2 * a + 2 - h) * half].to_broadcast([P, half])
                                sp.dma_start(gsrc[:, 2 * n + 1, (2 * a + h) * half:(2 * a + h + 1) * half], src).then_inc(s.gain, 16)
                w_sp(sp)

                def step(U):
                    if T := U.at(5):
                        t, hf, par = T
                        sp.wait_ge(s.eptr, t + 1)
                        sp.dma_start(g.qT_tile(t), qT[:, par].rearrange("p h q -> p (h q)").bitcast(F32)).then_inc([s.qout0, s.qout1][par], 16)
                        if cond_of(t):
                            r = (t - N_LAT) * P
                            sp.dma_start(g.new_k[r:r + P, :], rot[:, par, AH:NH, :].rearrange("p h d -> p (h d)")).then_inc(s.cache, 16)
                            sp.dma_start(g.new_v[r:r + P, :], qkv[:, par, NH * HD:D_ATT]).then_inc(s.cache, 16)
                    if T := U.at(0):
                        fr.load(sp, T)
                    if T := U.at(2):
                        t, hf, par = T
                        wait(sp, s.cs, t - 1)
                        sp.dma_start(rope[:, par].rearrange("p a d -> p (a d)"), g.rope_tile(t)).then_inc([s.rope0, s.rope1][par], 16)

                steps(sp, 5, step)
                sp.wait_ge(s.qout0, 16 * (NT // 2))
                sp.wait_ge(s.qout1, 16 * (NT // 2))
                sp.wait_ge(s.cache, 16 * 2 * N_CTX)

            @block.scalar
            def _(act):
                w_act(act)

                def step(U):
                    if T := U.at(0):
                        fr.squares(act, T)
                    if T := U.at(1):
                        fr.modulate(act, T)
                    if T := U.at(3):
                        t, hf, par = T
                        act.wait_ge(s.mq, t + 1)
                        wait(act, s.vlo, t - 1)
                        act.activation(qkv[:, par, 0:NQ], p_q[par][:, :], ACT.Copy).then_inc(s.eq, 1)
                        act.wait_ge(s.mkv, t + 1)
                        act.activation(qkv[:, par, NQ:D_ATT], p_kv[:, 0:D_ATT - NQ], ACT.Copy).then_inc(s.ekv, 1)
                        act.wait_ge(s.ekv, t + 1)
                        act.wait_ge(s.eq, t + 1)
                        wait(act, s.ssh, t)
                        act.activation(psq[:, :], qkv[:, par, 0:NH * HD], ACT.Square).then_inc(s.psq, 1)
                    if T := U.at(4):
                        t, hf, par = T
                        act.wait_ge(s.ptr, t + 1)
                        if isinstance(t, int) and t < 2:
                            pass
                        else:
                            act.wait_ge([s.qout0, s.qout1][par], hf * 16)
                        act.activation(qT[:, par], p_t[:, 0:AH * P].rearrange("p (h q) -> p h q", h=AH), ACT.Copy).then_inc(s.eptr, 1)
                        kt = key_tile(t)
                        col = kt * P
                        act.activation(g.keysT[:, :, :, bass.ds(col, P)],
                                       p_t[:, AH * P:(AH + 4) * P].rearrange("p (g a q) -> p g a q", g=KVH, a=2), ACT.Copy).then_inc(s.eptk, 1)

                steps(act, 4, step)
                act.wait_ge(s.eptk, NT)

            @block.vector
            def _(dve):
                dve.wait_ge(s.gain, 16 * 10)
                for n in range(2):
                    dve.tensor_scalar(gain[:, n, 0:AH, :], bc(gsrc[:, n, :], 1, AH), HD ** -0.5, None, ALU.mult)
                    last = dve.tensor_copy(gain[:, n, AH:NH, :], bc(gsrc[:, 2 + n, :], 1, KVH))
                last.then_inc(s.gmul, 1)
                w_dve(dve)

                def step(U):
                    if T := U.at(0):
                        fr.normalise(dve, T)
                    if T := U.at(1):
                        fr.split(dve, T)
                    if T := U.at(3):
                        t, hf, par = T
                        dve.wait_ge(s.psq, t + 1)
                        dve.tensor_reduce(ssh[:, :], psq[:, :].rearrange("p (h d) -> p h d", d=HD), AX.X, ALU.add).then_inc(s.ssh, 1)
                        dve.wait_ge(s.ssh, t + 1)
                        dve.tensor_scalar(msh[:, :], ssh[:, :], 1.0 / HD, EPS, ALU.mult, ALU.add).then_inc(s.msh, 1)
                        vt = key_tile(t)
                        src = qkv[:, par, NH * HD:D_ATT].rearrange("p (g d) -> p g d", g=KVH)
                        dve.wait_ge(s.ekv, t + 1)
                        v_here = g.vals[:, bass.ds(vt * KVH, KVH), :]
                        dve.tensor_copy(v_here[:, :, 0:HD], src).then_inc(s.vhi, 1)
                        dve.wait_ge(s.rsh, t + 1)
                        dve.tensor_tensor(qn[:, :, :], qkv[:, par, 0:NH * HD].rearrange("p (h d) -> p h d", d=HD),
                                          bc(rsh[:, :], 2, HD), ALU.mult).then_inc(s.qn, 1)
                        dve.wait_ge(s.vhi, t + 1)
                        dve.tensor_tensor(v_here[:, :, HD:2 * HD], src, v_here[:, :, 0:HD].bitcast(F32), ALU.subtract).then_inc(s.vlo, 1)
                        dve.wait_ge(s.qn, t + 1)
                        dve.wait_ge(s.cs, t + 1)
                        dve.tensor_tensor(m1[:, :, :], qn[:, :, :], cs[:, 0], ALU.mult).then_inc(s.m1, 1)
                        dve.wait_ge(s.m1, t + 1)
                        dve.wait_ge(s.m2, t + 1)
                        dve.tensor_tensor(rot[:, par], m1[:, :, :], m2[:, :, :], ALU.add).then_inc(s.rot, 1)
                        dve.wait_ge(s.rot, t + 1)
                        wait(dve, s.ptr, t)
                        dve.tensor_copy(qhl[:, :, 0, :], rot[:, par, 0:AH, :]).then_inc(s.hq, 1)
                        dve.tensor_copy(khl[:, :, 0:2, :], bc(rot[:, par, AH:NH, :], 2, 2)).then_inc(s.hk, 1)
                        dve.wait_ge(s.hq, t + 1)
                        dve.tensor_tensor(qhl[:, :, 1, :], rot[:, par, 0:AH, :], qhl[:, :, 0, :].bitcast(F32), ALU.subtract).then_inc(s.lo_q, 1)
                        dve.wait_ge(s.hk, t + 1)
                        dve.tensor_tensor(khl[:, :, 2:4, :], bc(rot[:, par, AH:NH, :], 2, 2), khl[:, :, 0:2, :].bitcast(F32),
                                          ALU.subtract).then_inc(s.lo_k, 1)

                steps(dve, 4, step)

            @block.gpsimd
            def _(pool):
                pool.wait_ge(s.gmul, 1)

                def step(U):
                    if T := U.at(0):
                        fr.root(pool, T)
                    if T := U.at(3):
                        t, hf, par = T
                        pool.wait_ge([s.rope0, s.rope1][par], (hf + 1) * 16)
                        wait(pool, s.m1, t)
                        wait(pool, s.m2, t)
                        pool.tensor_tensor(cs[:, 0], gain[:, 0], bc(rope[:, par, 0, :], 1, NH), ALU.mult)
                        pool.tensor_tensor(cs[:, 1], gain[:, 1], bc(rope[:, par, 1, :], 1, NH), ALU.mult).then_inc(s.cs, 1)
                        pool.wait_ge(s.msh, t + 1)
                        pool.tensor_tensor(rsh[:, :], msh[:, :], g.neg_half[:, 0:NH], ALU.pow).then_inc(s.rsh, 1)
                        pool.wait_ge(s.cs, t + 1)
                        pool.wait_ge(s.qn, t + 1)
                        wait(pool, s.rot, t)
                        v5 = [x.rearrange("p h (a e d) -> p (h a) e d", a=2, e=2) for x in (m2[:, :, :], qn[:, :, :], cs[:, 1])]
                        for e in range(2):
                            last = pool.tensor_tensor(v5[0][:, :, e, :], v5[1][:, :, 1 - e, :], v5[2][:, :, e, :], ALU.mult)
                        last.then_inc(s.m2, 1)

                steps(pool, 4, step)

            @block.tensor
            def _(pe):
                pe.wait_ge(s.w_lo, KC)

                def step(U):
                    if T := U.at(1):
                        fr.transpose(pe, T)
                    if T := U.at(2):
                        t, hf, par = T
                        pe.wait_ge(s.split, t + 1)
                        wait(pe, s.eq, t - 1)
                        for k in range(KC):
                            last = split_product(pe, p_q[par][:, :], ((fr.hi[:, par, k], fr.lo[:, par, k]),
                                                 (w_hi[:, k, 0:NQ], w_lo[:, k, 0:NQ])), k == 0, k == KC - 1)
                        last.then_inc(s.mq, 1)
                        wait(pe, s.ekv, t)
                        for k in range(KC):
                            last = split_product(pe, p_kv[:, 0:D_ATT - NQ], ((fr.hi[:, par, k], fr.lo[:, par, k]),
                                                 (w_hi[:, k, NQ:D_ATT], w_lo[:, k, NQ:D_ATT])), k == 0, k == KC - 1)
                        last.then_inc(s.mkv, 1)
                    if T := U.at(3):
                        t, hf, par = T
                        pe.wait_ge(s.lo_q, t + 1)
                        pe.wait_ge(s.lo_k, t + 1)
                        wait(pe, s.eptr, t)
                        wait(pe, s.eptk, t)
                        for h in range(AH):
                            pe.transpose(p_t[:, h * P:(h + 1) * P], qhl[:, h].rearrange("p a d -> p (a d)").bitcast(F32), g.ident[:, :])
                        for n in range(4):
                            last = pe.transpose(p_t[:, (AH + n) * P:(AH + n + 1) * P],
                                                khl[:, n // 2, 2 * (n % 2):2 * (n % 2) + 2, :].rearrange("p a d -> p (a d)").bitcast(F32),
                                                g.ident[:, :])
                        last.then_inc(s.ptr, 1)

                steps(pe, 4, step)


def attention(nc, g):
    G4 = AH // KVH
    NKT = (T_LAT + PAST) // P
    NKC = T_CTX // P
    ITEMS = NKT + 1
    LAG = 2
    with ExitStack() as stack:
        ph = Phase(nc, stack, "att")
        s = ph.s
        (s.ck, s.cv, s.ckh, s.ckl, s.ctr, s.cte, s.q0, s.q1, s.sc, s.mx, s.nm, s.ex, s.inv, s.lb, s.tT, s.thi, s.tlo,
         s.pv, s.osb, s.osum, s.oo, s.st0, s.st1) = ph.semaphores(
            "ck cv ckh ckl ctr cte q0 q1 sc mx nm ex inv lb tT thi tlo pv osb osum oo st0 st1")
        ckr = ph.sb("ckr", [P, 2, KVH, HD])
        cvr = ph.sb("cvr", [P, 2, KVH, HD])
        ckp = ph.sb("ckp", [P, 2, KVH, 4, HD], F32R)
        qT = ph.sb("qT", [P, 2, G4, P], F32R)
        prob = ph.sb("prob", [P, 2, G4, NKT * P])
        mx = ph.sb("mx", [P, 4])
        nm = ph.sb("nm", [P, 2])
        rs = ph.sb("rs", [P, 2, G4])
        inv = ph.sb("inv", [P, G4])
        lb = ph.sb("lb", [P, G4, HD])
        thi = ph.sb("thi", [P, 4, G4 * P], F32R)
        tlo = ph.sb("tlo", [P, 4, G4 * P], F32R)
        osb = ph.sb("osb", [HD, G4 * P])
        osum = ph.sb("osum", [P, 2, P])
        oo = ph.sb("oo", [P, 2, 2 * P])
        p_s = ph.ps("p_s", 2560)
        p_t = [ph.ps("p_t0"), ph.ps("p_t1")]
        p_o = ph.ps("p_o")
        PIECES = [(0, 1024), (1024, 2048), (2048, 2304)]

        def unit(n, qt, kv):
            u = Names()
            u.n, u.qt, u.kv = n, qt, kv
            if isinstance(n, int) and n >= 2 * N_LAT:
                u.nkt, u.kt0 = NKC, NKT
                u.items0 = 2 * N_LAT * ITEMS + (n - 2 * N_LAT) * (NKC + 1)
                u.pieces = [(0, T_CTX)]
                u.piece0 = 2 * N_LAT * G4 * 3 + (n - 2 * N_LAT) * G4
                u.tile0 = 2 * N_LAT * NKT + (n - 2 * N_LAT) * NKC
                u.slot0 = u.tile0
            else:
                u.nkt, u.kt0 = NKT, 0
                u.items0 = n * ITEMS
                u.pieces = PIECES
                u.piece0 = n * (G4 * 3)
                u.tile0 = n * NKT
            return u

        def units(eng, body):
            before = None
            for kv in range(KVH):
                u = unit(kv, 0, kv)
                body(u, before)
                before = u
            with eng.Fori(1, N_LAT) as qt:
                before = unit(qt * 2 - 1, qt - 1, 1)
                for kv in range(KVH):
                    u = unit(qt * 2 + kv, qt, kv)
                    body(u, before)
                    before = u
            before = unit(2 * N_LAT - 1, N_LAT - 1, 1)
            for qt in range(N_LAT, NT):
                for kv in range(KVH):
                    u = unit(2 * qt + kv, qt, kv)
                    body(u, before)
                    before = u
            body(None, before)

        def share(b, h):
            if b is None:
                return []
            n = b.nkt + 1
            cut = [n * x // G4 for x in range(G4 + 1)]
            return list(range(cut[h], cut[h + 1]))

        def bank(b, j):
            if isinstance(b.n, int) and b.n >= 2 * N_LAT:
                return (b.items0 + j) % 2
            return (b.kv * ITEMS + j) % 2

        def slot(b, j):
            if isinstance(b.n, int) and b.n >= 2 * N_LAT:
                return (b.tile0 + j) % 4
            return (b.kv * NKT + j) % 4

        with nc.Block() as block:

            @block.sync
            def _(sp):
                for t in range(2):
                    sp.dma_start(ckr[:, t].rearrange("p g d -> p (g d)"), g.cache_k[t * P:(t + 1) * P, :]).then_inc(s.ck, 16)
                    sp.dma_start(cvr[:, t].rearrange("p g d -> p (g d)"), g.cache_v[t * P:(t + 1) * P, :]).then_inc(s.cv, 16)

                def body(u, b):
                    if u is not None:
                        wait(sp, s.sc, u.piece0 - len(u.pieces) * G4)
                        sp.dma_start(qT[:, u.kv].rearrange("p h q -> p (h q)").bitcast(F32), g.qT_tile(u.qt)[:, u.kv * G4 * P:(u.kv + 1) * G4 * P]
                                     ).then_inc([s.q0, s.q1][u.kv], 16)

                units(sp, body)

            @block.gpsimd
            def _(pool):
                def body(u, b):
                    if b is not None:
                        pool.wait_ge(s.oo, b.n + 1)
                        pool.dma_start(g.mix_tile(b.qt)[:, (4 + 2 * b.kv) * P:(6 + 2 * b.kv) * P], oo[:, b.kv, :]
                                       ).then_inc([s.st0, s.st1][b.kv], 16)

                units(pool, body)
                pool.wait_ge(s.st0, 16 * NT)
                pool.wait_ge(s.st1, 16 * NT)

            @block.tensor
            def _(pe):
                pe.wait_ge(s.ckl, 1)
                for t in range(2):
                    for n in range(4):
                        last = pe.transpose(p_s[:, (t * 4 + n) * P:(t * 4 + n + 1) * P],
                                            ckp[:, t, n // 2, 2 * (n % 2):2 * (n % 2) + 2, :].rearrange("p a d -> p (a d)").bitcast(F32),
                                            g.ident[:, :])
                last.then_inc(s.ctr, 1)
                pe.wait_ge(s.cte, 2)

                def values(b, j):
                    pe.wait_ge(s.tlo, b.tile0 + (j + 1))
                    if j == 0:
                        wait(pe, s.osum, b.n)
                    sl = slot(b, j)
                    v = g.vals[:, (b.kt0 + j) * KVH + b.kv, :]
                    pe.matmul(p_o[:, :], v, thi[:, sl, :], start=j == 0, stop=False)
                    pe.matmul(p_o[:, :], v, tlo[:, sl, :], start=False, stop=j == b.nkt - 1).then_inc(s.pv, 1)

                def ring(b, j):
                    if j < b.nkt:
                        if j == 0:
                            pe.wait_ge(s.ex, b.n * G4 + G4)
                        if j >= 2:
                            pe.wait_ge(s.tlo, b.tile0 + (j - 1))
                        elif j == 1:
                            wait(pe, s.oo, b.n)
                        else:
                            wait(pe, s.tlo, b.tile0)
                        for h in range(G4):
                            last = pe.transpose(p_t[bank(b, j)][:, h * P:(h + 1) * P], prob[:, b.kv, h, j * P:(j + 1) * P], g.ident[:, :])
                        last.then_inc(s.tT, 1)
                    else:
                        pe.wait_ge(s.lb, b.n + 1)
                        pe.wait_ge(s.tlo, b.tile0 + (j - 1))
                        for n in range(2):
                            last = pe.transpose(p_t[bank(b, j)][:, n * P:(n + 1) * P],
                                                lb[:, 2 * n:2 * n + 2, :].rearrange("p h d -> p (h d)"), g.ident[:, :])
                        last.then_inc(s.tT, 1)
                    if j >= LAG:
                        values(b, j - LAG)
                    if j == b.nkt:
                        for jj in range(b.nkt - LAG + 1, b.nkt):
                            values(b, jj)

                def body(u, b):
                    for h in range(G4):
                        if u is not None:
                            if h == 0:
                                pe.wait_ge([s.q0, s.q1][u.kv], u.qt * 16 + 16)
                            wait(pe, s.ex, u.n * G4 + h)
                            for i, (c0, c1) in enumerate(u.pieces):
                                for c in range(c0, c1, 512):
                                    e = min(c + 512, c1)
                                    q = qT[:, u.kv, h]
                                    for ab in range(2):
                                        last = pe.matmul(p_s[:, c:e], q, g.keysT[:, u.kv, ab, u.kt0 * P + c:u.kt0 * P + e],
                                                         start=ab == 0, stop=ab == 1)
                                last.then_inc(s.sc, 1)
                        for j in share(b, h):
                            ring(b, j)

                units(pe, body)

            @block.scalar
            def _(act):
                act.wait_ge(s.ctr, 1)
                for t in range(2):
                    act.activation(g.keysT[:, :, :, (N_LAT + t) * P:(N_LAT + t + 1) * P],
                                   p_s[:, t * 512:(t + 1) * 512].rearrange("p (g a q) -> p g a q", g=KVH, a=2), ACT.Copy).then_inc(s.cte, 1)

                def high(b, j):
                    if j == b.nkt:
                        return
                    act.wait_ge(s.tT, b.items0 + (j + 1))
                    wait(act, s.pv, b.tile0 + (j - 3))
                    act.activation(thi[:, slot(b, j), :], p_t[bank(b, j)][:, :], ACT.Copy).then_inc(s.thi, 1)

                def body(u, b):
                    for h in range(G4):
                        js = share(b, h)
                        for j in js[:2]:
                            high(b, j)
                        if u is not None:
                            act.wait_ge(s.nm, u.n * G4 + (h + 1))
                            if h == 0:
                                if isinstance(u.n, int):
                                    pb = unit(u.n - 1, 0, 1 - u.kv).items0 if u.n >= 2 else 0
                                    wait(act, s.tT, pb)
                                else:
                                    act.wait_ge(s.tT, (u.n - 1) * ITEMS)
                                wait(act, s.inv, u.n - 1)
                            w = u.nkt * P
                            act.activation(prob[:, u.kv, h, 0:w], p_s[:, 0:w], ACT.Exp, bias=nm[:, h % 2:h % 2 + 1],
                                           accum_out=rs[:, u.kv, h:h + 1]).then_inc(s.ex, 1)
                        for j in js[2:]:
                            high(b, j)
                    if b is not None:
                        act.wait_ge(s.pv, b.tile0 + b.nkt)
                        wait(act, s.osum, b.n)
                        act.activation(osb[:, :], p_o[HD:P, :], ACT.Copy).then_inc(s.osb, 1)

                units(act, body)

            @block.vector
            def _(dve):
                dve.wait_ge(s.cv, 32)
                for t in range(2):
                    v_here = g.vals[:, (N_LAT + t) * KVH:(N_LAT + t + 1) * KVH, :]
                    dve.tensor_copy(v_here[:, :, 0:HD], cvr[:, t]).then_inc(s.ckh, 1)
                dve.wait_ge(s.ck, 32)
                for t in range(2):
                    dve.tensor_copy(ckp[:, t, :, 0:2, :], bc(ckr[:, t], 2, 2)).then_inc(s.ckh, 1)
                dve.wait_ge(s.ckh, 4)
                for t in range(2):
                    v_here = g.vals[:, (N_LAT + t) * KVH:(N_LAT + t + 1) * KVH, :]
                    dve.tensor_tensor(v_here[:, :, HD:2 * HD], cvr[:, t], v_here[:, :, 0:HD].bitcast(F32), ALU.subtract)
                    last = dve.tensor_tensor(ckp[:, t, :, 2:4, :], bc(ckr[:, t], 2, 2), ckp[:, t, :, 0:2, :].bitcast(F32), ALU.subtract)
                last.then_inc(s.ckl, 1)

                def low(b, j):
                    if j == b.nkt:
                        return
                    dve.wait_ge(s.thi, b.tile0 + (j + 1))
                    sl = slot(b, j)
                    dve.tensor_tensor(tlo[:, sl, :], p_t[bank(b, j)][:, :], thi[:, sl, :].bitcast(F32), ALU.subtract).then_inc(s.tlo, 1)

                def body(u, b):
                    for h in range(G4):
                        if u is not None:
                            for i, (c0, c1) in enumerate(u.pieces):
                                dve.wait_ge(s.sc, u.piece0 + (h * len(u.pieces) + i + 1))
                                last = dve.tensor_reduce(mx[:, i:i + 1], p_s[:, c0:c1], AX.X, ALU.max)
                            last.then_inc(s.mx, 1)
                            dve.wait_ge(s.mx, u.n * G4 + (h + 1))
                            wait(dve, s.ex, u.n * G4 + (h - 1))
                            dve.tensor_reduce(nm[:, h % 2:h % 2 + 1], mx[:, 0:len(u.pieces)], AX.X, ALU.max, negate=True).then_inc(s.nm, 1)
                        if b is not None and h == 0:
                            dve.wait_ge(s.ex, b.n * G4 + G4)
                            dve.reciprocal(inv[:, :], rs[:, b.kv, :]).then_inc(s.inv, 1)
                            dve.wait_ge(s.inv, b.n + 1)
                            dve.tensor_copy(lb[:, :, :], bc(inv[:, :], 2, HD)).then_inc(s.lb, 1)
                        for j in share(b, h):
                            low(b, j)
                    if b is not None:
                        dve.wait_ge(s.osb, b.n + 1)
                        ov = p_o[0:HD, :].rearrange("p (n e q) -> p n e q", e=2, q=P)
                        sv = osb[:, :].rearrange("p (n e q) -> p n e q", e=2, q=P)
                        for e in range(2):
                            last = dve.tensor_tensor(osum[e * HD:(e + 1) * HD, :, :], ov[:, :, e, :], sv[:, :, e, :], ALU.add)
                        last.then_inc(s.osum, 1)
                        dve.wait_ge(s.osum, b.n + 1)
                        dve.wait_ge(s.tT, b.items0 + (b.nkt + 1))
                        if not (isinstance(b.qt, int) and b.qt == 0):
                            dve.wait_ge([s.st0, s.st1][b.kv], b.qt * 16)
                        dve.tensor_tensor(oo[:, b.kv, :], osum[:, :, :].rearrange("p n q -> p (n q)"),
                                          p_t[bank(b, b.nkt)][:, 0:2 * P], ALU.mult).then_inc(s.oo, 1)

                units(dve, body)


def gla_projection(nc, g):
    NB = 4
    BW = D_GLA // NB
    with ExitStack() as stack:
        ph = Phase(nc, stack, "gp")
        s = ph.s
        (s.b0, s.b1, s.b2, s.b3, s.e0, s.e1, s.e2, s.e3, s.o0, s.o1) = ph.semaphores(
            "b0 b1 b2 b3 e0 e1 e2 e3 o0 o1")
        b, e, o = [s.b0, s.b1, s.b2, s.b3], [s.e0, s.e1, s.e2, s.e3], [s.o0, s.o1]
        fr = Front(ph, s, g, 0, b[NB - 1])
        w_hi = ph.sb("w_hi", [P, KC, D_GLA], F32R)
        w_lo = ph.sb("w_lo", [P, KC, D_GLA], F32R)
        stage = ph.sb("stage", [P, 2, D_GLA])
        out = ph.sb("out", [P, 2, D_GLA])
        p_b = [ph.ps(f"p_b{j}") for j in range(NB)]
        w_sp, w_act, w_dve = load_split_weights(ph, s, g.w_in[0, :, 0:D_GLA], KC, D_GLA, w_hi, w_lo, stage)

        def evacuate(eng, copy, T, banks):
            t, hf, par = T
            for j in banks:
                eng.wait_ge(b[j], t + 1)
                if not (isinstance(t, int) and t < 2):
                    eng.wait_ge(o[par], hf * 16)
                copy(out[:, par, j * BW:(j + 1) * BW], p_b[j][:, 0:BW]).then_inc(e[j], 1)

        with nc.Block() as block:

            @block.sync
            def _(sp):
                w_sp(sp)

                def step(U):
                    if T := U.at(3):
                        t, hf, par = T
                        for j in range(NB):
                            sp.wait_ge(e[j], t + 1)
                        sp.dma_start(g.proj_tile(t), out[:, par, :]).then_inc(o[par], 16)
                    if T := U.at(0):
                        fr.load(sp, T)

                steps(sp, 3, step)
                for par in range(2):
                    sp.wait_ge(o[par], 16 * (NT // 2))

            @block.scalar
            def _(act):
                w_act(act)

                def step(U):
                    if T := U.at(0):
                        fr.squares(act, T)
                    if T := U.at(1):
                        fr.modulate(act, T)
                    if T := U.at(2):
                        evacuate(act, lambda a, c: act.activation(a, c, ACT.Copy), T, (0, 2))

                steps(act, 3, step)

            @block.vector
            def _(dve):
                w_dve(dve)

                def step(U):
                    if T := U.at(0):
                        fr.normalise(dve, T)
                    if T := U.at(1):
                        fr.split(dve, T)
                    if T := U.at(2):
                        evacuate(dve, dve.tensor_copy, T, (1, 3))

                steps(dve, 3, step)

            @block.gpsimd
            def _(pool):
                def step(U):
                    if T := U.at(0):
                        fr.root(pool, T)

                steps(pool, 3, step)

            @block.tensor
            def _(pe):
                pe.wait_ge(s.w_lo, KC)

                def step(U):
                    if T := U.at(1):
                        fr.transpose(pe, T)
                    if T := U.at(2):
                        t, hf, par = T
                        pe.wait_ge(s.split, t + 1)
                        for j in range(NB):
                            wait(pe, e[j], t)
                            for k in range(KC):
                                last = split_product(pe, p_b[j][:, 0:BW], ((fr.hi[:, par, k], fr.lo[:, par, k]),
                                                     (w_hi[:, k, j * BW:(j + 1) * BW], w_lo[:, k, j * BW:(j + 1) * BW])),
                                                     k == 0, k == KC - 1)
                            last.then_inc(b[j], 1)

                steps(pe, 3, step)


def slot_of(chunk, ctx):
    return LAT_SLOTS + 1 + chunk if ctx else chunk + 1


def gla_states(nc, g):
    NG = 2 * GH * DK
    with ExitStack() as stack:
        ph = Phase(nc, stack, "gs")
        s = ph.s
        (s.const, s.wgz, s.in0, s.in1, s.v0, s.v1, s.lrp, s.lrT, s.gk, s.ab, s.ex1, s.ln, s.mn, s.gate, s.cum, s.dec,
         s.e1, s.e2, s.e3, s.edec, s.qs, s.qt, s.kt, s.ke, s.tq, s.tk, s.u, s.etq, s.etk, s.scan, s.ub, s.out0, s.out1,
         s.init, s.z, s.back, s.fin) = ph.semaphores(
            "const wgz in0 in1 v0 v1 lrp lrT gk ab ex1 ln mn gate cum dec e1 e2 e3 edec qs qt kt ke tq tk u etq etk scan ub out0 out1 init z back fin")
        s.inp, s.vin, s.out = [s.in0, s.in1], [s.v0, s.v1], [s.out0, s.out1]
        tri = ph.sb("tri", [P, 4, P])
        ind = ph.sb("ind", [P, 2])
        wg = ph.sb("wg", [2 * LR + 1, GH, 2, DK])
        lrT = ph.sb("lrT", [2 * LR + 1, P])
        qk = ph.sb("qk", [P, 2, 2 * GH * DK])
        lr = ph.sb("lr", [P, 2, 2 * LR])
        vin = ph.sb("vin", [P, 2, GH * DV])
        ab = ph.sb("ab", [P, NG])
        mn = ph.sb("mn", [P, NG])
        gate = ph.sb("gate", [P, 2, GH, 2, DK])
        e1 = ph.sb("e1", [P, GH, 2, DK])
        e2 = ph.sb("e2", [P, GH, 2, DK])
        e3 = ph.sb("e3", [P, GH, 2, DK])
        qs = ph.sb("qs", [P, GH, DK])
        qt = ph.sb("qt", [P, GH, 2, DK])
        kt = ph.sb("kt", [P, GH, 2, DK])
        ke = ph.sb("ke", [P, GH, 2, DK])
        qkT = ph.sb("qkT", [P, 2, GH, 2, P])
        p_a = ph.ps("p_a")
        p_g = ph.ps("p_g")
        p_inc = ph.ps("p_inc")
        p_exc = ph.ps("p_exc")
        p_q = ph.ps("p_q")
        p_k = ph.ps("p_k")
        p_u = [ph.ps("p_u0"), ph.ps("p_u1")]
        V0 = 2 * GH * DK
        LR0 = D_GLA - 2 * LR

        with nc.Block() as block:

            @block.sync
            def _(sp):
                sp.dma_start(tri[:, :, :], g.d_tri).then_inc(s.const, 16)
                sp.dma_start(ind[:, :], g.d_ind).then_inc(s.const, 16)
                sp.wait_ge(s.wgz, 1)
                for r in range(2):
                    sp.dma_start(wg[r * LR:(r + 1) * LR, :, r, :], g.w_gk2[0, r].rearrange("l (h d) -> l h d", h=GH)).then_inc(s.const, 16)
                    sp.dma_start(wg[2 * LR:2 * LR + 1, :, r, :], g.b_gk2[:, r, :].rearrange("l (h d) -> l h d", h=GH)).then_inc(s.const, 16)
                sp.wait_ge(s.z, 1)
                sp.dma_start(g.states[0:DK, slot_of(0, False)], g.state_f.rearrange("h k v -> k h v")).then_inc(s.init, 16)
                sp.dma_start(g.states[DK:P, slot_of(T_LAT // CH - 1, False)], g.state_b.rearrange("h k v -> k h v")).then_inc(s.init, 16)

                def step(U):
                    if T := U.at(4):
                        t, hf, par = T
                        sp.wait_ge(s.etq, t + 1)
                        sp.wait_ge(s.etk, t + 1)
                        sp.dma_start(g.qkT_tile(t), qkT[:, par].rearrange("p h a q -> p (h a q)")).then_inc(s.out[par], 16)
                    if T := U.at(0):
                        t, hf, par = T
                        wait(sp, s.kt, t - 1)
                        wait(sp, s.ke, t - 1)
                        sp.dma_start(qk[:, par, :], g.proj_tile(t)[:, 0:V0]).then_inc(s.inp[par], 16)
                        sp.dma_start(lr[:, par, :], g.proj_tile(t)[:, LR0:D_GLA]).then_inc(s.inp[par], 16)
                    if T := U.at(2):
                        t, hf, par = T
                        wait(sp, s.u, t - 1)
                        sp.dma_start(vin[:, par, :], g.proj_tile(t)[:, V0:V0 + GH * DV]).then_inc(s.vin[par], 16)

                steps(sp, 4, step)
                sp.wait_ge(s.out0, 16 * (NT // 2))
                sp.wait_ge(s.out1, 16 * (NT // 2))
                sp.wait_ge(s.back, 1)
                for n, (out, idx) in enumerate(((g.new_f, slot_of(T_CTX // CH, True)), (g.new_b, slot_of(-1, True)))):
                    sp.dma_start(out.rearrange("h k v -> k h v"), g.states[n * DK:(n + 1) * DK, idx]).then_inc(s.fin, 16)
                sp.wait_ge(s.fin, 32)

            @block.gpsimd
            def _(pool):
                pool.memset(wg[:, :, :, :], 0.0).then_inc(s.wgz, 1)

                def step(U):
                    if T := U.at(2):
                        t, hf, par = T
                        pool.wait_ge(s.e3, t + 1)
                        wait(pool, s.u, t)
                        pool.tensor_tensor(ke[:, :, :, :], bc(qk[:, par, GH * DK:V0].rearrange("p (h d) -> p h d", h=GH), 2, 2),
                                           e3[:, :, :, :], ALU.mult).then_inc(s.ke, 1)

                steps(pool, 4, step)

            @block.tensor
            def _(pe):
                pe.wait_ge(s.const, 16 * 6)

                def step(U):
                    if T := U.at(1):
                        t, hf, par = T
                        pe.wait_ge(s.inp[par], (hf + 1) * 32)
                        wait(pe, s.edec, t - 1)
                        wait(pe, s.lrT, t)
                        pe.transpose(p_a[0:2 * LR, 0:P], lr[:, par, :], g.ident[:, :]).then_inc(s.lrp, 1)
                        pe.wait_ge(s.lrT, t + 1)
                        wait(pe, s.mn, t)
                        pe.matmul(p_g[:, :], lrT[:, :], wg[:, :, :, :].rearrange("l h r d -> l (h r d)"), start=True, stop=True).then_inc(s.gk, 1)
                    if T := U.at(2):
                        t, hf, par = T
                        pe.wait_ge(s.gate, t + 1)
                        wait(pe, s.e3, t)
                        for r in range(2):
                            pe.matmul(p_inc[:, :].rearrange("p (h r d) -> p h r d", h=GH, r=2)[:, :, r, :], tri[:, r, :], gate[:, par, :, r, :],
                                      start=r == 0, stop=True, skip_group_check=True)
                        for r in range(2):
                            last = pe.matmul(p_exc[:, :].rearrange("p (h r d) -> p h r d", h=GH, r=2)[:, :, r, :], tri[:, 2 + r, :],
                                             gate[:, par, :, r, :], start=r == 0, stop=True, skip_group_check=True)
                        last.then_inc(s.cum, 1)
                        wait(pe, s.edec, t)
                        for h in range(GH):
                            last = pe.matmul(p_a[:, 256 + 2 * h:258 + 2 * h], gate[:, par, h].rearrange("p r d -> p (r d)"), ind[:, :], start=True, stop=True)
                        last.then_inc(s.dec, 1)
                    if T := U.at(3):
                        t, hf, par = T
                        pe.wait_ge(s.qt, t + 1)
                        wait(pe, s.etq, t)
                        for h in range(GH):
                            last = pe.transpose(p_q[:, h * P:(h + 1) * P], qt[:, h].rearrange("p r d -> p (r d)"), g.ident[:, :])
                        last.then_inc(s.tq, 1)
                        pe.wait_ge(s.kt, t + 1)
                        wait(pe, s.etk, t)
                        for h in range(GH):
                            last = pe.transpose(p_k[:, h * P:(h + 1) * P], kt[:, h].rearrange("p r d -> p (r d)"), g.ident[:, :])
                        last.then_inc(s.tk, 1)
                        pe.wait_ge(s.ke, t + 1)
                        pe.wait_ge(s.vin[par], (hf + 1) * 16)
                        wait(pe, s.ub, t)
                        wait(pe, s.scan, 2 * GH * t)
                        for c in range(2):
                            rows = slice(c * CH, (c + 1) * CH)
                            for h in range(GH):
                                last = pe.matmul(p_u[c][:, h * DV:(h + 1) * DV], ke[rows, h].rearrange("p r d -> p (r d)"),
                                                 vin[rows, par, h * DV:(h + 1) * DV], start=True, stop=True)
                        last.then_inc(s.u, 1)

                steps(pe, 4, step)

            @block.scalar
            def _(act):
                def step(U):
                    if T := U.at(1):
                        t, hf, par = T
                        act.wait_ge(s.gk, t + 1)
                        wait(act, s.gate, t)
                        act.activation(ab[:, :], p_g[:, :], ACT.Abs).then_inc(s.ab, 1)
                        act.wait_ge(s.ab, t + 1)
                        act.activation(ab[:, :], ab[:, :], ACT.Exp, scale=-1.0).then_inc(s.ex1, 1)
                        act.wait_ge(s.ex1, t + 1)
                        act.activation(ab[:, :], ab[:, :], ACT.Ln, bias=1.0).then_inc(s.ln, 1)
                    if T := U.at(2):
                        t, hf, par = T
                        act.wait_ge(s.cum, t + 1)
                        wait(act, s.kt, t)
                        wait(act, s.ke, t)
                        r3 = lambda p: p[:, :].rearrange("p (h r d) -> p h r d", h=GH, r=2)
                        act.activation(e1[:, :, :, :], r3(p_inc), ACT.Exp, scale=1.0 / 16).then_inc(s.e1, 1)
                        act.activation(e2[:, :, :, :], r3(p_inc), ACT.Exp, scale=-1.0 / 16).then_inc(s.e2, 1)
                        act.activation(e3[:, :, :, :], r3(p_exc), ACT.Exp, scale=1.0 / 16).then_inc(s.e3, 1)
                        act.wait_ge(s.dec, t + 1)
                        act.activation(g.decay[:, :, bass.ds(2 * t, 2)], p_a[:, 256:256 + 2 * GH].rearrange("p (h c) -> p h c", c=2),
                                       ACT.Exp, scale=1.0 / 16).then_inc(s.edec, 1)
                    if T := U.at(3):
                        t, hf, par = T
                        act.wait_ge(s.tq, t + 1)
                        if not (isinstance(t, int) and t < 2):
                            act.wait_ge(s.out[par], hf * 16)
                        act.activation(qkT[:, par, :, 0, :], p_q[:, :].rearrange("p (h q) -> p h q", h=GH), ACT.Copy).then_inc(s.etq, 1)
                        act.wait_ge(s.tk, t + 1)
                        act.activation(qkT[:, par, :, 1, :], p_k[:, :].rearrange("p (h q) -> p h q", h=GH), ACT.Copy).then_inc(s.etk, 1)
                        ctx = cond_of(t)
                        chunk = 2 * (t - N_LAT) if ctx else 2 * t
                        act.wait_ge(s.scan, 2 * GH * (t + 1))
                        act.wait_ge(s.u, t + 1)
                        for c in range(2):
                            idx = slot_of(chunk + c - 1, ctx)
                            last = act.activation(g.states[DK:P, bass.ds(idx, 1)].rearrange("p o h v -> p (o h) v"),
                                                  p_u[c][DK:P, :].rearrange("p (h v) -> p h v", h=GH), ACT.Copy)
                        last.then_inc(s.ub, 1)

                steps(act, 4, step)

            @block.vector
            def _(dve):
                last_state = slot_of(T_CTX // CH - 1, True)
                dve.memset(g.states[0:DK, slot_of(0, True)], 0.0)
                dve.memset(g.states[DK:P, last_state], 0.0)
                dve.memset(lrT[2 * LR:2 * LR + 1, :], 1.0).then_inc(s.z, 1)
                dve.wait_ge(s.z, 1)
                dve.wait_ge(s.init, 32)

                def step(U):
                    if T := U.at(1):
                        t, hf, par = T
                        dve.wait_ge(s.lrp, t + 1)
                        wait(dve, s.gk, t)
                        dve.tensor_copy(lrT[0:2 * LR, :], p_a[0:2 * LR, 0:P]).then_inc(s.lrT, 1)
                    if T := U.at(2):
                        t, hf, par = T
                        dve.tensor_scalar(qs[:, :, :], qk[:, par, 0:GH * DK].rearrange("p (h d) -> p h d", h=GH), DK ** -0.5, None,
                                          ALU.mult).then_inc(s.qs, 1)
                        dve.wait_ge(s.qs, t + 1)
                        dve.wait_ge(s.e1, t + 1)
                        wait(dve, s.tq, t)
                        dve.tensor_tensor(qt[:, :, :, :], bc(qs[:, :, :], 2, 2), e1[:, :, :, :], ALU.mult).then_inc(s.qt, 1)
                        dve.wait_ge(s.e2, t + 1)
                        wait(dve, s.tk, t)
                        dve.tensor_tensor(kt[:, :, :, :], bc(qk[:, par, GH * DK:V0].rearrange("p (h d) -> p h d", h=GH), 2, 2),
                                          e2[:, :, :, :], ALU.mult).then_inc(s.kt, 1)
                    if T := U.at(1):
                        t, hf, par = T
                        dve.wait_ge(s.ln, t + 1)
                        dve.tensor_scalar(mn[:, :], p_g[:, :], 0.0, None, ALU.min).then_inc(s.mn, 1)
                        dve.wait_ge(s.mn, t + 1)
                        dve.tensor_tensor(gate[:, par].rearrange("p h r d -> p (h r d)"), mn[:, :], ab[:, :], ALU.subtract).then_inc(s.gate, 1)
                    if T := U.at(3):
                        t, hf, par = T
                        ctx = cond_of(t)
                        chunk = 2 * (t - N_LAT) if ctx else 2 * t
                        dve.wait_ge(s.u, t + 1)
                        dve.wait_ge(s.edec, t + 1)
                        for c in range(2):
                            if c:
                                dve.wait_ge(s.scan, 2 * GH * t + GH)
                            else:
                                wait(dve, s.scan, 2 * GH * t)
                            for h in range(GH):
                                idx = slot_of(chunk + c, ctx)
                                state = lambda i: g.states[0:DK, bass.ds(i, 1), h, :].rearrange("p o v -> p (o v)")
                                dve.scalar_tensor_tensor(state(idx + 1), state(idx), g.decay[0:DK, h, bass.ds(2 * t + c, 1)],
                                                         p_u[c][0:DK, h * DV:(h + 1) * DV], ALU.mult, ALU.add).then_inc(s.scan, 1)

                steps(dve, 4, step)
                dve.wait_ge(s.ub, NT)
                base = 2 * GH * NT

                def backwards(idx, tile_chunk, n):
                    dve.wait_ge(s.scan, base + n * GH)
                    for h in range(GH):
                        state = lambda i: g.states[DK:P, bass.ds(i, 1), h, :].rearrange("p o v -> p (o v)")
                        last = dve.scalar_tensor_tensor(state(idx - 1), state(idx), g.decay[DK:P, h, bass.ds(tile_chunk, 1)],
                                                        state(idx - 1), ALU.mult, ALU.add)
                        last.then_inc(s.scan, 1)
                    return last

                n_ctx = T_CTX // CH
                for n in range(n_ctx):
                    c = n_ctx - 1 - n
                    backwards(slot_of(c, True), T_LAT // CH + c, n)
                dve.wait_ge(s.scan, base + n_ctx * GH)
                dve.memset(ab[:, 0:1], 0.0).then_inc(s.back, 1)
                n_lat = T_LAT // CH
                with dve.Fori(0, n_lat - 1) as n:
                    backwards(n * -1 + n_lat, n * -1 + (n_lat - 1), n + n_ctx)
                dve.wait_ge(s.scan, base + (n_ctx + n_lat - 1) * GH)


def gla_outputs(nc, g):
    with ExitStack() as stack:
        ph = Phase(nc, stack, "go")
        s = ph.s
        (s.const, s.z0, s.qk0, s.qk1, s.vo0, s.vo1, s.af, s.abk, s.mf, s.mb, s.o, s.sq, s.ss, s.ms, s.rs, s.on, s.sg,
         s.gg, s.mix, s.tr, s.et, s.st0, s.st1) = ph.semaphores(
            "const z0 qk0 qk1 vo0 vo1 af abk mf mb o sq ss ms rs on sg gg mix tr et st0 st1")
        s.qk, s.vo, s.st = [s.qk0, s.qk1], [s.vo0, s.vo1], [s.st0, s.st1]
        qp = ph.sb("qp", [P, 2, GH, 4, CH])
        kT = ph.sb("kT", [P, 2, GH, P])
        vo = ph.sb("vo", [P, 2, 2 * GH * DV])
        mask = ph.sb("mask", [P, 2, P], U32)
        af = ph.sb("af", [P, 2, GH, P])
        ab = ph.sb("ab", [P, 2, GH, P])
        gg_ = ph.sb("gg_", [P, DV])
        sq = ph.sb("sq", [P, GH, DV])
        ss = ph.sb("ss", [P, GH])
        ms = ph.sb("ms", [P, GH])
        rs = ph.sb("rs", [P, GH])
        on = ph.sb("on", [P, GH, DV])
        sg = ph.sb("sg", [P, GH, DV])
        gg = ph.sb("gg", [P, GH, DV])
        mix = ph.sb("mix", [P, GH, DV])
        mT = ph.sb("mT", [P, 2, GH * P])
        p_f = ph.ps("p_f")
        p_b = ph.ps("p_b")
        p_o = [ph.ps("p_o0"), ph.ps("p_o1")]
        p_m = ph.ps("p_m")
        V0 = 2 * GH * DK

        with nc.Block() as block:

            @block.sync
            def _(sp):
                sp.dma_start(mask[:, :, :], g.d_mask).then_inc(s.const, 16)
                sp.dma_start(gg_[:, :], g.gla_norm_g.to_broadcast([P, DV])).then_inc(s.const, 16)
                sp.wait_ge(s.z0, 1)

                def step(U):
                    if T := U.at(3):
                        t, hf, par = T
                        sp.wait_ge(s.et, t + 1)
                        sp.dma_start(g.mix_tile(t)[:, 0:GH * P], mT[:, par, :]).then_inc(s.st[par], 16)
                    if T := U.at(0):
                        t, hf, par = T
                        wait(sp, s.o, t - 1)
                        src = g.qkT_tile(t).rearrange("p (h a c q) -> p h a c q", h=GH, a=2, c=2)
                        for c in range(2):
                            sp.dma_start(qp[:, par, :, 3 * c, :], src[:, :, 0, c, :]).then_inc(s.qk[par], 16)
                        sp.dma_start(kT[:, par], g.qkT_tile(t).rearrange("p (h a q) -> p h a q", h=GH, a=2)[:, :, 1, :]).then_inc(s.qk[par], 16)
                        wait(sp, s.sg, t - 1)
                        sp.dma_start(vo[:, par, :], g.proj_tile(t)[:, V0:V0 + 2 * GH * DV]).then_inc(s.vo[par], 16)

                steps(sp, 3, step)
                for par in range(2):
                    sp.wait_ge(s.st[par], 16 * (NT // 2))

            @block.gpsimd
            def _(pool):
                pool.wait_ge(s.const, 32)

                def step(U):
                    if T := U.at(1):
                        t, hf, par = T
                        pool.wait_ge(s.sg, t + 1)
                        wait(pool, s.mix, t)
                        pool.tensor_tensor(gg[:, :, :], sg[:, :, :], bc(gg_[:, :], 1, GH), ALU.mult).then_inc(s.gg, 1)
                        pool.wait_ge(s.ms, t + 1)
                        pool.tensor_tensor(rs[:, :], ms[:, :], g.neg_half[:, 0:GH], ALU.pow).then_inc(s.rs, 1)

                steps(pool, 3, step)

            @block.tensor
            def _(pe):
                def step(U):
                    if T := U.at(1):
                        t, hf, par = T
                        pe.wait_ge(s.qk[par], (hf + 1) * 48)
                        wait(pe, s.mf, t)
                        for r, (bank, done, free) in enumerate(((p_f, s.af, s.mf), (p_b, s.abk, s.mb))):
                            wait(pe, free, t)
                            rows = slice(r * DK, (r + 1) * DK)
                            for h in range(GH):
                                last = pe.matmul(bank[:, h * P:(h + 1) * P], kT[rows, par, h, :], qp[rows, par, h, 0:4:3, :], start=True, stop=True)
                            last.then_inc(done, 1)
                        pe.wait_ge(s.mf, t + 1)
                        pe.wait_ge(s.mb, t + 1)
                        pe.wait_ge(s.vo[par], (hf + 1) * 16)
                        wait(pe, s.on, t - 1)
                        ctx = cond_of(t)
                        chunk = 2 * (t - N_LAT) if ctx else 2 * t
                        for h in range(GH):
                            out = p_o[par][:, h * DV:(h + 1) * DV]
                            v = vo[:, par, h * DV:(h + 1) * DV]
                            pe.matmul(out, af[:, par, h, :], v, start=True, stop=False)
                            pe.matmul(out, ab[:, par, h, :], v, start=False, stop=False)
                            for c in range(2):
                                last = pe.matmul(out, qp[:, par, h, 2 * c:2 * c + 2, :].rearrange("p a q -> p (a q)"),
                                                 g.states[:, bass.ds(slot_of(chunk + c, ctx), 1), h, :].rearrange("p o v -> p (o v)"),
                                                 start=False, stop=c == 1)
                        last.then_inc(s.o, 1)
                    if T := U.at(2):
                        t, hf, par = T
                        pe.wait_ge(s.mix, t + 1)
                        wait(pe, s.et, t)
                        for h in range(GH):
                            last = pe.transpose(p_m[:, h * P:(h + 1) * P], mix[:, h, :], g.ident[:, :])
                        last.then_inc(s.tr, 1)

                steps(pe, 3, step)

            @block.scalar
            def _(act):
                def step(U):
                    if T := U.at(1):
                        t, hf, par = T
                        act.wait_ge(s.vo[par], (hf + 1) * 16)
                        wait(act, s.gg, t)
                        act.activation(sg[:, :, :].rearrange("p h v -> p (h v)"), vo[:, par, GH * DV:2 * GH * DV], ACT.Silu).then_inc(s.sg, 1)
                        act.wait_ge(s.o, t + 1)
                        wait(act, s.ss, t)
                        act.activation(sq[:, :, :].rearrange("p h v -> p (h v)"), p_o[par][:, :], ACT.Square).then_inc(s.sq, 1)
                    if T := U.at(2):
                        t, hf, par = T
                        act.wait_ge(s.tr, t + 1)
                        if not (isinstance(t, int) and t < 2):
                            act.wait_ge(s.st[par], hf * 16)
                        act.activation(mT[:, par, :], p_m[:, :], ACT.Copy).then_inc(s.et, 1)

                steps(act, 3, step)

            @block.vector
            def _(dve):
                dve.memset(qp[:, :, :, 1:3, :], 0.0).then_inc(s.z0, 1)
                dve.wait_ge(s.const, 32)

                def step(U):
                    if T := U.at(1):
                        t, hf, par = T
                        for r, (bank, done, to, got) in enumerate(((p_f, s.mf, af, s.af), (p_b, s.mb, ab, s.abk))):
                            dve.wait_ge(got, t + 1)
                            wait(dve, s.o, t - 1)
                            dve.tensor_tensor(to[:, par].bitcast(U32), bank[:, :].rearrange("p (h q) -> p h q", h=GH).bitcast(U32),
                                              bc(mask[:, r, :], 1, GH), ALU.bitwise_and).then_inc(done, 1)
                        dve.wait_ge(s.sq, t + 1)
                        dve.tensor_reduce(ss[:, :], sq[:, :, :], AX.X, ALU.add).then_inc(s.ss, 1)
                        dve.wait_ge(s.ss, t + 1)
                        dve.tensor_scalar(ms[:, :], ss[:, :], 1.0 / DV, EPS, ALU.mult, ALU.add).then_inc(s.ms, 1)
                        dve.wait_ge(s.rs, t + 1)
                        dve.tensor_tensor(on[:, :, :], p_o[par][:, :].rearrange("p (h v) -> p h v", h=GH), bc(rs[:, :], 2, DV),
                                          ALU.mult).then_inc(s.on, 1)
                        dve.wait_ge(s.on, t + 1)
                        dve.wait_ge(s.gg, t + 1)
                        wait(dve, s.tr, t)
                        dve.tensor_tensor(mix[:, :, :], on[:, :, :], gg[:, :, :], ALU.mult).then_inc(s.mix, 1)

                steps(dve, 3, step)


def output_projection(nc, g):
    with ExitStack() as stack:
        ph = Phase(nc, stack, "op")
        s = ph.s
        (s.gates, s.m0, s.m1, s.x0, s.x1, s.mhi, s.mlo, s.y0, s.y1, s.g0, s.g1, s.r, s.xs0, s.xs1, s.sq, s.ms, s.rstd,
         s.xn, s.tr, s.hT, s.hs0, s.hs1) = ph.semaphores(
            "gates m0 m1 x0 x1 mhi mlo y0 y1 g0 g1 r xs0 xs1 sq ms rstd xn tr hT hs0 hs1")
        s.m, s.x, s.y, s.gt, s.xs, s.hs = [s.m0, s.m1], [s.x0, s.x1], [s.y0, s.y1], [s.g0, s.g1], [s.xs0, s.xs1], [s.hs0, s.hs1]
        w_hi = ph.sb("w_hi", [P, KC, D_MODEL], F32R)
        w_lo = ph.sb("w_lo", [P, KC, D_MODEL], F32R)
        stage = ph.sb("stage", [P, 2, D_MODEL])
        gate = ph.sb("gate", [P, 2, D_MODEL])
        m = ph.sb("m", [P, 2, KC, P])
        mhi = ph.sb("mhi", [P, 2, KC, P], F32R)
        mlo = ph.sb("mlo", [P, 2, KC, P], F32R)
        x = ph.sb("x", [P, 2, D_MODEL])
        y = ph.sb("y", [P, D_MODEL])
        x1 = ph.sb("x1", [P, 2, D_MODEL])
        xn = ph.sb("xn", [P, D_MODEL])
        junk = ph.sb("junk", [P, D_MODEL])
        ss = ph.sb("ss", [P, 1])
        ms = ph.sb("ms", [P, 1])
        rstd = ph.sb("rstd", [P, 1])
        hT = ph.sb("hT", [P, 2, KC, P])
        p_y = [[ph.ps(f"p_y{a}{b}") for b in range(2)] for a in range(2)]
        p_t = ph.ps("p_t", 1024)
        w_sp, w_act, w_dve = load_split_weights(ph, s, g.w_out[0], KC, D_MODEL, w_hi, w_lo, stage)

        with nc.Block() as block:

            @block.sync
            def _(sp):
                for c in range(2):
                    sp.dma_start(gate[:, c, :], g.mod_d[c:c + 1, 2 * D_MODEL:3 * D_MODEL].to_broadcast([P, D_MODEL])).then_inc(s.gates, 16)
                w_sp(sp)

                def step(U):
                    if T := U.at(0):
                        t, hf, par = T
                        wait(sp, s.mlo, t - 1)
                        sp.dma_start(m[:, par].rearrange("p k q -> p (k q)"), g.mix_tile(t)).then_inc(s.m[par], 16)
                        wait(sp, s.r, t - 1)
                        sp.dma_start(x[:, par, :], g.x_tile(t)).then_inc(s.x[par], 16)
                    if T := U.at(3):
                        t, hf, par = T
                        sp.wait_ge(s.r, t + 1)
                        sp.dma_start(g.x1_tile(t), x1[:, par, :]).then_inc(s.xs[par], 16)
                steps(sp, 4, step)
                for par in range(2):
                    sp.wait_ge(s.xs[par], 16 * (NT // 2))

            @block.gpsimd
            def _(pool):
                def step(U):
                    if T := U.at(2):
                        t, hf, par = T
                        pool.wait_ge(s.ms, t + 1)
                        pool.tensor_tensor(rstd[:, :], ms[:, :], g.neg_half[:, 0:1], ALU.pow).then_inc(s.rstd, 1)
                    if T := U.at(4):
                        t, hf, par = T
                        pool.wait_ge(s.hT, t + 1)
                        pool.dma_start(g.h2_tile(t), hT[:, par]).then_inc(s.hs[par], 16)

                steps(pool, 4, step)
                for par in range(2):
                    pool.wait_ge(s.hs[par], 16 * (NT // 2))

            @block.tensor
            def _(pe):
                pe.wait_ge(s.w_lo, KC)

                def step(U):
                    if T := U.at(1):
                        t, hf, par = T
                        pe.wait_ge(s.mlo, t + 1)
                        for n in range(2):
                            wait(pe, s.gt[n], t - 1)
                            for k in range(KC):
                                last = split_product(pe, p_y[par][n][:, :], ((mhi[:, par, k], mlo[:, par, k]),
                                                     (w_hi[:, k, n * 512:(n + 1) * 512], w_lo[:, k, n * 512:(n + 1) * 512])),
                                                     k == 0, k == KC - 1)
                            last.then_inc(s.y[n], 1)
                    if T := U.at(3):
                        t, hf, par = T
                        pe.wait_ge(s.xn, t + 1)
                        wait(pe, s.hT, t)
                        for k in range(KC):
                            last = pe.transpose(p_t[:, k * P:(k + 1) * P], xn[:, k * P:(k + 1) * P], g.ident[:, :])
                        last.then_inc(s.tr, 1)

                steps(pe, 4, step)

            @block.scalar
            def _(act):
                w_act(act)

                def step(U):
                    if T := U.at(0):
                        t, hf, par = T
                        act.wait_ge(s.m[par], (hf + 1) * 16)
                        wait(act, s.y[1], t - 1)
                        act.activation(mhi[:, par], m[:, par], ACT.Copy).then_inc(s.mhi, 1)
                    if T := U.at(2):
                        t, hf, par = T
                        act.wait_ge(s.r, t + 1)
                        wait(act, s.ms, t)
                        act.activation(junk[:, :], x1[:, par, :], ACT.Square, accum_out=ss[:, :]).then_inc(s.sq, 1)
                    if T := U.at(3):
                        t, hf, par = T
                        act.wait_ge(s.tr, t + 1)
                        if not (isinstance(t, int) and t < 2):
                            act.wait_ge(s.hs[par], hf * 16)
                        c = cond_of(t)
                        for k in range(KC):
                            last = act.activation(hT[:, par, k, :], p_t[:, k * P:(k + 1) * P], ACT.Identity,
                                                  bias=g.lnp[:, 1, c, 1, k:k + 1], scale=g.lnp[:, 1, c, 0, k:k + 1])
                        last.then_inc(s.hT, 1)

                steps(act, 4, step)

            @block.vector
            def _(dve):
                w_dve(dve)
                dve.wait_ge(s.gates, 32)

                def step(U):
                    if T := U.at(0):
                        t, hf, par = T
                        dve.wait_ge(s.mhi, t + 1)
                        dve.tensor_tensor(mlo[:, par], m[:, par], mhi[:, par].bitcast(F32), ALU.subtract).then_inc(s.mlo, 1)
                    if T := U.at(2):
                        t, hf, par = T
                        c = cond_of(t)
                        for n in range(2):
                            dve.wait_ge(s.y[n], t + 1)
                            cols = slice(n * 512, (n + 1) * 512)
                            dve.tensor_tensor(y[:, cols], p_y[par][n][:, :], gate[:, c, cols], ALU.mult).then_inc(s.gt[n], 1)
                        dve.wait_ge(s.gt[0], t + 1)
                        dve.wait_ge(s.gt[1], t + 1)
                        dve.wait_ge(s.x[par], (hf + 1) * 16)
                        if not (isinstance(t, int) and t < 2):
                            dve.wait_ge(s.xs[par], hf * 16)
                        dve.tensor_tensor(x1[:, par, :], y[:, :], x[:, par, :], ALU.add).then_inc(s.r, 1)
                        dve.wait_ge(s.sq, t + 1)
                        dve.tensor_scalar(ms[:, :], ss[:, :], 1.0 / D_MODEL, EPS, ALU.mult, ALU.add).then_inc(s.ms, 1)
                        dve.wait_ge(s.rstd, t + 1)
                        wait(dve, s.tr, t)
                        dve.tensor_scalar(xn[:, :], x1[:, par, :], rstd[:, :], None, ALU.mult).then_inc(s.xn, 1)

                steps(dve, 4, step)


def feed_forward(nc, g):
    BT = 512
    BTT = BT // P
    HN = 512
    KG = 4
    DOWN = [(n, k, min(k + KG, NF)) for n in range(2) for k in range(0, NF, KG)]
    ITEMS = NF + len(DOWN)
    N_LB = T_LAT // BT
    with ExitStack() as stack:
        ph = Phase(nc, stack, "ff")
        s = ph.s
        (s.w0, s.w1, s.w_hi, s.w_lo, s.h0, s.h1, s.h_hi, s.h_lo, s.fing, s.x, s.a, s.used, s.silu, s.mul, s.ghi, s.glo,
         s.y, s.gt, s.res, s.sq, s.ms, s.rs, s.fin, s.out) = ph.semaphores(
            "w0 w1 w_hi w_lo h0 h1 h_hi h_lo fing x a used silu mul ghi glo y gt res sq ms rs fin out")
        s.w = [s.w0, s.w1]
        ws = ph.sb("ws", [P, 2, 2 * KC * P])
        whi = ph.sb("whi", [P, 2, 2 * KC * P], F32R)
        wlo = ph.sb("wlo", [P, 2, 2 * KC * P], F32R)
        hs = ph.sb("hs", [P, 2, BT])
        hhi = ph.sb("hhi", [P, KC, BT], F32R)
        hlo = ph.sb("hlo", [P, KC, BT], F32R)
        ghi = ph.sb("ghi", [P, NF, BT], F32R)
        glo = ph.sb("glo", [P, NF, BT], F32R)
        sil = ph.sb("sil", [P, 2, BT])
        tmp = ph.sb("tmp", [P, HN])
        x1 = ph.sb("x1", [P, BTT, D_MODEL])
        gate = ph.sb("gate", [P, D_MODEL])
        fing = ph.sb("fing", [P, D_MODEL])
        ss = ph.sb("ss", [P, BTT])
        ms = ph.sb("ms", [P, BTT])
        rs = ph.sb("rs", [P, BTT])
        bank = [ph.ps(f"p{j}") for j in range(8)]
        w13 = [w[0].rearrange("(k p) n -> p k n", p=P) for w in (g.w_ffn1, g.w_ffn3)]
        w2 = g.w_ffn2[0].rearrange("(k p) n -> p k n", p=P)

        def width(b):
            return T_CTX if isinstance(b, int) and b == N_LB else BT

        def blocks(eng, body):
            body(0)
            with eng.Fori(1, N_LB - 1) as b:
                body(b)
            body(N_LB - 1)
            body(N_LB)

        def up_items(eng, b, body):
            for par in range(2):
                body(par, par, b * ITEMS + par, b * (ITEMS // 2))
            with eng.Fori(1, NF // 2) as i:
                for par in range(2):
                    body(i * 2 + par, par, b * ITEMS + i * 2 + par, b * (ITEMS // 2) + i)

        def down_items(b, body):
            for i, (n, k0, k1) in enumerate(DOWN):
                body(i, n, k0, k1, i % 2, b * ITEMS + (NF + i), b * (ITEMS // 2) + (NF + i) // 2)

        def h_rows(i):
            return range(2 * (i - 1), 2 * i) if 1 <= i <= KC // 2 else ()

        with nc.Block() as block:

            @block.sync
            def _(sp):
                def load_h(b, k):
                    wait(sp, s.h_lo, b * KC + (k - 1))
                    sp.dma_start(hs[:, k % 2, 0:width(b)], g.h2_rows(b, k, width(b))).then_inc([s.h0, s.h1][k % 2], 16)

                for k in range(KC):
                    load_h(0, k)

                def body(b):
                    def up(f, par, item, pair):
                        wait(sp, s.w_lo, item - 1)
                        for j in range(2):
                            sp.dma_start(ws[:, par, j * KC * P:(j + 1) * KC * P].rearrange("p (k n) -> p k n", k=KC),
                                         w13[j][:, :, bass.ds(f * P, P)]).then_inc(s.w[par], 16)

                    def down(i, n, k0, k1, par, item, pair):
                        wait(sp, s.w_lo, item - 1)
                        mid = (k0 + k1) // 2
                        for ka, kb in ((k0, mid), (mid, k1)):
                            sp.dma_start(ws[:, par, (ka - k0) * HN:(kb - k0) * HN].rearrange("p (k n) -> p k n", n=HN),
                                         w2[:, ka:kb, n * HN:(n + 1) * HN]).then_inc(s.w[par], 16)
                        if not (isinstance(b, int) and b == N_LB):
                            for k in h_rows(i):
                                load_h(b + 1, k)

                    up_items(sp, b, up)
                    down_items(b, down)

                blocks(sp, body)

            @block.gpsimd
            def _(pool):
                pool.dma_start(fing[:, :], g.final_g.rearrange("(a n) -> a n", a=1).to_broadcast([P, D_MODEL])).then_inc(s.fing, 16)

                def body(b):
                    nt = width(b) // P
                    wait(pool, s.out, b * (16 * BTT))
                    pool.dma_start(x1[:, 0:nt, :], g.x1_rows(b, width(b))).then_inc(s.x, 16)
                    pool.dma_start(gate[:, :], g.gate2(b)).then_inc(s.x, 16)
                    for t in range(nt):
                        pool.wait_ge(s.ms, b * BTT + (t + 1))
                        pool.tensor_tensor(rs[:, t:t + 1], ms[:, t:t + 1], g.neg_half[:, 0:1], ALU.pow).then_inc(s.rs, 1)
                    for t in range(nt):
                        pool.wait_ge(s.fin, b * BTT + (t + 1))
                        pool.dma_start(g.y_rows(b, t), x1[:, t, :]).then_inc(s.out, 16)

                blocks(pool, body)
                pool.wait_ge(s.out, 16 * NT)

            @block.tensor
            def _(pe):
                def body(b):
                    bt = width(b)
                    nt = bt // P

                    def up(f, par, item, pair):
                        pe.wait_ge(s.w_lo, item + 1)
                        if isinstance(f, int) and f == 0:
                            pe.wait_ge(s.h_lo, b * KC + KC)
                            wait(pe, s.res, b * (2 * BTT))
                        wait(pe, s.glo, b * NF + (f - 1))
                        for j in range(2):
                            for k in range(KC):
                                c = slice((j * KC + k) * P, (j * KC + k + 1) * P)
                                last = split_product(pe, bank[2 * par + j][:, 0:bt], ((whi[:, par, c], wlo[:, par, c]),
                                                     (hhi[:, k, 0:bt], hlo[:, k, 0:bt])), k == 0, k == KC - 1)
                            last.then_inc(s.used if j else s.a, 1)

                    def down(i, n, k0, k1, par, item, pair):
                        pe.wait_ge(s.w_lo, item + 1)
                        pe.wait_ge(s.glo, b * NF + (k1 if n == 0 else NF))
                        last_item = k1 == NF
                        order = [(k, t) for t in range(nt) for k in range(k0, k1)] if last_item else \
                                [(k, t) for k in range(k0, k1) for t in range(nt)]
                        for k, t in order:
                            c = slice((k - k0) * HN, (k - k0 + 1) * HN)
                            q = slice(t * P, (t + 1) * P)
                            last = split_product(pe, bank[4 * (1 - n) + t][:, :], ((ghi[:, k, q], glo[:, k, q]),
                                                 (whi[:, par, c], wlo[:, par, c])), k == 0, k == NF - 1)
                            if k == NF - 1 and t < nt - 1:
                                last.then_inc(s.y, 1)
                        last.then_inc(s.used, 1)

                    up_items(pe, b, up)
                    down_items(b, down)

                blocks(pe, body)

            def weights_high(act, par, item, pair, cols):
                act.wait_ge(s.w[par], pair * 32 + 32)
                wait(act, s.used, item - 1)
                act.activation(whi[:, par, 0:cols], ws[:, par, 0:cols], ACT.Copy).then_inc(s.w_hi, 1)

            def weights_low(dve, par, item, pair, cols):
                dve.wait_ge(s.w_hi, item + 1)
                dve.tensor_tensor(wlo[:, par, 0:cols], ws[:, par, 0:cols], whi[:, par, 0:cols].bitcast(F32), ALU.subtract).then_inc(s.w_lo, 1)

            @block.scalar
            def _(act):
                def h_high(b, k):
                    act.wait_ge([s.h0, s.h1][k % 2], b * (KC // 2 * 16) + (k // 2 + 1) * 16)
                    act.activation(hhi[:, k, 0:width(b)], hs[:, k % 2, 0:width(b)], ACT.Copy).then_inc(s.h_hi, 1)

                for k in range(KC):
                    h_high(0, k)

                def squares(b):
                    for t in range(width(b) // P):
                        act.wait_ge(s.res, b * (2 * BTT) + (width(b) // P + t + 1))
                        wait(act, s.sq, b * BTT + t)
                        act.activation(sil[:, :, :].rearrange("p a n -> p (a n)"), x1[:, t, :], ACT.Square, accum_out=ss[:, t:t + 1]).then_inc(s.sq, 1)

                def silu(b, f, par):
                    act.wait_ge(s.a, b * NF + (f + 1))
                    wait(act, s.glo, b * NF + (f - 1))
                    act.activation(sil[:, par, 0:width(b)], bank[2 * par][:, 0:width(b)], ACT.Silu).then_inc(s.silu, 1)

                def body(b):
                    def up(f, par, item, pair):
                        weights_high(act, par, item, pair, 2 * KC * P)
                        if isinstance(f, int) and f == 0:
                            return
                        if isinstance(f, int) and f == 1 and not (isinstance(b, int) and b == 0):
                            act.wait_ge(s.glo, b * NF)
                            squares(b - 1)
                            act.wait_ge(s.sq, b * BTT)
                        silu(b, f - 1, 1 - par)

                    def down(i, n, k0, k1, par, item, pair):
                        weights_high(act, par, item, pair, (k1 - k0) * HN)
                        if i == 0:
                            silu(b, NF - 1, 1)
                        if not (isinstance(b, int) and b == N_LB):
                            for k in h_rows(i):
                                act.wait_ge(s.used, b * ITEMS + NF)
                                h_high(b + 1, k)

                    up_items(act, b, up)
                    down_items(b, down)

                blocks(act, body)
                squares(N_LB)

            @block.vector
            def _(dve):
                def h_low(b, k):
                    dve.wait_ge(s.h_hi, b * KC + (k + 1))
                    dve.tensor_tensor(hlo[:, k, 0:width(b)], hs[:, k % 2, 0:width(b)], hhi[:, k, 0:width(b)].bitcast(F32), ALU.subtract).then_inc(s.h_lo, 1)

                for k in range(KC):
                    h_low(0, k)

                def residual(b, n):
                    nt = width(b) // P
                    cols = slice(n * HN, (n + 1) * HN)
                    for t in range(nt):
                        done = b * (2 * BTT) + (n * nt + t)
                        if t < nt - 1:
                            dve.wait_ge(s.y, b * (2 * (BTT - 1)) + (n * (nt - 1) + t + 1))
                        else:
                            dve.wait_ge(s.used, b * ITEMS + (NF + (n + 1) * (len(DOWN) // 2)))
                        wait(dve, s.res, done)
                        dve.tensor_tensor(tmp[:, :], bank[4 * (1 - n) + t][:, :], gate[:, cols], ALU.mult).then_inc(s.gt, 1)
                        dve.wait_ge(s.gt, done + 1)
                        dve.tensor_tensor(x1[:, t, cols], x1[:, t, cols], tmp[:, :], ALU.add).then_inc(s.res, 1)

                def final_norm(b):
                    for t in range(width(b) // P):
                        done = b * BTT + t
                        dve.wait_ge(s.sq, done + 1)
                        dve.tensor_scalar(ms[:, t:t + 1], ss[:, t:t + 1], 1.0 / D_MODEL, EPS, ALU.mult, ALU.add).then_inc(s.ms, 1)
                        dve.wait_ge(s.rs, done + 1)
                        dve.scalar_tensor_tensor(x1[:, t, :], x1[:, t, :], rs[:, t:t + 1], fing[:, :], ALU.mult, ALU.mult).then_inc(s.fin, 1)

                def gated(b, f, par):
                    dve.wait_ge(s.silu, b * NF + (f + 1))
                    dve.wait_ge(s.used, b * ITEMS + (f + 1))
                    bt = width(b)
                    dve.tensor_tensor(sil[:, par, 0:bt], sil[:, par, 0:bt], bank[2 * par + 1][:, 0:bt], ALU.mult).then_inc(s.mul, 1)
                    dve.wait_ge(s.mul, b * NF + (f + 1))
                    hi = ghi[:, bass.ds(f, 1), 0:bt].rearrange("p o q -> p (o q)")
                    lo = glo[:, bass.ds(f, 1), 0:bt].rearrange("p o q -> p (o q)")
                    dve.tensor_copy(hi, sil[:, par, 0:bt]).then_inc(s.ghi, 1)
                    dve.wait_ge(s.ghi, b * NF + (f + 1))
                    dve.tensor_tensor(lo, sil[:, par, 0:bt], hi.bitcast(F32), ALU.subtract).then_inc(s.glo, 1)

                def body(b):
                    def up(f, par, item, pair):
                        weights_low(dve, par, item, pair, 2 * KC * P)
                        begin = isinstance(f, int) and not (isinstance(b, int) and b == 0)
                        if begin and f == 0:
                            residual(b - 1, 1)
                        if begin and f == 1:
                            final_norm(b - 1)
                        if not (isinstance(f, int) and f == 0):
                            gated(b, f - 1, 1 - par)

                    def down(i, n, k0, k1, par, item, pair):
                        weights_low(dve, par, item, pair, (k1 - k0) * HN)
                        if i == 0:
                            gated(b, NF - 1, 1)
                        if not (isinstance(b, int) and b == N_LB):
                            for k in h_rows(i):
                                h_low(b + 1, k)
                        if i == len(DOWN) // 2 + 1:
                            dve.wait_ge(s.x, b * 32 + 32)
                            residual(b, 0)

                    up_items(dve, b, up)
                    down_items(b, down)

                dve.wait_ge(s.fing, 16)
                blocks(dve, body)
                residual(N_LB, 1)
                final_norm(N_LB)


def hybrid_block(nc, a, outs, consts):
    with ExitStack() as top:
        g = Names()
        (g.c, g.c_ctx, g.ada_w, g.ada_b, g.norm1_g, g.norm2_g, g.w_in, g.w_gk2, g.b_gk2, g.gla_norm_g, g.q_norm_g, g.k_norm_g,
         g.w_out, g.w_ffn1, g.w_ffn3, g.w_ffn2, g.final_g) = (a[name] for name in _INS[6:])
        g.d_ident, g.d_tri, g.d_ind, g.d_mask, d_rope = consts
        y_prompt, y_sample, new_k, new_v, new_f, new_b = outs
        g.new_k = new_k.rearrange("b l t h d -> (b l t) (h d)")
        g.new_v = new_v.rearrange("b l t h d -> (b l t) (h d)")
        g.new_f, g.new_b = new_f[0, 0], new_b[0, 0]
        g.cache_k = a["cache_k"].rearrange("b l t h d -> (b l t) (h d)")
        g.cache_v = a["cache_v"].rearrange("b l t h d -> (b l t) (h d)")
        g.state_f, g.state_b = a["state_gla_fwd"][0, 0], a["state_gla_bwd"][0, 0]

        def scratch(name, shape, dt=F32):
            return nc.dram_tensor(name, shape, dt, kind="Internal").ap()

        g.mod_d = scratch("mod_d", (2, N_MOD * D_MODEL))
        qT_d = scratch("qT_d", (NT, P, AH * P))
        mix_d = scratch("mix_d", (NT, P, KC * P))
        proj_d = scratch("proj_d", (NT * P, D_GLA))
        qkT_d = scratch("qkT_d", (NT, P, 2 * GH * P))
        x1_d = scratch("x1_d", (NT * P, D_MODEL))
        h2_d = scratch("h2_d", (KC, P, NT * P))

        def tile_of(d):
            return lambda t: d[bass.ds(t, 1)].rearrange("o p n -> (o p) n")

        def rows_of(lat, ctx):
            return lambda t: ctx[(t - N_LAT) * P:(t - N_LAT + 1) * P, :] if cond_of(t) else lat[bass.ds(t * P, P), :]

        g.qT_tile, g.mix_tile, g.qkT_tile = tile_of(qT_d), tile_of(mix_d), tile_of(qkT_d)
        g.proj_tile = lambda t: proj_d[bass.ds(t * P, P), :]
        g.rope_tile = lambda t: d_rope[bass.ds(t * P, P), :]
        g.x1_tile = lambda t: x1_d[bass.ds(t * P, P), :]
        g.x_tile = rows_of(a["x_sample"][0], a["x_prompt"][0])
        g.h2_tile = lambda t: h2_d[:, :, bass.ds(t * P, P)].rearrange("k p q -> p k q")
        g.h2_rows = lambda b, k, n: h2_d[k, :, bass.ds(b * 512, n)]
        g.x1_rows = lambda b, n: x1_d[bass.ds(b * 512, n), :].rearrange("(t p) n -> p t n", p=P)
        y_tile = rows_of(y_sample[0], y_prompt[0])
        g.y_rows = lambda b, t: y_tile(b * 4 + t)

        def gate2(b):
            c = 1 if isinstance(b, int) and b == T_LAT // 512 else 0
            return g.mod_d[c:c + 1, 5 * D_MODEL:6 * D_MODEL].to_broadcast([P, D_MODEL])

        g.gate2 = gate2
        g.ident = top.enter_context(nc.sbuf_tensor("ident", [P, P], F32))
        g.lnp = top.enter_context(nc.sbuf_tensor("lnp", [P, 2, 2, 2, KC], F32))
        g.neg_half = top.enter_context(nc.sbuf_tensor("neg_half", [P, 16], F32))
        modulation(nc, g)
        with ExitStack() as att:
            g.keysT = att.enter_context(nc.sbuf_tensor("keysT", [P, KVH, 2, (N_LAT + 4) * P], F32R))
            g.vals = att.enter_context(nc.sbuf_tensor("vals", [P, (N_LAT + 4) * KVH, 2 * HD], F32R))
            attention_projection(nc, g)
            attention(nc, g)
        gla_projection(nc, g)
        with ExitStack() as gla:
            g.states = gla.enter_context(nc.sbuf_tensor("states", [P, SLOTS, GH, DV], F32))
            g.decay = gla.enter_context(nc.sbuf_tensor("decay", [P, GH, NT * 2], F32))
            gla_states(nc, g)
            gla_outputs(nc, g)
        output_projection(nc, g)
        feed_forward(nc, g)


_INS = ["x_prompt", "x_sample", "cache_k", "cache_v", "state_gla_fwd", "state_gla_bwd", "c", "c_ctx", "ada_w", "ada_b", "norm1_g",
        "norm2_g", "w_in", "w_gk2", "b_gk2", "gla_norm_g", "q_norm_g", "k_norm_g", "w_out", "w_ffn1", "w_ffn3", "w_ffn2", "final_g"]
_OUTS = [(1, T_CTX, D_MODEL), (1, T_LAT, D_MODEL), (1, 1, T_CTX, KVH, HD), (1, 1, T_CTX, KVH, HD), (1, 1, GH, DK, DV), (1, 1, GH, DK, DV)]


def _constants():
    j, i = np.meshgrid(np.arange(P), np.arange(P), indexing="ij")
    same = (i // CH) == (j // CH)
    tri = np.stack([same & (j <= i), same & (j >= i), same & (j > i), same & (j < i)], axis=1).astype(np.float32)
    ind = ((np.arange(P)[:, None] // CH) == np.arange(2)[None, :]).astype(np.float32)
    t = np.arange(T_LAT)
    half = HD // 4
    inv = (np.float32(10000.0) ** (-np.arange(0, 2 * half, 2, dtype=np.float32) / np.float32(2 * half))).astype(np.float32)
    pos = np.stack([t // GRID_W, t % GRID_W], axis=1).astype(np.float32)
    ang = pos[:, :, None] * inv
    c, sn = np.cos(ang), np.sin(ang)
    rope = np.zeros((NT * P, 2, 2, 2, half), np.float32)
    rope[:, 0] = 1.0
    rope[:T_LAT, 0] = c[:, :, None, :]
    rope[:T_LAT, 1, :, 0] = -sn
    rope[:T_LAT, 1, :, 1] = sn
    bits = np.where(tri[:, 0:2] > 0, np.uint32(0xFFFFFFFF), np.uint32(0))
    return [np.eye(P, dtype=np.float32), tri, ind, bits, rope.reshape(NT * P, 2 * HD)]


def lay_out(nc, inputs):
    arrays, args, outs, consts = {}, {}, [], []
    for name in _INS:
        x = np.ascontiguousarray(inputs[name])
        arrays[f"in_{name}_dram"] = x
        args[name] = nc.dram_tensor(f"in_{name}_dram", x.shape, mybir.dt.from_np(x.dtype), kind="ExternalInput").ap()
    for n, x in enumerate(_constants()):
        arrays[f"const_{n}_dram"] = x
        consts.append(nc.dram_tensor(f"const_{n}_dram", x.shape, mybir.dt.from_np(x.dtype), kind="ExternalInput").ap())
    for n, shape in enumerate(_OUTS):
        outs.append(nc.dram_tensor(f"out_{n}_dram", shape, F32, kind="ExternalOutput").ap())
    hybrid_block(nc, args, outs, consts)
    return arrays


def kernel(**inputs):
    import concourse.bacc as _bacc
    from concourse.bass_utils import run_bass_kernel_spmd as _run

    nc = _bacc.Bacc("TRN2", target_bir_lowering=False, num_devices=1)
    arrays = lay_out(nc, inputs)
    r = _run(nc, [arrays], core_ids=[0])
    return tuple(r.results[0][f"out_{n}_dram"] for n in range(len(_OUTS)))
```

```python
from contextlib import ExitStack

import numpy as np

import concourse.bass as bass
from concourse import mybir

F32 = mybir.dt.float32
F32R = mybir.dt.float32r
U32 = mybir.dt.uint32
ALU = mybir.AluOpType
ACT = mybir.ActivationFunctionType
AX = mybir.AxisListType

P = 128
D_MODEL = 1024
KC = D_MODEL // P
T_LAT = 2048
T_CTX = 256
PAST = 256
N_LAT = T_LAT // P
N_CTX = T_CTX // P
NT = N_LAT + N_CTX
GH = 4
DK = 64
DV = 128
LR = 16
AH = 8
KVH = 2
HD = 64
D_GLA = 2 * GH * DK + 2 * GH * DV + 2 * LR
D_ATT = AH * HD + 2 * KVH * HD
D_FF = 2816
NF = D_FF // P
EPS = 1e-6
CH = 64
N_MOD = 6
GRID_W = 64
LAT_SLOTS = T_LAT // CH + 2
CTX_SLOTS = T_CTX // CH + 2
SLOTS = LAT_SLOTS + CTX_SLOTS


def wait(eng, sem, value):
    if not (isinstance(value, int) and value <= 0):
        eng.wait_ge(sem, value)


class Step:

    def __init__(self, half, par, static):
        self.half, self.par, self.static = half, par, static

    def at(self, off):
        t = 2 * self.half + self.par - off if self.static else self.half * 2 + (self.par - off)
        if self.static:
            return (t, t // 2, t % 2) if 0 <= t < NT else None
        return t, self.half + (self.par - off) // 2, (self.par - off) % 2


def steps(eng, depth, body):
    first = (depth + 2) // 2
    for u in range(2 * first):
        body(Step(u // 2, u % 2, True))
    with eng.Fori(first, N_LAT // 2) as i:
        for par in range(2):
            body(Step(i, par, False))
    for u in range(N_LAT, NT + depth):
        body(Step(u // 2, u % 2, True))


def cond_of(t):
    return 1 if isinstance(t, int) and t >= N_LAT else 0


def bc(ap, axis, n):
    a = ap.unsqueeze(axis)
    shape = list(a.shape)
    shape[axis] = n
    return a.to_broadcast(shape)


class Names:
    pass


class Phase:

    def __init__(self, nc, stack, name):
        self.nc, self.stack, self.name = nc, stack, name
        self.s = Names()
        self.handles = []
        stack.callback(self.clear)

    def semaphores(self, names):
        new = [self.nc.alloc_semaphore(name=f"{self.name}_{n}") for n in names.split()]
        self.handles += new
        return new

    def clear(self):
        self.nc.clear_and_free_semaphores(self.handles)
        self.nc.all_engine_barrier()

    def sb(self, name, shape, dt=F32):
        return self.stack.enter_context(self.nc.sbuf_tensor(f"{self.name}_{name}", shape, dt))

    def ps(self, name, cols=512):
        return self.stack.enter_context(self.nc.psum_tensor(f"{self.name}_{name}", [P, cols], F32))


def modulation(nc, g):
    NCH = N_MOD * D_MODEL // 512
    with ExitStack() as stack:
        ph = Phase(nc, stack, "mod")
        s = ph.s
        (s.rows, s.w0, s.w1, s.silu, s.tr, s.cT, s.acc, s.bias, s.out, s.back, s.mtr, s.mT, s.done) = ph.semaphores(
            "rows w0 w1 silu tr cT acc bias out back mtr mT done")
        s.w = [s.w0, s.w1]
        crow = ph.sb("crow", [2 * KC, P])
        nrow = ph.sb("nrow", [2 * KC, P])
        srow = ph.sb("srow", [2 * KC, P])
        adab = ph.sb("adab", [2, N_MOD * D_MODEL])
        mod = ph.sb("mod", [2, N_MOD * D_MODEL])
        aw = ph.sb("aw", [P, 2, KC, 512])
        cT = ph.sb("cT", [P, 2 * KC])
        nT = ph.sb("nT", [P, 2 * KC])
        modr = ph.sb("modr", [2 * N_MOD * KC, P])
        modT = ph.sb("modT", [P, 2, N_MOD, KC])
        p_tr = ph.ps("p_tr")
        p_acc = [ph.ps("p_acc0"), ph.ps("p_acc1")]
        ada_w = g.ada_w.rearrange("l (k p) n -> p (l k) n", p=P)

        with nc.Block() as block:

            @block.sync
            def _(sp):
                sp.dma_start(g.ident[:, :], g.d_ident).then_inc(s.rows, 16)
                sp.dma_start(crow[0:KC, :], g.c.rearrange("a (k p) -> (a k) p", p=P)).then_inc(s.rows, 16)
                sp.dma_start(crow[KC:2 * KC, :], g.c_ctx.rearrange("(k p) -> k p", p=P)).then_inc(s.rows, 16)
                sp.dma_start(nrow[0:KC, :], g.norm1_g.rearrange("l (k p) -> (l k) p", p=P)).then_inc(s.rows, 16)
                sp.dma_start(nrow[KC:2 * KC, :], g.norm2_g.rearrange("l (k p) -> (l k) p", p=P)).then_inc(s.rows, 16)
                for r in range(2):
                    sp.dma_start(adab[r:r + 1, :], g.ada_b).then_inc(s.rows, 16)
                for n in range(2):
                    sp.dma_start(aw[:, n], ada_w[:, :, n * 512:(n + 1) * 512]).then_inc(s.w[n], 16)
                with sp.Fori(1, NCH // 2) as i:
                    for par in range(2):
                        sp.wait_ge(s.acc, i * 2 + (par - 1))
                        sp.dma_start(aw[:, par], ada_w[:, :, bass.ds(i * 1024 + par * 512, 512)]).then_inc(s.w[par], 16)
                sp.wait_ge(s.bias, NCH)
                sp.dma_start(g.mod_d, mod[:, :]).then_inc(s.out, 16)
                sp.wait_ge(s.out, 16)
                sp.dma_start(modr[:, :], g.mod_d.rearrange("c (j p) -> (c j) p", p=P)).then_inc(s.back, 16)

            @block.scalar
            def _(act):
                act.wait_ge(s.rows, 16 * 7)
                act.activation(srow[:, :], crow[:, :], ACT.Silu).then_inc(s.silu, 1)

            @block.tensor
            def _(pe):
                pe.wait_ge(s.silu, 1)
                pe.transpose(p_tr[:, 0:2 * KC], srow[:, :], g.ident[0:2 * KC, 0:2 * KC])
                pe.transpose(p_tr[:, 2 * KC:4 * KC], nrow[:, :], g.ident[0:2 * KC, 0:2 * KC]).then_inc(s.tr, 1)
                pe.wait_ge(s.cT, 1)

                def chunk(n, half, par):
                    pe.wait_ge(s.w[par], (half + 1) * 16)
                    wait(pe, s.bias, n - 1)
                    for k in range(KC):
                        last = pe.matmul(p_acc[par][0:2, :], cT[:, k::KC], aw[:, par, k, :], start=k == 0, stop=k == KC - 1)
                    last.then_inc(s.acc, 1)

                chunk(0, 0, 0)
                chunk(1, 0, 1)
                with pe.Fori(1, NCH // 2) as i:
                    for par in range(2):
                        chunk(i * 2 + par, i, par)
                pe.wait_ge(s.back, 16)
                pe.transpose(p_tr[:, 64:64 + 2 * N_MOD * KC], modr[:, :], g.ident[0:96, 0:96]).then_inc(s.mtr, 1)

            @block.vector
            def _(dve):
                dve.memset(g.neg_half[:, :], -0.5)
                dve.wait_ge(s.tr, 1)
                dve.tensor_copy(nT[:, :], p_tr[:, 2 * KC:4 * KC])
                dve.tensor_copy(cT[:, :], p_tr[:, 0:2 * KC]).then_inc(s.cT, 1)
                with dve.Fori(0, NCH // 2) as i:
                    for par in range(2):
                        dve.wait_ge(s.acc, i * 2 + (par + 1))
                        cols = bass.ds(i * 1024 + par * 512, 512)
                        dve.tensor_tensor(mod[:, cols], p_acc[par][0:2, :], adab[:, cols], ALU.add).then_inc(s.bias, 1)
                dve.wait_ge(s.mtr, 1)
                dve.tensor_copy(modT[:, :, :, :], p_tr[:, 64:64 + 2 * N_MOD * KC].rearrange("p (c m k) -> p c m k", c=2, m=N_MOD)).then_inc(s.mT, 1)
                dve.wait_ge(s.mT, 1)
                for n in range(2):
                    for c in range(2):
                        dve.scalar_tensor_tensor(g.lnp[:, n, c, 0, :], modT[:, c, 3 * n + 1, :], 1.0,
                                                 nT[:, n * KC:(n + 1) * KC], ALU.add, ALU.mult)
                        last = dve.tensor_copy(g.lnp[:, n, c, 1, :], modT[:, c, 3 * n, :])
                last.then_inc(s.done, 1)
                dve.wait_ge(s.done, 1)


class Front:

    def __init__(self, ph, s, g, norm, used):
        self.s, self.g, self.norm, self.used = s, g, norm, used
        (s.x0, s.x1, s.sq, s.ms, s.rstd, s.xn, s.tr, s.hT, s.hi, s.split) = ph.semaphores("x0 x1 sq ms rstd xn tr hT hi split")
        self.x = ph.sb("x", [P, 2, D_MODEL])
        self.junk = ph.sb("junk", [P, D_MODEL])
        self.ss = ph.sb("ss", [P, 2, 1])
        self.ms = ph.sb("ms", [P, 2, 1])
        self.rstd = ph.sb("rstd", [P, 2, 1])
        self.hT = ph.sb("hT", [P, KC, P])
        self.hi = ph.sb("hi", [P, 2, KC, P], F32R)
        self.lo = ph.sb("lo", [P, 2, KC, P], F32R)
        self.p_tr = ph.ps("p_tr", 1024)

    def load(self, sp, T):
        t, half, par = T
        wait(sp, self.s.tr, t - 1)
        src = self.g.x_tile(t)
        sp.dma_start(self.x[:, par, :], src).then_inc([self.s.x0, self.s.x1][par], 16)

    def squares(self, act, T):
        t, half, par = T
        act.wait_ge([self.s.x0, self.s.x1][par], (half + 1) * 16)
        wait(act, self.s.sq, t)
        act.activation(self.junk[:, :], self.x[:, par, :], ACT.Square, accum_out=self.ss[:, par, :]).then_inc(self.s.sq, 1)

    def normalise(self, dve, T):
        t, half, par = T
        dve.wait_ge(self.s.sq, t + 1)
        dve.tensor_scalar(self.ms[:, par, :], self.ss[:, par, :], 1.0 / D_MODEL, EPS, ALU.mult, ALU.add).then_inc(self.s.ms, 1)
        dve.wait_ge(self.s.rstd, t + 1)
        dve.tensor_scalar(self.x[:, par, :], self.x[:, par, :], self.rstd[:, par, :], None, ALU.mult).then_inc(self.s.xn, 1)

    def root(self, pool, T):
        t, half, par = T
        pool.wait_ge(self.s.ms, t + 1)
        pool.tensor_tensor(self.rstd[:, par, :], self.ms[:, par, :], self.g.neg_half[:, 0:1], ALU.pow).then_inc(self.s.rstd, 1)

    def transpose(self, pe, T):
        t, half, par = T
        pe.wait_ge(self.s.xn, t + 1)
        wait(pe, self.s.hT, t)
        for k in range(KC):
            last = pe.transpose(self.p_tr[:, k * P:(k + 1) * P], self.x[:, par, k * P:(k + 1) * P], self.g.ident[:, :])
        last.then_inc(self.s.tr, 1)

    def modulate(self, act, T):
        t, half, par = T
        act.wait_ge(self.s.tr, t + 1)
        wait(act, self.s.split, t)
        c = cond_of(t)
        for k in range(KC):
            last = act.activation(self.hT[:, k, :], self.p_tr[:, k * P:(k + 1) * P], ACT.Identity,
                                  bias=self.g.lnp[:, self.norm, c, 1, k:k + 1], scale=self.g.lnp[:, self.norm, c, 0, k:k + 1])
        last.then_inc(self.s.hT, 1)

    def split(self, dve, T):
        t, half, par = T
        dve.wait_ge(self.s.hT, t + 1)
        wait(dve, self.used, t - 1)
        dve.tensor_copy(self.hi[:, par], self.hT[:, :, :]).then_inc(self.s.hi, 1)
        dve.wait_ge(self.s.hi, t + 1)
        dve.tensor_tensor(self.lo[:, par], self.hT[:, :, :], self.hi[:, par].bitcast(F32), ALU.subtract).then_inc(self.s.split, 1)


def load_split_weights(ph, s, w_dram, n_k, cols, w_hi, w_lo, stage):
    (s.w0, s.w1, s.w_hi, s.w_lo) = ph.semaphores("w0 w1 w_hi w_lo")

    def sp_part(sp):
        for k in range(n_k):
            wait(sp, s.w_lo, k - 1)
            sp.dma_start(stage[:, k % 2, 0:cols], w_dram[k * P:(k + 1) * P, :]).then_inc([s.w0, s.w1][k % 2], 16)

    def act_part(act):
        for k in range(n_k):
            act.wait_ge([s.w0, s.w1][k % 2], 16 * (k // 2 + 1))
            act.activation(w_hi[:, k, :], stage[:, k % 2, 0:cols], ACT.Copy).then_inc(s.w_hi, 1)

    def dve_part(dve):
        for k in range(n_k):
            dve.wait_ge(s.w_hi, k + 1)
            dve.tensor_tensor(w_lo[:, k, :], stage[:, k % 2, 0:cols], w_hi[:, k, :].bitcast(F32), ALU.subtract).then_inc(s.w_lo, 1)

    return sp_part, act_part, dve_part


def split_product(pe, out, parts, first, last):
    (ah, al), (bh, bl) = parts
    pe.matmul(out, ah, bh, start=first, stop=False)
    pe.matmul(out, ah, bl, start=False, stop=False)
    return pe.matmul(out, al, bh, start=False, stop=last)


def constant_parts(dve, parts):
    dve.memset(parts[:, :, 3, 1:HD].bitcast(F32), 0.0)
    dve.memset(parts[:, :, 3, 0:1].bitcast(F32), -1.0)


def attention_projection(nc, g):
    NH = AH + KVH
    with ExitStack() as stack:
        ph = Phase(nc, stack, "qkv")
        s = ph.s
        (s.gain, s.gmul, s.rope0, s.rope1, s.mq, s.mkv, s.eq, s.ekv, s.psq, s.ssh, s.msh, s.rsh, s.cs, s.qn, s.m1, s.m2,
         s.rot, s.hq, s.lo_q, s.hk, s.lo_k, s.vhi, s.vlo, s.ptr, s.eptr, s.eptk, s.qout0, s.qout1, s.cache) = ph.semaphores(
            "gain gmul rope0 rope1 mq mkv eq ekv psq ssh msh rsh cs qn m1 m2 rot hq lo_q hk lo_k vhi vlo ptr eptr eptk qout0 qout1 cache")
        fr = Front(ph, s, g, 0, s.mkv)
        w_hi = ph.sb("w_hi", [P, KC, D_ATT], F32R)
        w_lo = ph.sb("w_lo", [P, KC, D_ATT], F32R)
        stage = ph.sb("stage", [P, 2, D_ATT])
        gsrc = ph.sb("gsrc", [P, 4, HD])
        gain = ph.sb("gain", [P, 2, NH, HD])
        rope = ph.sb("rope", [P, 2, 2, HD])
        qkv = ph.sb("qkv", [P, 2, D_ATT])
        psq = ph.sb("psq", [P, NH * HD])
        ssh = ph.sb("ssh", [P, NH])
        msh = ph.sb("msh", [P, NH])
        rsh = ph.sb("rsh", [P, NH])
        cs = ph.sb("cs", [P, 2, NH, HD])
        qn = ph.sb("qn", [P, NH, HD])
        m1 = ph.sb("m1", [P, NH, HD])
        m2 = ph.sb("m2", [P, NH, HD])
        rot = ph.sb("rot", [P, 2, NH, HD])
        qhl = ph.sb("qhl", [P, AH, 2, HD], F32R)
        khl = ph.sb("khl", [P, KVH, 4, HD], F32R)
        qT = ph.sb("qT", [P, 2, AH, P], F32R)
        p_q = [ph.ps("p_q0"), ph.ps("p_q1")]
        p_kv = ph.ps("p_kv")
        p_t = ph.ps("p_t", 1536)
        w_sp, w_act, w_dve = load_split_weights(ph, s, g.w_in[0, :, D_GLA:D_GLA + D_ATT], KC, D_ATT, w_hi, w_lo, stage)
        NQ = AH * HD

        def key_tile(t):
            return t + 2 if cond_of(t) else t

        with nc.Block() as block:

            @block.sync
            def _(sp):
                q_g, k_g = g.q_norm_g, g.k_norm_g
                half = HD // 4
                with nc.allow_non_contiguous_dma(reason="gains"):
                    for n, gg in enumerate((q_g, k_g)):
                        sp.dma_start(gsrc[:, 2 * n, :], gg.to_broadcast([P, HD])).then_inc(s.gain, 16)
                        for a in range(2):
                            for h in range(2):
                                src = gg[:, (2 * a + 1 - h) * half:(2 * a + 2 - h) * half].to_broadcast([P, half])
                                sp.dma_start(gsrc[:, 2 * n + 1, (2 * a + h) * half:(2 * a + h + 1) * half], src).then_inc(s.gain, 16)
                w_sp(sp)

                def step(U):
                    if T := U.at(5):
                        t, hf, par = T
                        sp.wait_ge(s.eptr, t + 1)
                        sp.dma_start(g.qT_tile(t), qT[:, par].rearrange("p h q -> p (h q)").bitcast(F32)).then_inc([s.qout0, s.qout1][par], 16)
                        if cond_of(t):
                            r = (t - N_LAT) * P
                            sp.dma_start(g.new_k[r:r + P, :], rot[:, par, AH:NH, :].rearrange("p h d -> p (h d)")).then_inc(s.cache, 16)
                            sp.dma_start(g.new_v[r:r + P, :], qkv[:, par, NH * HD:D_ATT]).then_inc(s.cache, 16)
                    if T := U.at(0):
                        fr.load(sp, T)
                    if T := U.at(2):
                        t, hf, par = T
                        wait(sp, s.cs, t - 1)
                        sp.dma_start(rope[:, par].rearrange("p a d -> p (a d)"), g.rope_tile(t)).then_inc([s.rope0, s.rope1][par], 16)

                steps(sp, 5, step)
                sp.wait_ge(s.qout0, 16 * (NT // 2))
                sp.wait_ge(s.qout1, 16 * (NT // 2))
                sp.wait_ge(s.cache, 16 * 2 * N_CTX)

            @block.scalar
            def _(act):
                w_act(act)

                def step(U):
                    if T := U.at(0):
                        fr.squares(act, T)
                    if T := U.at(1):
                        fr.modulate(act, T)
                    if T := U.at(3):
                        t, hf, par = T
                        act.wait_ge(s.mq, t + 1)
                        wait(act, s.vlo, t - 1)
                        act.activation(qkv[:, par, 0:NQ], p_q[par][:, :], ACT.Copy).then_inc(s.eq, 1)
                        act.wait_ge(s.mkv, t + 1)
                        act.activation(qkv[:, par, NQ:D_ATT], p_kv[:, 0:D_ATT - NQ], ACT.Copy).then_inc(s.ekv, 1)
                        act.wait_ge(s.ekv, t + 1)
                        act.wait_ge(s.eq, t + 1)
                        wait(act, s.ssh, t)
                        act.activation(psq[:, :], qkv[:, par, 0:NH * HD], ACT.Square).then_inc(s.psq, 1)
                    if T := U.at(4):
                        t, hf, par = T
                        act.wait_ge(s.ptr, t + 1)
                        if isinstance(t, int) and t < 2:
                            pass
                        else:
                            act.wait_ge([s.qout0, s.qout1][par], hf * 16)
                        act.activation(qT[:, par], p_t[:, 0:AH * P].rearrange("p (h q) -> p h q", h=AH), ACT.Copy).then_inc(s.eptr, 1)
                        kt = key_tile(t)
                        col = kt * P
                        act.activation(g.keysT[:, :, :, bass.ds(col, P)],
                                       p_t[:, AH * P:(AH + 4) * P].rearrange("p (g a q) -> p g a q", g=KVH, a=2), ACT.Copy).then_inc(s.eptk, 1)

                steps(act, 4, step)
                act.wait_ge(s.eptk, NT)

            @block.vector
            def _(dve):
                constant_parts(dve, khl)
                dve.wait_ge(s.gain, 16 * 10)
                for n in range(2):
                    dve.tensor_scalar(gain[:, n, 0:AH, :], bc(gsrc[:, n, :], 1, AH), HD ** -0.5, None, ALU.mult)
                    last = dve.tensor_copy(gain[:, n, AH:NH, :], bc(gsrc[:, 2 + n, :], 1, KVH))
                last.then_inc(s.gmul, 1)
                w_dve(dve)

                def step(U):
                    if T := U.at(0):
                        fr.normalise(dve, T)
                    if T := U.at(1):
                        fr.split(dve, T)
                    if T := U.at(3):
                        t, hf, par = T
                        dve.wait_ge(s.psq, t + 1)
                        dve.tensor_reduce(ssh[:, :], psq[:, :].rearrange("p (h d) -> p h d", d=HD), AX.X, ALU.add).then_inc(s.ssh, 1)
                        dve.wait_ge(s.ssh, t + 1)
                        dve.tensor_scalar(msh[:, :], ssh[:, :], 1.0 / HD, EPS, ALU.mult, ALU.add).then_inc(s.msh, 1)
                        vt = key_tile(t)
                        src = qkv[:, par, NH * HD:D_ATT].rearrange("p (g d) -> p g d", g=KVH)
                        dve.wait_ge(s.ekv, t + 1)
                        v_here = g.vals[:, bass.ds(vt * KVH, KVH), :]
                        dve.tensor_copy(v_here[:, :, 0:HD], src).then_inc(s.vhi, 1)
                        dve.wait_ge(s.rsh, t + 1)
                        dve.tensor_tensor(qn[:, :, :], qkv[:, par, 0:NH * HD].rearrange("p (h d) -> p h d", d=HD),
                                          bc(rsh[:, :], 2, HD), ALU.mult).then_inc(s.qn, 1)
                        dve.wait_ge(s.vhi, t + 1)
                        dve.tensor_tensor(v_here[:, :, HD:2 * HD], src, v_here[:, :, 0:HD].bitcast(F32), ALU.subtract).then_inc(s.vlo, 1)
                        dve.wait_ge(s.qn, t + 1)
                        dve.wait_ge(s.cs, t + 1)
                        dve.tensor_tensor(m1[:, :, :], qn[:, :, :], cs[:, 0], ALU.mult).then_inc(s.m1, 1)
                        dve.wait_ge(s.m1, t + 1)
                        dve.wait_ge(s.m2, t + 1)
                        dve.tensor_tensor(rot[:, par], m1[:, :, :], m2[:, :, :], ALU.add).then_inc(s.rot, 1)
                        dve.wait_ge(s.rot, t + 1)
                        wait(dve, s.ptr, t)
                        dve.tensor_copy(qhl[:, :, 0, :], rot[:, par, 0:AH, :]).then_inc(s.hq, 1)
                        dve.tensor_copy(khl[:, :, 0:2, :], bc(rot[:, par, AH:NH, :], 2, 2)).then_inc(s.hk, 1)
                        dve.wait_ge(s.hq, t + 1)
                        dve.tensor_tensor(qhl[:, :, 1, :], rot[:, par, 0:AH, :], qhl[:, :, 0, :].bitcast(F32), ALU.subtract).then_inc(s.lo_q, 1)
                        dve.wait_ge(s.hk, t + 1)
                        dve.tensor_tensor(khl[:, :, 2, :], rot[:, par, AH:NH, :], khl[:, :, 0, :].bitcast(F32), ALU.subtract).then_inc(s.lo_k, 1)

                steps(dve, 4, step)

            @block.gpsimd
            def _(pool):
                pool.wait_ge(s.gmul, 1)

                def step(U):
                    if T := U.at(0):
                        fr.root(pool, T)
                    if T := U.at(3):
                        t, hf, par = T
                        pool.wait_ge([s.rope0, s.rope1][par], (hf + 1) * 16)
                        wait(pool, s.m1, t)
                        wait(pool, s.m2, t)
                        pool.tensor_tensor(cs[:, 0], gain[:, 0], bc(rope[:, par, 0, :], 1, NH), ALU.mult)
                        pool.tensor_tensor(cs[:, 1], gain[:, 1], bc(rope[:, par, 1, :], 1, NH), ALU.mult).then_inc(s.cs, 1)
                        pool.wait_ge(s.msh, t + 1)
                        pool.tensor_tensor(rsh[:, :], msh[:, :], g.neg_half[:, 0:NH], ALU.pow).then_inc(s.rsh, 1)
                        pool.wait_ge(s.cs, t + 1)
                        pool.wait_ge(s.qn, t + 1)
                        wait(pool, s.rot, t)
                        v5 = [x.rearrange("p h (a e d) -> p (h a) e d", a=2, e=2) for x in (m2[:, :, :], qn[:, :, :], cs[:, 1])]
                        for e in range(2):
                            last = pool.tensor_tensor(v5[0][:, :, e, :], v5[1][:, :, 1 - e, :], v5[2][:, :, e, :], ALU.mult)
                        last.then_inc(s.m2, 1)

                steps(pool, 4, step)

            @block.tensor
            def _(pe):
                pe.wait_ge(s.w_lo, KC)

                def step(U):
                    if T := U.at(1):
                        fr.transpose(pe, T)
                    if T := U.at(2):
                        t, hf, par = T
                        pe.wait_ge(s.split, t + 1)
                        wait(pe, s.eq, t - 1)
                        for k in range(KC):
                            last = split_product(pe, p_q[par][:, :], ((fr.hi[:, par, k], fr.lo[:, par, k]),
                                                 (w_hi[:, k, 0:NQ], w_lo[:, k, 0:NQ])), k == 0, k == KC - 1)
                        last.then_inc(s.mq, 1)
                        wait(pe, s.ekv, t)
                        for k in range(KC):
                            last = split_product(pe, p_kv[:, 0:D_ATT - NQ], ((fr.hi[:, par, k], fr.lo[:, par, k]),
                                                 (w_hi[:, k, NQ:D_ATT], w_lo[:, k, NQ:D_ATT])), k == 0, k == KC - 1)
                        last.then_inc(s.mkv, 1)
                    if T := U.at(3):
                        t, hf, par = T
                        pe.wait_ge(s.lo_q, t + 1)
                        pe.wait_ge(s.lo_k, t + 1)
                        wait(pe, s.eptr, t)
                        wait(pe, s.eptk, t)
                        for h in range(AH):
                            pe.transpose(p_t[:, h * P:(h + 1) * P], qhl[:, h].rearrange("p a d -> p (a d)").bitcast(F32), g.ident[:, :])
                        for n in range(4):
                            last = pe.transpose(p_t[:, (AH + n) * P:(AH + n + 1) * P],
                                                khl[:, n // 2, 2 * (n % 2):2 * (n % 2) + 2, :].rearrange("p a d -> p (a d)").bitcast(F32),
                                                g.ident[:, :])
                        last.then_inc(s.ptr, 1)

                steps(pe, 4, step)


def attention(nc, g):
    G4 = AH // KVH
    NKT = (T_LAT + PAST) // P
    NKC = T_CTX // P
    NS = NKT // 2
    ROW = 4 * P
    SLOTS_P = 6
    Q_SLOTS = 4
    FULL = T_LAT // ROW
    N_PIECES = G4 * FULL + G4 // 2
    PLAN = [2, 2, 2, 3, 2, 3, 2, 2, 0]
    L_UNITS = 2 * N_LAT
    U_UNITS = 2 * NT
    with ExitStack() as stack:
        ph = Phase(nc, stack, "att")
        s = ph.s
        (s.zero, s.ck, s.cv, s.ckh, s.ckl, s.ctr, s.cte, s.q0, s.q1, s.q2, s.q3, s.piece, s.mx, s.nm, s.turn, s.aux, s.st, s.ex, s.hi, s.lo,
         s.pv, s.acc, s.ls, s.rec, s.lb, s.tsums, s.osb, s.osum, s.oo, s.out0, s.out1) = ph.semaphores(
            "zero ck cv ckh ckl ctr cte q0 q1 q2 q3 piece mx nm turn aux st ex hi lo pv acc ls rec lb tsums osb osum oo out0 out1")
        s.q, s.out = [s.q0, s.q1, s.q2, s.q3], [s.out0, s.out1]
        ckr = ph.sb("ckr", [P, 2, KVH, HD])
        cvr = ph.sb("cvr", [P, 2, KVH, HD])
        ckp = ph.sb("ckp", [P, 2, KVH, 4, HD], F32R)
        qa = ph.sb("qa", [P, Q_SLOTS, ROW], F32R)
        qb = ph.sb("qb", [P, Q_SLOTS, ROW], F32R)
        mx = ph.sb("mx", [P, 2, G4, FULL + 1])
        wm = ph.sb("wm", [P, 2, G4, P], F32R)
        prob = ph.sb("prob", [P, SLOTS_P, 2 * ROW])
        thi = ph.sb("thi", [P, SLOTS_P, 2 * ROW], F32R)
        tlo = ph.sb("tlo", [P, SLOTS_P, 2 * ROW], F32R)
        acc = ph.sb("acc", [P, 2 + KVH * N_CTX, ROW])
        ones = ph.sb("ones", [P, G4])
        osb = ph.sb("osb", [HD, ROW])
        rec = ph.sb("rec", [P, G4])
        lb = ph.sb("lb", [P, G4, HD])
        osum = ph.sb("osum", [P, 2, P])
        oo = ph.sb("oo", [P, 2, 2 * P])
        p_s = [ph.ps("p_s0", 2 * ROW), ph.ps("p_s1", 2 * ROW)]
        p_r = [ph.ps("p_r0"), ph.ps("p_r1")]
        p_o = [ph.ps("p_o0"), ph.ps("p_o1")]

        def unit(n, qt, kv, q, q_round):
            u = Names()
            u.n, u.qt, u.kv, u.q, u.q_round = n, qt, kv, q, q_round
            if isinstance(n, int) and n >= L_UNITS:
                m = n - L_UNITS
                u.nds, u.kt0, u.pieces = NKC // 2, NKT, G4 // 2
                u.g0, u.p0, u.a0 = L_UNITS * NS + m, L_UNITS * N_PIECES + m * u.pieces, L_UNITS * (2 * NS - 1) + m
                u.step_no, u.sums = [L_UNITS * NS + m], 2 + m
            else:
                u.nds, u.kt0, u.pieces = NS, 0, N_PIECES
                u.g0, u.p0, u.a0 = n * NS, n * N_PIECES, n * (2 * NS - 1)
                u.sums = kv
                u.step_no = [kv * NS + j for j in range(NS)]
            return u

        def of(n):
            return unit(n, n // 2, n % 2, n % Q_SLOTS, n // Q_SLOTS)

        def turn_unit(i, m):
            return unit(i * 4 + (2 + m), i * 2 + (1 + m // 2), m % 2, (2 + m) % Q_SLOTS, i + (2 + m) // Q_SLOTS)

        class Walk:

            def __init__(self, e=None, b=None):
                self.index, self.fin, self.out, self.store, self.done, self.ring = 1, None, None, None, [None, None, None], [None, None]
                if e is not None:
                    self.index, self.done = 0, [(b, NS - 3), (b, NS - 2), (b, NS - 1)]
                    self.ring = [(s.mx, e.p0 + N_PIECES), (s.aux, e.n + 1)]

            def item(self, sem, count):
                bank, before = self.index % 2, self.ring[0]
                self.index += 1
                self.ring = [self.ring[1], (sem, count)]
                return p_r[bank], before

            def pieces(self, v, i0, n):
                return [(v, i, self.item(s.mx, v.p0 + (i + 1))) for i in range(i0, i0 + n)]

            def step(self, e, j, v, i0, n, turn, load=None):
                S = Names()
                S.now = (e, j) if e is not None else None
                S.load = load
                S.low, S.val, S.fin = self.done[1], self.done[0], None
                S.early = self.pieces(v, i0, n) if n and (e is None or e.nds == 1) else []
                S.turn = (v, self.item(s.aux, v.n + 1)) if turn else None
                S.turn_sums = (self.out, self.item(s.oo, self.out.n + 1)) if self.out is not None else None
                if self.fin is not None:
                    S.fin = (self.fin, self.item(s.rec, self.fin.n + 1))
                S.max = self.pieces(v, i0, n) if n and not S.early else []
                S.store = self.store
                self.store, self.out = self.out, self.fin
                self.fin = S.val[0] if S.val is not None and S.val[1] == S.val[0].nds - 1 else None
                self.done = [self.done[1], self.done[2], S.now]
                return S

            def unit_steps(self, e, v, w=None):
                i0 = 0
                for j in range(e.nds):
                    n = 0
                    if v is not None:
                        n = min(PLAN[j], v.pieces - i0) if e.nds > 1 else v.pieces
                    yield self.step(e, j, v, i0, n, v is not None and j == e.nds - 1, w if j == 0 else None)
                    i0 += n

        def schedule(eng, step):
            w = Walk()
            step(w.step(None, 0, of(0), 0, N_PIECES, True, of(0)))
            step(w.step(None, 0, None, 0, 0, False, of(1)))
            for n in range(2):
                for S in w.unit_steps(of(n), of(n + 1), of(n + 2)):
                    step(S)
            with eng.Fori(0, (N_LAT - 2) // 2) as i:
                w = Walk(turn_unit(i, 0), turn_unit(i, -1))
                for m in range(4):
                    for S in w.unit_steps(turn_unit(i, m), turn_unit(i, m + 1), turn_unit(i, m + 2)):
                        step(S)
            w = Walk(of(L_UNITS - 2), of(L_UNITS - 3))
            for n in range(L_UNITS - 2, U_UNITS):
                for S in w.unit_steps(of(n), *(of(m) if m < U_UNITS else None for m in (n + 1, n + 2))):
                    step(S)
            for _ in range(6):
                step(w.step(None, 0, None, 0, 0, False))

        with nc.Block() as block:

            @block.sync
            def _(sp):
                for t in range(2):
                    sp.dma_start(ckr[:, t].rearrange("p g d -> p (g d)"), g.cache_k[t * P:(t + 1) * P, :]).then_inc(s.ck, 16)
                    sp.dma_start(cvr[:, t].rearrange("p g d -> p (g d)"), g.cache_v[t * P:(t + 1) * P, :]).then_inc(s.cv, 16)

                def load(v):
                    src = g.qT_tile(v.qt)[:, v.kv * ROW:(v.kv + 1) * ROW]
                    sp.dma_start(qa[:, v.q, :].bitcast(F32), src).then_inc(s.q[v.q], 16)
                    sp.dma_start(qb[0:HD, v.q, :].bitcast(F32), src[0:HD, :]).then_inc(s.q[v.q], 16)

                def step(S):
                    if S.load is not None:
                        n = S.load.n
                        wait(sp, s.st, of(n - Q_SLOTS + 1).g0 if isinstance(n, int) and n >= Q_SLOTS else (n - Q_SLOTS + 1) * NS)
                        load(S.load)

                schedule(sp, step)

            @block.gpsimd
            def _(pool):
                def step(S):
                    if S.fin:
                        b = S.fin[0]
                        pool.wait_ge(s.rec, b.n + 1)
                        wait(pool, s.tsums, b.n)
                        pool.tensor_tensor(lb[:, :, :], bc(rec[:, :], 2, HD), bc(ones[:, :], 2, HD), ALU.mult).then_inc(s.lb, 1)
                    if S.now:
                        e, j = S.now
                        sl = e.step_no[j] % SLOTS_P
                        before = e.a0 + 2 * j - 1
                        pool.wait_ge(s.ex, e.g0 + (j + 1))
                        a, b = prob[:, sl, 0:ROW], prob[:, sl, ROW:2 * ROW]
                        if j == 0:
                            if e.nds > 1:
                                wait(pool, s.ls, e.n - 1)
                            pool.tensor_tensor(acc[:, e.sums, :], a, b, ALU.add).then_inc(s.acc, 1)
                        else:
                            pool.wait_ge(s.acc, before)
                            pool.tensor_tensor(acc[:, e.sums, :], acc[:, e.sums, :], a, ALU.add).then_inc(s.acc, 1)
                            pool.wait_ge(s.acc, before + 1)
                            pool.tensor_tensor(acc[:, e.sums, :], acc[:, e.sums, :], b, ALU.add).then_inc(s.acc, 1)
                    if S.store:
                        b = S.store
                        pool.wait_ge(s.oo, b.n + 1)
                        pool.dma_start(g.mix_tile(b.qt)[:, (4 + 2 * b.kv) * P:(6 + 2 * b.kv) * P], oo[:, b.kv, :]).then_inc(s.out[b.kv], 16)

                schedule(pool, step)
                for kv in range(KVH):
                    pool.wait_ge(s.out[kv], 16 * NT)

            @block.tensor
            def _(pe):
                pe.wait_ge(s.ckl, 1)
                for t in range(2):
                    for n in range(4):
                        last = pe.transpose(p_s[0][:, (t * 4 + n) * P:(t * 4 + n + 1) * P],
                                            ckp[:, t, n // 2, 2 * (n % 2):2 * (n % 2) + 2, :].rearrange("p a d -> p (a d)").bitcast(F32),
                                            g.ident[:, :])
                last.then_inc(s.ctr, 1)
                pe.wait_ge(s.cte, 2)

                def piece(v, i, item):
                    bank, before = item
                    if i == 0:
                        pe.wait_ge(s.q[v.q], v.q_round * 32 + 32)
                    if before:
                        pe.wait_ge(*before)
                    if v.nds > 1 and i < G4 * FULL:
                        h, c = i // FULL, i % FULL
                        pe.matmul(bank[:, :], qa[:, v.q, h * P:(h + 1) * P], g.keysT[:, v.kv, 0, c * ROW:(c + 1) * ROW],
                                  start=True, stop=True).then_inc(s.piece, 1)
                    else:
                        h0 = 2 * (i - G4 * FULL if v.nds > 1 else i)
                        k0 = (v.kt0 + 2 * (v.nds - 1)) * P
                        for n in range(2):
                            last = pe.matmul(bank[:, n * 2 * P:(n + 1) * 2 * P], qa[:, v.q, (h0 + n) * P:(h0 + n + 1) * P],
                                             g.keysT[:, v.kv, 0, k0:k0 + 2 * P], start=True, stop=True)
                        last.then_inc(s.piece, 1)

                def step(S):
                    for v, i, item in S.early:
                        piece(v, i, item)
                    if S.turn:
                        v, (bank, before) = S.turn
                        pe.wait_ge(s.nm, v.n + 1)
                        pe.wait_ge(*before)
                        for h in range(G4):
                            last = pe.transpose(bank[:, h * P:(h + 1) * P], wm[:, v.kv, h, :].bitcast(F32), g.ident[:, :])
                        last.then_inc(s.turn, 1)
                    if S.now:
                        e, j = S.now
                        if j == 0:
                            pe.wait_ge(s.aux, e.n + 1)
                            pe.wait_ge(s.q[e.q], e.q_round * 32 + 32)
                        wait(pe, s.ex, e.g0 + (j - 1))
                        bank = p_s[e.step_no[j] % 2]
                        for i in range(2):
                            kt = slice((e.kt0 + 2 * j + i) * P, (e.kt0 + 2 * j + i + 1) * P)
                            pe.matmul(bank[:, i * ROW:(i + 1) * ROW], g.keysT[:, e.kv, 0, kt], qa[:, e.q, :], start=True, stop=False)
                            last = pe.matmul(bank[:, i * ROW:(i + 1) * ROW], g.keysT[:, e.kv, 1, kt], qb[:, e.q, :], start=False, stop=True)
                        last.then_inc(s.st, 1)
                    if S.turn_sums:
                        b, (bank, before) = S.turn_sums
                        pe.wait_ge(s.lb, b.n + 1)
                        pe.wait_ge(*before)
                        for n in range(2):
                            last = pe.transpose(bank[:, n * P:(n + 1) * P], lb[:, 2 * n:2 * n + 2, :].rearrange("p h d -> p (h d)"), g.ident[:, :])
                        last.then_inc(s.tsums, 1)
                    if S.fin:
                        b, (bank, before) = S.fin
                        pe.wait_ge(s.acc, b.a0 + (2 * b.nds - 1))
                        pe.wait_ge(*before)
                        for h in range(G4):
                            last = pe.matmul(bank[:, h:h + 1], acc[:, b.sums, h * P:(h + 1) * P], ones[:, 0:1], start=True, stop=True)
                        last.then_inc(s.ls, 1)
                    pieces = list(S.max)
                    if S.val:
                        b, j = S.val
                        pe.wait_ge(s.lo, b.g0 + (j + 1))
                        if j == 0:
                            wait(pe, s.osum, b.n - 1)
                        sl = b.step_no[j] % SLOTS_P
                        for i in range(2):
                            v = g.vals[:, (b.kt0 + 2 * j + i) * KVH + b.kv, :]
                            cols = slice(i * ROW, (i + 1) * ROW)
                            pe.matmul(p_o[b.kv][:, :], v, thi[:, sl, cols], start=j == 0 and i == 0, stop=False)
                            last = pe.matmul(p_o[b.kv][:, :], v, tlo[:, sl, cols], start=False, stop=j == b.nds - 1 and i == 1)
                            if i == 1:
                                last.then_inc(s.pv, 1)
                            if pieces:
                                piece(*pieces.pop(0))
                    for p in pieces:
                        piece(*p)

                schedule(pe, step)

            @block.scalar
            def _(act):
                act.wait_ge(s.ctr, 1)
                for t in range(2):
                    act.activation(g.keysT[:, :, :, (N_LAT + t) * P:(N_LAT + t + 1) * P],
                                   p_s[0][:, t * 512:(t + 1) * 512].rearrange("p (g a q) -> p g a q", g=KVH, a=2), ACT.Copy).then_inc(s.cte, 1)

                def step(S):
                    if S.turn:
                        v, (bank, _) = S.turn
                        act.wait_ge(s.turn, v.n + 1)
                        wait(act, s.st, v.g0 - (NS if v.nds > 1 else 1))
                        act.activation(qb[HD:P, v.q, :], bank[HD:P, :], ACT.Copy).then_inc(s.aux, 1)
                    if S.fin:
                        b = S.fin[0]
                        act.wait_ge(s.pv, b.g0 + b.nds)
                        wait(act, s.osum, b.n)
                        act.activation(osb[:, :], p_o[b.kv][HD:P, :], ACT.Copy).then_inc(s.osb, 1)
                    if S.now:
                        e, j = S.now
                        sl = e.step_no[j] % SLOTS_P
                        act.wait_ge(s.st, e.g0 + (j + 1))
                        wait(act, s.lo, e.g0 + (j - SLOTS_P + 1))
                        if j >= SLOTS_P:
                            act.wait_ge(s.acc, e.a0 + (2 * (j - SLOTS_P) + 1))
                        elif e.nds > 1:
                            wait(act, s.acc, e.a0 + 2 * (j - SLOTS_P + 1))
                        else:
                            act.wait_ge(s.acc, e.a0)
                        act.activation(prob[:, sl, :], p_s[e.step_no[j] % 2][:, :], ACT.Exp).then_inc(s.ex, 1)
                        act.wait_ge(s.ex, e.g0 + (j + 1))
                        wait(act, s.pv, e.g0 + (j - SLOTS_P + 1))
                        act.activation(thi[:, sl, :], prob[:, sl, :], ACT.Copy).then_inc(s.hi, 1)

                schedule(act, step)

            @block.vector
            def _(dve):
                dve.memset(ones[:, :], 1.0)
                dve.memset(wm[:, :, :, :].bitcast(F32), 0.0).then_inc(s.zero, 1)
                for t in range(2):
                    constant_parts(dve, ckp[:, t])
                dve.wait_ge(s.cv, 32)
                for t in range(2):
                    v_here = g.vals[:, (N_LAT + t) * KVH:(N_LAT + t + 1) * KVH, :]
                    dve.tensor_copy(v_here[:, :, 0:HD], cvr[:, t]).then_inc(s.ckh, 1)
                dve.wait_ge(s.ck, 32)
                for t in range(2):
                    dve.tensor_copy(ckp[:, t, :, 0:2, :], bc(ckr[:, t], 2, 2)).then_inc(s.ckh, 1)
                dve.wait_ge(s.ckh, 4)
                for t in range(2):
                    v_here = g.vals[:, (N_LAT + t) * KVH:(N_LAT + t + 1) * KVH, :]
                    dve.tensor_tensor(v_here[:, :, HD:2 * HD], cvr[:, t], v_here[:, :, 0:HD].bitcast(F32), ALU.subtract)
                    last = dve.tensor_tensor(ckp[:, t, :, 2, :], ckr[:, t], ckp[:, t, :, 0, :].bitcast(F32), ALU.subtract)
                last.then_inc(s.ckl, 1)
                dve.wait_ge(s.zero, 1)

                def piece(v, i, item):
                    bank = item[0]
                    if i == 0:
                        wait(dve, s.nm, v.n - 1)
                    dve.wait_ge(s.piece, v.p0 + (i + 1))
                    if v.nds > 1 and i < G4 * FULL:
                        h, c = i // FULL, i % FULL
                        dve.tensor_reduce(mx[:, v.kv, h, c:c + 1], bank[:, :], AX.X, ALU.max).then_inc(s.mx, 1)
                    else:
                        h0 = 2 * (i - G4 * FULL if v.nds > 1 else i)
                        dve.tensor_reduce(mx[:, v.kv, h0:h0 + 2, FULL], bank[:, :].rearrange("p (h k) -> p h k", h=2), AX.X, ALU.max).then_inc(s.mx, 1)
                    if i == v.pieces - 1:
                        dve.wait_ge(s.mx, v.p0 + v.pieces)
                        wait(dve, s.turn, v.n - 1)
                        parts = mx[:, v.kv, :, :] if v.nds > 1 else mx[:, v.kv, :, FULL:FULL + 1]
                        dve.tensor_reduce(wm[:, v.kv, :, HD], parts, AX.X, ALU.max).then_inc(s.nm, 1)

                def step(S):
                    for p in S.early:
                        piece(*p)
                    if S.low:
                        b, j = S.low
                        sl = b.step_no[j] % SLOTS_P
                        dve.wait_ge(s.hi, b.g0 + (j + 1))
                        dve.tensor_tensor(tlo[:, sl, :], prob[:, sl, :], thi[:, sl, :].bitcast(F32), ALU.subtract).then_inc(s.lo, 1)
                    if S.turn_sums:
                        b, (bank, _) = S.turn_sums
                        dve.wait_ge(s.osum, b.n + 1)
                        dve.wait_ge(s.tsums, b.n + 1)
                        if not (isinstance(b.qt, int) and b.qt == 0):
                            dve.wait_ge(s.out[b.kv], b.qt * 16)
                        dve.tensor_tensor(oo[:, b.kv, :], osum[:, :, :].rearrange("p n q -> p (n q)"), bank[:, 0:2 * P], ALU.mult).then_inc(s.oo, 1)
                    if S.fin:
                        b, (bank, _) = S.fin
                        dve.wait_ge(s.osb, b.n + 1)
                        wait(dve, s.oo, b.n)
                        ov = p_o[b.kv][0:HD, :].rearrange("p (n e q) -> p n e q", e=2, q=P)
                        sv = osb[:, :].rearrange("p (n e q) -> p n e q", e=2, q=P)
                        for e in range(2):
                            last = dve.tensor_tensor(osum[e * HD:(e + 1) * HD, :, :], ov[:, :, e, :], sv[:, :, e, :], ALU.add)
                        last.then_inc(s.osum, 1)
                        dve.wait_ge(s.ls, b.n + 1)
                        wait(dve, s.lb, b.n)
                        dve.reciprocal(rec[:, :], bank[:, 0:G4]).then_inc(s.rec, 1)
                    for p in S.max:
                        piece(*p)

                schedule(dve, step)


def gla_projection(nc, g):
    NB = 4
    BW = D_GLA // NB
    with ExitStack() as stack:
        ph = Phase(nc, stack, "gp")
        s = ph.s
        (s.b0, s.b1, s.b2, s.b3, s.e0, s.e1, s.e2, s.e3, s.o0, s.o1) = ph.semaphores(
            "b0 b1 b2 b3 e0 e1 e2 e3 o0 o1")
        b, e, o = [s.b0, s.b1, s.b2, s.b3], [s.e0, s.e1, s.e2, s.e3], [s.o0, s.o1]
        fr = Front(ph, s, g, 0, b[NB - 1])
        w_hi = ph.sb("w_hi", [P, KC, D_GLA], F32R)
        w_lo = ph.sb("w_lo", [P, KC, D_GLA], F32R)
        stage = ph.sb("stage", [P, 2, D_GLA])
        out = ph.sb("out", [P, 2, D_GLA])
        p_b = [ph.ps(f"p_b{j}") for j in range(NB)]
        w_sp, w_act, w_dve = load_split_weights(ph, s, g.w_in[0, :, 0:D_GLA], KC, D_GLA, w_hi, w_lo, stage)

        def evacuate(eng, copy, T, banks):
            t, hf, par = T
            for j in banks:
                eng.wait_ge(b[j], t + 1)
                if not (isinstance(t, int) and t < 2):
                    eng.wait_ge(o[par], hf * 16)
                copy(out[:, par, j * BW:(j + 1) * BW], p_b[j][:, 0:BW]).then_inc(e[j], 1)

        with nc.Block() as block:

            @block.sync
            def _(sp):
                w_sp(sp)

                def step(U):
                    if T := U.at(3):
                        t, hf, par = T
                        for j in range(NB):
                            sp.wait_ge(e[j], t + 1)
                        sp.dma_start(g.proj_tile(t), out[:, par, :]).then_inc(o[par], 16)
                    if T := U.at(0):
                        fr.load(sp, T)

                steps(sp, 3, step)
                for par in range(2):
                    sp.wait_ge(o[par], 16 * (NT // 2))

            @block.scalar
            def _(act):
                w_act(act)

                def step(U):
                    if T := U.at(0):
                        fr.squares(act, T)
                    if T := U.at(1):
                        fr.modulate(act, T)
                    if T := U.at(2):
                        evacuate(act, lambda a, c: act.activation(a, c, ACT.Copy), T, (0, 2))

                steps(act, 3, step)

            @block.vector
            def _(dve):
                w_dve(dve)

                def step(U):
                    if T := U.at(0):
                        fr.normalise(dve, T)
                    if T := U.at(1):
                        fr.split(dve, T)
                    if T := U.at(2):
                        evacuate(dve, dve.tensor_copy, T, (1, 3))

                steps(dve, 3, step)

            @block.gpsimd
            def _(pool):
                def step(U):
                    if T := U.at(0):
                        fr.root(pool, T)

                steps(pool, 3, step)

            @block.tensor
            def _(pe):
                pe.wait_ge(s.w_lo, KC)

                def step(U):
                    if T := U.at(1):
                        fr.transpose(pe, T)
                    if T := U.at(2):
                        t, hf, par = T
                        pe.wait_ge(s.split, t + 1)
                        for j in range(NB):
                            wait(pe, e[j], t)
                            for k in range(KC):
                                last = split_product(pe, p_b[j][:, 0:BW], ((fr.hi[:, par, k], fr.lo[:, par, k]),
                                                     (w_hi[:, k, j * BW:(j + 1) * BW], w_lo[:, k, j * BW:(j + 1) * BW])),
                                                     k == 0, k == KC - 1)
                            last.then_inc(b[j], 1)

                steps(pe, 3, step)


def slot_of(chunk, ctx):
    return LAT_SLOTS + 1 + chunk if ctx else chunk + 1


def gla_states(nc, g):
    NG = 2 * GH * DK
    with ExitStack() as stack:
        ph = Phase(nc, stack, "gs")
        s = ph.s
        (s.const, s.wgz, s.in0, s.in1, s.v0, s.v1, s.lrp, s.lrT, s.gk, s.ab, s.ex1, s.ln, s.mn, s.gate, s.cum, s.dec,
         s.e1, s.e2, s.e3, s.edec, s.qs, s.qt, s.kt, s.ke, s.tq, s.tk, s.u, s.etq, s.etk, s.scan, s.ub, s.out0, s.out1,
         s.init, s.z, s.back, s.fin) = ph.semaphores(
            "const wgz in0 in1 v0 v1 lrp lrT gk ab ex1 ln mn gate cum dec e1 e2 e3 edec qs qt kt ke tq tk u etq etk scan ub out0 out1 init z back fin")
        s.inp, s.vin, s.out = [s.in0, s.in1], [s.v0, s.v1], [s.out0, s.out1]
        tri = ph.sb("tri", [P, 4, P])
        ind = ph.sb("ind", [P, 2])
        wg = ph.sb("wg", [2 * LR + 1, GH, 2, DK])
        lrT = ph.sb("lrT", [2 * LR + 1, P])
        qk = ph.sb("qk", [P, 2, 2 * GH * DK])
        lr = ph.sb("lr", [P, 2, 2 * LR])
        vin = ph.sb("vin", [P, 2, GH * DV])
        ab = ph.sb("ab", [P, NG])
        mn = ph.sb("mn", [P, NG])
        gate = ph.sb("gate", [P, 2, GH, 2, DK])
        e1 = ph.sb("e1", [P, GH, 2, DK])
        e2 = ph.sb("e2", [P, GH, 2, DK])
        e3 = ph.sb("e3", [P, GH, 2, DK])
        qs = ph.sb("qs", [P, GH, DK])
        qt = ph.sb("qt", [P, GH, 2, DK])
        kt = ph.sb("kt", [P, GH, 2, DK])
        ke = ph.sb("ke", [P, GH, 2, DK])
        qkT = ph.sb("qkT", [P, 2, GH, 2, P])
        p_a = ph.ps("p_a")
        p_g = ph.ps("p_g")
        p_inc = ph.ps("p_inc")
        p_exc = ph.ps("p_exc")
        p_q = ph.ps("p_q")
        p_k = ph.ps("p_k")
        p_u = [ph.ps("p_u0"), ph.ps("p_u1")]
        V0 = 2 * GH * DK
        LR0 = D_GLA - 2 * LR

        with nc.Block() as block:

            @block.sync
            def _(sp):
                sp.dma_start(tri[:, :, :], g.d_tri).then_inc(s.const, 16)
                sp.dma_start(ind[:, :], g.d_ind).then_inc(s.const, 16)
                sp.wait_ge(s.wgz, 1)
                for r in range(2):
                    sp.dma_start(wg[r * LR:(r + 1) * LR, :, r, :], g.w_gk2[0, r].rearrange("l (h d) -> l h d", h=GH)).then_inc(s.const, 16)
                    sp.dma_start(wg[2 * LR:2 * LR + 1, :, r, :], g.b_gk2[:, r, :].rearrange("l (h d) -> l h d", h=GH)).then_inc(s.const, 16)
                sp.wait_ge(s.z, 1)
                sp.dma_start(g.states[0:DK, slot_of(0, False)], g.state_f.rearrange("h k v -> k h v")).then_inc(s.init, 16)
                sp.dma_start(g.states[DK:P, slot_of(T_LAT // CH - 1, False)], g.state_b.rearrange("h k v -> k h v")).then_inc(s.init, 16)

                def step(U):
                    if T := U.at(4):
                        t, hf, par = T
                        sp.wait_ge(s.etq, t + 1)
                        sp.wait_ge(s.etk, t + 1)
                        sp.dma_start(g.qkT_tile(t), qkT[:, par].rearrange("p h a q -> p (h a q)")).then_inc(s.out[par], 16)
                    if T := U.at(0):
                        t, hf, par = T
                        wait(sp, s.kt, t - 1)
                        wait(sp, s.ke, t - 1)
                        sp.dma_start(qk[:, par, :], g.proj_tile(t)[:, 0:V0]).then_inc(s.inp[par], 16)
                        sp.dma_start(lr[:, par, :], g.proj_tile(t)[:, LR0:D_GLA]).then_inc(s.inp[par], 16)
                    if T := U.at(2):
                        t, hf, par = T
                        wait(sp, s.u, t - 1)
                        sp.dma_start(vin[:, par, :], g.proj_tile(t)[:, V0:V0 + GH * DV]).then_inc(s.vin[par], 16)

                steps(sp, 4, step)
                sp.wait_ge(s.out0, 16 * (NT // 2))
                sp.wait_ge(s.out1, 16 * (NT // 2))
                sp.wait_ge(s.back, 1)
                for n, (out, idx) in enumerate(((g.new_f, slot_of(T_CTX // CH, True)), (g.new_b, slot_of(-1, True)))):
                    sp.dma_start(out.rearrange("h k v -> k h v"), g.states[n * DK:(n + 1) * DK, idx]).then_inc(s.fin, 16)
                sp.wait_ge(s.fin, 32)

            @block.gpsimd
            def _(pool):
                pool.memset(wg[:, :, :, :], 0.0).then_inc(s.wgz, 1)

                def step(U):
                    if T := U.at(2):
                        t, hf, par = T
                        pool.wait_ge(s.e3, t + 1)
                        wait(pool, s.u, t)
                        pool.tensor_tensor(ke[:, :, :, :], bc(qk[:, par, GH * DK:V0].rearrange("p (h d) -> p h d", h=GH), 2, 2),
                                           e3[:, :, :, :], ALU.mult).then_inc(s.ke, 1)

                steps(pool, 4, step)

            @block.tensor
            def _(pe):
                pe.wait_ge(s.const, 16 * 6)

                def step(U):
                    if T := U.at(1):
                        t, hf, par = T
                        pe.wait_ge(s.inp[par], (hf + 1) * 32)
                        wait(pe, s.edec, t - 1)
                        wait(pe, s.lrT, t)
                        pe.transpose(p_a[0:2 * LR, 0:P], lr[:, par, :], g.ident[:, :]).then_inc(s.lrp, 1)
                        pe.wait_ge(s.lrT, t + 1)
                        wait(pe, s.mn, t)
                        pe.matmul(p_g[:, :], lrT[:, :], wg[:, :, :, :].rearrange("l h r d -> l (h r d)"), start=True, stop=True).then_inc(s.gk, 1)
                    if T := U.at(2):
                        t, hf, par = T
                        pe.wait_ge(s.gate, t + 1)
                        wait(pe, s.e3, t)
                        for r in range(2):
                            pe.matmul(p_inc[:, :].rearrange("p (h r d) -> p h r d", h=GH, r=2)[:, :, r, :], tri[:, r, :], gate[:, par, :, r, :],
                                      start=r == 0, stop=True, skip_group_check=True)
                        for r in range(2):
                            last = pe.matmul(p_exc[:, :].rearrange("p (h r d) -> p h r d", h=GH, r=2)[:, :, r, :], tri[:, 2 + r, :],
                                             gate[:, par, :, r, :], start=r == 0, stop=True, skip_group_check=True)
                        last.then_inc(s.cum, 1)
                        wait(pe, s.edec, t)
                        for h in range(GH):
                            last = pe.matmul(p_a[:, 256 + 2 * h:258 + 2 * h], gate[:, par, h].rearrange("p r d -> p (r d)"), ind[:, :], start=True, stop=True)
                        last.then_inc(s.dec, 1)
                    if T := U.at(3):
                        t, hf, par = T
                        pe.wait_ge(s.qt, t + 1)
                        wait(pe, s.etq, t)
                        for h in range(GH):
                            last = pe.transpose(p_q[:, h * P:(h + 1) * P], qt[:, h].rearrange("p r d -> p (r d)"), g.ident[:, :])
                        last.then_inc(s.tq, 1)
                        pe.wait_ge(s.kt, t + 1)
                        wait(pe, s.etk, t)
                        for h in range(GH):
                            last = pe.transpose(p_k[:, h * P:(h + 1) * P], kt[:, h].rearrange("p r d -> p (r d)"), g.ident[:, :])
                        last.then_inc(s.tk, 1)
                        pe.wait_ge(s.ke, t + 1)
                        pe.wait_ge(s.vin[par], (hf + 1) * 16)
                        wait(pe, s.ub, t)
                        wait(pe, s.scan, 2 * GH * t)
                        for c in range(2):
                            rows = slice(c * CH, (c + 1) * CH)
                            for h in range(GH):
                                last = pe.matmul(p_u[c][:, h * DV:(h + 1) * DV], ke[rows, h].rearrange("p r d -> p (r d)"),
                                                 vin[rows, par, h * DV:(h + 1) * DV], start=True, stop=True)
                        last.then_inc(s.u, 1)

                steps(pe, 4, step)

            @block.scalar
            def _(act):
                def step(U):
                    if T := U.at(1):
                        t, hf, par = T
                        act.wait_ge(s.gk, t + 1)
                        wait(act, s.gate, t)
                        act.activation(ab[:, :], p_g[:, :], ACT.Abs).then_inc(s.ab, 1)
                        act.wait_ge(s.ab, t + 1)
                        act.activation(ab[:, :], ab[:, :], ACT.Exp, scale=-1.0).then_inc(s.ex1, 1)
                        act.wait_ge(s.ex1, t + 1)
                        act.activation(ab[:, :], ab[:, :], ACT.Ln, bias=1.0).then_inc(s.ln, 1)
                    if T := U.at(2):
                        t, hf, par = T
                        act.wait_ge(s.cum, t + 1)
                        wait(act, s.kt, t)
                        wait(act, s.ke, t)
                        r3 = lambda p: p[:, :].rearrange("p (h r d) -> p h r d", h=GH, r=2)
                        act.activation(e1[:, :, :, :], r3(p_inc), ACT.Exp, scale=1.0 / 16).then_inc(s.e1, 1)
                        act.activation(e2[:, :, :, :], r3(p_inc), ACT.Exp, scale=-1.0 / 16).then_inc(s.e2, 1)
                        act.activation(e3[:, :, :, :], r3(p_exc), ACT.Exp, scale=1.0 / 16).then_inc(s.e3, 1)
                        act.wait_ge(s.dec, t + 1)
                        act.activation(g.decay[:, :, bass.ds(2 * t, 2)], p_a[:, 256:256 + 2 * GH].rearrange("p (h c) -> p h c", c=2),
                                       ACT.Exp, scale=1.0 / 16).then_inc(s.edec, 1)
                    if T := U.at(3):
                        t, hf, par = T
                        act.wait_ge(s.tq, t + 1)
                        if not (isinstance(t, int) and t < 2):
                            act.wait_ge(s.out[par], hf * 16)
                        act.activation(qkT[:, par, :, 0, :], p_q[:, :].rearrange("p (h q) -> p h q", h=GH), ACT.Copy).then_inc(s.etq, 1)
                        act.wait_ge(s.tk, t + 1)
                        act.activation(qkT[:, par, :, 1, :], p_k[:, :].rearrange("p (h q) -> p h q", h=GH), ACT.Copy).then_inc(s.etk, 1)
                        ctx = cond_of(t)
                        chunk = 2 * (t - N_LAT) if ctx else 2 * t
                        act.wait_ge(s.scan, 2 * GH * (t + 1))
                        act.wait_ge(s.u, t + 1)
                        for c in range(2):
                            idx = slot_of(chunk + c - 1, ctx)
                            last = act.activation(g.states[DK:P, bass.ds(idx, 1)].rearrange("p o h v -> p (o h) v"),
                                                  p_u[c][DK:P, :].rearrange("p (h v) -> p h v", h=GH), ACT.Copy)
                        last.then_inc(s.ub, 1)

                steps(act, 4, step)

            @block.vector
            def _(dve):
                last_state = slot_of(T_CTX // CH - 1, True)
                dve.memset(g.states[0:DK, slot_of(0, True)], 0.0)
                dve.memset(g.states[DK:P, last_state], 0.0)
                dve.memset(lrT[2 * LR:2 * LR + 1, :], 1.0).then_inc(s.z, 1)
                dve.wait_ge(s.z, 1)
                dve.wait_ge(s.init, 32)

                def step(U):
                    if T := U.at(1):
                        t, hf, par = T
                        dve.wait_ge(s.lrp, t + 1)
                        wait(dve, s.gk, t)
                        dve.tensor_copy(lrT[0:2 * LR, :], p_a[0:2 * LR, 0:P]).then_inc(s.lrT, 1)
                    if T := U.at(2):
                        t, hf, par = T
                        dve.tensor_scalar(qs[:, :, :], qk[:, par, 0:GH * DK].rearrange("p (h d) -> p h d", h=GH), DK ** -0.5, None,
                                          ALU.mult).then_inc(s.qs, 1)
                        dve.wait_ge(s.qs, t + 1)
                        dve.wait_ge(s.e1, t + 1)
                        wait(dve, s.tq, t)
                        dve.tensor_tensor(qt[:, :, :, :], bc(qs[:, :, :], 2, 2), e1[:, :, :, :], ALU.mult).then_inc(s.qt, 1)
                        dve.wait_ge(s.e2, t + 1)
                        wait(dve, s.tk, t)
                        dve.tensor_tensor(kt[:, :, :, :], bc(qk[:, par, GH * DK:V0].rearrange("p (h d) -> p h d", h=GH), 2, 2),
                                          e2[:, :, :, :], ALU.mult).then_inc(s.kt, 1)
                    if T := U.at(1):
                        t, hf, par = T
                        dve.wait_ge(s.ln, t + 1)
                        dve.tensor_scalar(mn[:, :], p_g[:, :], 0.0, None, ALU.min).then_inc(s.mn, 1)
                        dve.wait_ge(s.mn, t + 1)
                        dve.tensor_tensor(gate[:, par].rearrange("p h r d -> p (h r d)"), mn[:, :], ab[:, :], ALU.subtract).then_inc(s.gate, 1)
                    if T := U.at(3):
                        t, hf, par = T
                        ctx = cond_of(t)
                        chunk = 2 * (t - N_LAT) if ctx else 2 * t
                        dve.wait_ge(s.u, t + 1)
                        dve.wait_ge(s.edec, t + 1)
                        for c in range(2):
                            if c:
                                dve.wait_ge(s.scan, 2 * GH * t + GH)
                            else:
                                wait(dve, s.scan, 2 * GH * t)
                            for h in range(GH):
                                idx = slot_of(chunk + c, ctx)
                                state = lambda i: g.states[0:DK, bass.ds(i, 1), h, :].rearrange("p o v -> p (o v)")
                                dve.scalar_tensor_tensor(state(idx + 1), state(idx), g.decay[0:DK, h, bass.ds(2 * t + c, 1)],
                                                         p_u[c][0:DK, h * DV:(h + 1) * DV], ALU.mult, ALU.add).then_inc(s.scan, 1)

                steps(dve, 4, step)
                dve.wait_ge(s.ub, NT)
                base = 2 * GH * NT

                def backwards(idx, tile_chunk, n):
                    dve.wait_ge(s.scan, base + n * GH)
                    for h in range(GH):
                        state = lambda i: g.states[DK:P, bass.ds(i, 1), h, :].rearrange("p o v -> p (o v)")
                        last = dve.scalar_tensor_tensor(state(idx - 1), state(idx), g.decay[DK:P, h, bass.ds(tile_chunk, 1)],
                                                        state(idx - 1), ALU.mult, ALU.add)
                        last.then_inc(s.scan, 1)
                    return last

                n_ctx = T_CTX // CH
                for n in range(n_ctx):
                    c = n_ctx - 1 - n
                    backwards(slot_of(c, True), T_LAT // CH + c, n)
                dve.wait_ge(s.scan, base + n_ctx * GH)
                dve.memset(ab[:, 0:1], 0.0).then_inc(s.back, 1)
                n_lat = T_LAT // CH
                with dve.Fori(0, n_lat - 1) as n:
                    backwards(n * -1 + n_lat, n * -1 + (n_lat - 1), n + n_ctx)
                dve.wait_ge(s.scan, base + (n_ctx + n_lat - 1) * GH)


def gla_outputs(nc, g):
    with ExitStack() as stack:
        ph = Phase(nc, stack, "go")
        s = ph.s
        (s.const, s.z0, s.qk0, s.qk1, s.vo0, s.vo1, s.af, s.abk, s.mf, s.mb, s.o, s.sq, s.ss, s.ms, s.rs, s.on, s.sg,
         s.gg, s.mix, s.tr, s.et, s.st0, s.st1) = ph.semaphores(
            "const z0 qk0 qk1 vo0 vo1 af abk mf mb o sq ss ms rs on sg gg mix tr et st0 st1")
        s.qk, s.vo, s.st = [s.qk0, s.qk1], [s.vo0, s.vo1], [s.st0, s.st1]
        qp = ph.sb("qp", [P, 2, GH, 4, CH])
        kT = ph.sb("kT", [P, 2, GH, P])
        vo = ph.sb("vo", [P, 2, 2 * GH * DV])
        mask = ph.sb("mask", [P, 2, P], U32)
        af = ph.sb("af", [P, 2, GH, P])
        ab = ph.sb("ab", [P, 2, GH, P])
        gg_ = ph.sb("gg_", [P, DV])
        sq = ph.sb("sq", [P, GH, DV])
        ss = ph.sb("ss", [P, GH])
        ms = ph.sb("ms", [P, GH])
        rs = ph.sb("rs", [P, GH])
        on = ph.sb("on", [P, GH, DV])
        sg = ph.sb("sg", [P, GH, DV])
        gg = ph.sb("gg", [P, GH, DV])
        mix = ph.sb("mix", [P, GH, DV])
        mT = ph.sb("mT", [P, 2, GH * P])
        p_f = ph.ps("p_f")
        p_b = ph.ps("p_b")
        p_o = [ph.ps("p_o0"), ph.ps("p_o1")]
        p_m = ph.ps("p_m")
        V0 = 2 * GH * DK

        with nc.Block() as block:

            @block.sync
            def _(sp):
                sp.dma_start(mask[:, :, :], g.d_mask).then_inc(s.const, 16)
                sp.dma_start(gg_[:, :], g.gla_norm_g.to_broadcast([P, DV])).then_inc(s.const, 16)
                sp.wait_ge(s.z0, 1)

                def step(U):
                    if T := U.at(3):
                        t, hf, par = T
                        sp.wait_ge(s.et, t + 1)
                        sp.dma_start(g.mix_tile(t)[:, 0:GH * P], mT[:, par, :]).then_inc(s.st[par], 16)
                    if T := U.at(0):
                        t, hf, par = T
                        wait(sp, s.o, t - 1)
                        src = g.qkT_tile(t).rearrange("p (h a c q) -> p h a c q", h=GH, a=2, c=2)
                        for c in range(2):
                            sp.dma_start(qp[:, par, :, 3 * c, :], src[:, :, 0, c, :]).then_inc(s.qk[par], 16)
                        sp.dma_start(kT[:, par], g.qkT_tile(t).rearrange("p (h a q) -> p h a q", h=GH, a=2)[:, :, 1, :]).then_inc(s.qk[par], 16)
                        wait(sp, s.sg, t - 1)
                        sp.dma_start(vo[:, par, :], g.proj_tile(t)[:, V0:V0 + 2 * GH * DV]).then_inc(s.vo[par], 16)

                steps(sp, 3, step)
                for par in range(2):
                    sp.wait_ge(s.st[par], 16 * (NT // 2))

            @block.gpsimd
            def _(pool):
                pool.wait_ge(s.const, 32)

                def step(U):
                    if T := U.at(1):
                        t, hf, par = T
                        pool.wait_ge(s.sg, t + 1)
                        wait(pool, s.mix, t)
                        pool.tensor_tensor(gg[:, :, :], sg[:, :, :], bc(gg_[:, :], 1, GH), ALU.mult).then_inc(s.gg, 1)
                        pool.wait_ge(s.ms, t + 1)
                        pool.tensor_tensor(rs[:, :], ms[:, :], g.neg_half[:, 0:GH], ALU.pow).then_inc(s.rs, 1)

                steps(pool, 3, step)

            @block.tensor
            def _(pe):
                def step(U):
                    if T := U.at(1):
                        t, hf, par = T
                        pe.wait_ge(s.qk[par], (hf + 1) * 48)
                        wait(pe, s.mf, t)
                        for r, (bank, done, free) in enumerate(((p_f, s.af, s.mf), (p_b, s.abk, s.mb))):
                            wait(pe, free, t)
                            rows = slice(r * DK, (r + 1) * DK)
                            for h in range(GH):
                                last = pe.matmul(bank[:, h * P:(h + 1) * P], kT[rows, par, h, :], qp[rows, par, h, 0:4:3, :], start=True, stop=True)
                            last.then_inc(done, 1)
                        pe.wait_ge(s.mf, t + 1)
                        pe.wait_ge(s.mb, t + 1)
                        pe.wait_ge(s.vo[par], (hf + 1) * 16)
                        wait(pe, s.on, t - 1)
                        ctx = cond_of(t)
                        chunk = 2 * (t - N_LAT) if ctx else 2 * t
                        for h in range(GH):
                            out = p_o[par][:, h * DV:(h + 1) * DV]
                            v = vo[:, par, h * DV:(h + 1) * DV]
                            pe.matmul(out, af[:, par, h, :], v, start=True, stop=False)
                            pe.matmul(out, ab[:, par, h, :], v, start=False, stop=False)
                            for c in range(2):
                                last = pe.matmul(out, qp[:, par, h, 2 * c:2 * c + 2, :].rearrange("p a q -> p (a q)"),
                                                 g.states[:, bass.ds(slot_of(chunk + c, ctx), 1), h, :].rearrange("p o v -> p (o v)"),
                                                 start=False, stop=c == 1)
                        last.then_inc(s.o, 1)
                    if T := U.at(2):
                        t, hf, par = T
                        pe.wait_ge(s.mix, t + 1)
                        wait(pe, s.et, t)
                        for h in range(GH):
                            last = pe.transpose(p_m[:, h * P:(h + 1) * P], mix[:, h, :], g.ident[:, :])
                        last.then_inc(s.tr, 1)

                steps(pe, 3, step)

            @block.scalar
            def _(act):
                def step(U):
                    if T := U.at(1):
                        t, hf, par = T
                        act.wait_ge(s.vo[par], (hf + 1) * 16)
                        wait(act, s.gg, t)
                        act.activation(sg[:, :, :].rearrange("p h v -> p (h v)"), vo[:, par, GH * DV:2 * GH * DV], ACT.Silu).then_inc(s.sg, 1)
                        act.wait_ge(s.o, t + 1)
                        wait(act, s.ss, t)
                        act.activation(sq[:, :, :].rearrange("p h v -> p (h v)"), p_o[par][:, :], ACT.Square).then_inc(s.sq, 1)
                    if T := U.at(2):
                        t, hf, par = T
                        act.wait_ge(s.tr, t + 1)
                        if not (isinstance(t, int) and t < 2):
                            act.wait_ge(s.st[par], hf * 16)
                        act.activation(mT[:, par, :], p_m[:, :], ACT.Copy).then_inc(s.et, 1)

                steps(act, 3, step)

            @block.vector
            def _(dve):
                dve.memset(qp[:, :, :, 1:3, :], 0.0).then_inc(s.z0, 1)
                dve.wait_ge(s.const, 32)

                def step(U):
                    if T := U.at(1):
                        t, hf, par = T
                        for r, (bank, done, to, got) in enumerate(((p_f, s.mf, af, s.af), (p_b, s.mb, ab, s.abk))):
                            dve.wait_ge(got, t + 1)
                            wait(dve, s.o, t - 1)
                            dve.tensor_tensor(to[:, par].bitcast(U32), bank[:, :].rearrange("p (h q) -> p h q", h=GH).bitcast(U32),
                                              bc(mask[:, r, :], 1, GH), ALU.bitwise_and).then_inc(done, 1)
                        dve.wait_ge(s.sq, t + 1)
                        dve.tensor_reduce(ss[:, :], sq[:, :, :], AX.X, ALU.add).then_inc(s.ss, 1)
                        dve.wait_ge(s.ss, t + 1)
                        dve.tensor_scalar(ms[:, :], ss[:, :], 1.0 / DV, EPS, ALU.mult, ALU.add).then_inc(s.ms, 1)
                        dve.wait_ge(s.rs, t + 1)
                        dve.tensor_tensor(on[:, :, :], p_o[par][:, :].rearrange("p (h v) -> p h v", h=GH), bc(rs[:, :], 2, DV),
                                          ALU.mult).then_inc(s.on, 1)
                        dve.wait_ge(s.on, t + 1)
                        dve.wait_ge(s.gg, t + 1)
                        wait(dve, s.tr, t)
                        dve.tensor_tensor(mix[:, :, :], on[:, :, :], gg[:, :, :], ALU.mult).then_inc(s.mix, 1)

                steps(dve, 3, step)


def output_projection(nc, g):
    with ExitStack() as stack:
        ph = Phase(nc, stack, "op")
        s = ph.s
        (s.gates, s.m0, s.m1, s.x0, s.x1, s.mhi, s.mlo, s.y0, s.y1, s.g0, s.g1, s.r, s.xs0, s.xs1, s.sq, s.ms, s.rstd,
         s.xn, s.tr, s.hT, s.hs0, s.hs1) = ph.semaphores(
            "gates m0 m1 x0 x1 mhi mlo y0 y1 g0 g1 r xs0 xs1 sq ms rstd xn tr hT hs0 hs1")
        s.m, s.x, s.y, s.gt, s.xs, s.hs = [s.m0, s.m1], [s.x0, s.x1], [s.y0, s.y1], [s.g0, s.g1], [s.xs0, s.xs1], [s.hs0, s.hs1]
        w_hi = ph.sb("w_hi", [P, KC, D_MODEL], F32R)
        w_lo = ph.sb("w_lo", [P, KC, D_MODEL], F32R)
        stage = ph.sb("stage", [P, 2, D_MODEL])
        gate = ph.sb("gate", [P, 2, D_MODEL])
        m = ph.sb("m", [P, 2, KC, P])
        mhi = ph.sb("mhi", [P, 2, KC, P], F32R)
        mlo = ph.sb("mlo", [P, 2, KC, P], F32R)
        x = ph.sb("x", [P, 2, D_MODEL])
        y = ph.sb("y", [P, D_MODEL])
        x1 = ph.sb("x1", [P, 2, D_MODEL])
        xn = ph.sb("xn", [P, D_MODEL])
        junk = ph.sb("junk", [P, D_MODEL])
        ss = ph.sb("ss", [P, 1])
        ms = ph.sb("ms", [P, 1])
        rstd = ph.sb("rstd", [P, 1])
        hT = ph.sb("hT", [P, 2, KC, P])
        p_y = [[ph.ps(f"p_y{a}{b}") for b in range(2)] for a in range(2)]
        p_t = ph.ps("p_t", 1024)
        w_sp, w_act, w_dve = load_split_weights(ph, s, g.w_out[0], KC, D_MODEL, w_hi, w_lo, stage)

        with nc.Block() as block:

            @block.sync
            def _(sp):
                for c in range(2):
                    sp.dma_start(gate[:, c, :], g.mod_d[c:c + 1, 2 * D_MODEL:3 * D_MODEL].to_broadcast([P, D_MODEL])).then_inc(s.gates, 16)
                w_sp(sp)

                def step(U):
                    if T := U.at(0):
                        t, hf, par = T
                        wait(sp, s.mlo, t - 1)
                        sp.dma_start(m[:, par].rearrange("p k q -> p (k q)"), g.mix_tile(t)).then_inc(s.m[par], 16)
                        wait(sp, s.r, t - 1)
                        sp.dma_start(x[:, par, :], g.x_tile(t)).then_inc(s.x[par], 16)
                    if T := U.at(3):
                        t, hf, par = T
                        sp.wait_ge(s.r, t + 1)
                        sp.dma_start(g.x1_tile(t), x1[:, par, :]).then_inc(s.xs[par], 16)
                steps(sp, 4, step)
                for par in range(2):
                    sp.wait_ge(s.xs[par], 16 * (NT // 2))

            @block.gpsimd
            def _(pool):
                def step(U):
                    if T := U.at(2):
                        t, hf, par = T
                        pool.wait_ge(s.ms, t + 1)
                        pool.tensor_tensor(rstd[:, :], ms[:, :], g.neg_half[:, 0:1], ALU.pow).then_inc(s.rstd, 1)
                    if T := U.at(4):
                        t, hf, par = T
                        pool.wait_ge(s.hT, t + 1)
                        pool.dma_start(g.h2_tile(t), hT[:, par]).then_inc(s.hs[par], 16)

                steps(pool, 4, step)
                for par in range(2):
                    pool.wait_ge(s.hs[par], 16 * (NT // 2))

            @block.tensor
            def _(pe):
                pe.wait_ge(s.w_lo, KC)

                def step(U):
                    if T := U.at(1):
                        t, hf, par = T
                        pe.wait_ge(s.mlo, t + 1)
                        for n in range(2):
                            wait(pe, s.gt[n], t - 1)
                            for k in range(KC):
                                last = split_product(pe, p_y[par][n][:, :], ((mhi[:, par, k], mlo[:, par, k]),
                                                     (w_hi[:, k, n * 512:(n + 1) * 512], w_lo[:, k, n * 512:(n + 1) * 512])),
                                                     k == 0, k == KC - 1)
                            last.then_inc(s.y[n], 1)
                    if T := U.at(3):
                        t, hf, par = T
                        pe.wait_ge(s.xn, t + 1)
                        wait(pe, s.hT, t)
                        for k in range(KC):
                            last = pe.transpose(p_t[:, k * P:(k + 1) * P], xn[:, k * P:(k + 1) * P], g.ident[:, :])
                        last.then_inc(s.tr, 1)

                steps(pe, 4, step)

            @block.scalar
            def _(act):
                w_act(act)

                def step(U):
                    if T := U.at(0):
                        t, hf, par = T
                        act.wait_ge(s.m[par], (hf + 1) * 16)
                        wait(act, s.y[1], t - 1)
                        act.activation(mhi[:, par], m[:, par], ACT.Copy).then_inc(s.mhi, 1)
                    if T := U.at(2):
                        t, hf, par = T
                        act.wait_ge(s.r, t + 1)
                        wait(act, s.ms, t)
                        act.activation(junk[:, :], x1[:, par, :], ACT.Square, accum_out=ss[:, :]).then_inc(s.sq, 1)
                    if T := U.at(3):
                        t, hf, par = T
                        act.wait_ge(s.tr, t + 1)
                        if not (isinstance(t, int) and t < 2):
                            act.wait_ge(s.hs[par], hf * 16)
                        c = cond_of(t)
                        for k in range(KC):
                            last = act.activation(hT[:, par, k, :], p_t[:, k * P:(k + 1) * P], ACT.Identity,
                                                  bias=g.lnp[:, 1, c, 1, k:k + 1], scale=g.lnp[:, 1, c, 0, k:k + 1])
                        last.then_inc(s.hT, 1)

                steps(act, 4, step)

            @block.vector
            def _(dve):
                w_dve(dve)
                dve.wait_ge(s.gates, 32)

                def step(U):
                    if T := U.at(0):
                        t, hf, par = T
                        dve.wait_ge(s.mhi, t + 1)
                        dve.tensor_tensor(mlo[:, par], m[:, par], mhi[:, par].bitcast(F32), ALU.subtract).then_inc(s.mlo, 1)
                    if T := U.at(2):
                        t, hf, par = T
                        c = cond_of(t)
                        for n in range(2):
                            dve.wait_ge(s.y[n], t + 1)
                            cols = slice(n * 512, (n + 1) * 512)
                            dve.tensor_tensor(y[:, cols], p_y[par][n][:, :], gate[:, c, cols], ALU.mult).then_inc(s.gt[n], 1)
                        dve.wait_ge(s.gt[0], t + 1)
                        dve.wait_ge(s.gt[1], t + 1)
                        dve.wait_ge(s.x[par], (hf + 1) * 16)
                        if not (isinstance(t, int) and t < 2):
                            dve.wait_ge(s.xs[par], hf * 16)
                        dve.tensor_tensor(x1[:, par, :], y[:, :], x[:, par, :], ALU.add).then_inc(s.r, 1)
                        dve.wait_ge(s.sq, t + 1)
                        dve.tensor_scalar(ms[:, :], ss[:, :], 1.0 / D_MODEL, EPS, ALU.mult, ALU.add).then_inc(s.ms, 1)
                        dve.wait_ge(s.rstd, t + 1)
                        wait(dve, s.tr, t)
                        dve.tensor_scalar(xn[:, :], x1[:, par, :], rstd[:, :], None, ALU.mult).then_inc(s.xn, 1)

                steps(dve, 4, step)


def feed_forward(nc, g):
    BT = 512
    BTT = BT // P
    HN = 512
    KG = 4
    DOWN = [(n, k, min(k + KG, NF)) for n in range(2) for k in range(0, NF, KG)]
    ITEMS = NF + len(DOWN)
    N_LB = T_LAT // BT
    with ExitStack() as stack:
        ph = Phase(nc, stack, "ff")
        s = ph.s
        (s.w0, s.w1, s.w_hi, s.w_lo, s.h0, s.h1, s.h_hi, s.h_lo, s.fing, s.x, s.a, s.used, s.silu, s.mul, s.ghi, s.glo,
         s.y, s.gt, s.res, s.sq, s.ms, s.rs, s.fin, s.out) = ph.semaphores(
            "w0 w1 w_hi w_lo h0 h1 h_hi h_lo fing x a used silu mul ghi glo y gt res sq ms rs fin out")
        s.w = [s.w0, s.w1]
        ws = ph.sb("ws", [P, 2, 2 * KC * P])
        whi = ph.sb("whi", [P, 2, 2 * KC * P], F32R)
        wlo = ph.sb("wlo", [P, 2, 2 * KC * P], F32R)
        hs = ph.sb("hs", [P, 2, BT])
        hhi = ph.sb("hhi", [P, KC, BT], F32R)
        hlo = ph.sb("hlo", [P, KC, BT], F32R)
        ghi = ph.sb("ghi", [P, NF, BT], F32R)
        glo = ph.sb("glo", [P, NF, BT], F32R)
        sil = ph.sb("sil", [P, 2, BT])
        tmp = ph.sb("tmp", [P, HN])
        x1 = ph.sb("x1", [P, BTT, D_MODEL])
        gate = ph.sb("gate", [P, D_MODEL])
        fing = ph.sb("fing", [P, D_MODEL])
        ss = ph.sb("ss", [P, BTT])
        ms = ph.sb("ms", [P, BTT])
        rs = ph.sb("rs", [P, BTT])
        bank = [ph.ps(f"p{j}") for j in range(8)]
        w13 = [w[0].rearrange("(k p) n -> p k n", p=P) for w in (g.w_ffn1, g.w_ffn3)]
        w2 = g.w_ffn2[0].rearrange("(k p) n -> p k n", p=P)

        def width(b):
            return T_CTX if isinstance(b, int) and b == N_LB else BT

        def blocks(eng, body):
            body(0)
            with eng.Fori(1, N_LB - 1) as b:
                body(b)
            body(N_LB - 1)
            body(N_LB)

        def up_items(eng, b, body):
            for par in range(2):
                body(par, par, b * ITEMS + par, b * (ITEMS // 2))
            with eng.Fori(1, NF // 2) as i:
                for par in range(2):
                    body(i * 2 + par, par, b * ITEMS + i * 2 + par, b * (ITEMS // 2) + i)

        def down_items(b, body):
            for i, (n, k0, k1) in enumerate(DOWN):
                body(i, n, k0, k1, i % 2, b * ITEMS + (NF + i), b * (ITEMS // 2) + (NF + i) // 2)

        def h_rows(i):
            return range(2 * (i - 1), 2 * i) if 1 <= i <= KC // 2 else ()

        with nc.Block() as block:

            @block.sync
            def _(sp):
                def load_h(b, k):
                    wait(sp, s.h_lo, b * KC + (k - 1))
                    sp.dma_start(hs[:, k % 2, 0:width(b)], g.h2_rows(b, k, width(b))).then_inc([s.h0, s.h1][k % 2], 16)

                for k in range(KC):
                    load_h(0, k)

                def body(b):
                    def up(f, par, item, pair):
                        wait(sp, s.w_lo, item - 1)
                        for j in range(2):
                            sp.dma_start(ws[:, par, j * KC * P:(j + 1) * KC * P].rearrange("p (k n) -> p k n", k=KC),
                                         w13[j][:, :, bass.ds(f * P, P)]).then_inc(s.w[par], 16)

                    def down(i, n, k0, k1, par, item, pair):
                        wait(sp, s.w_lo, item - 1)
                        mid = (k0 + k1) // 2
                        for ka, kb in ((k0, mid), (mid, k1)):
                            sp.dma_start(ws[:, par, (ka - k0) * HN:(kb - k0) * HN].rearrange("p (k n) -> p k n", n=HN),
                                         w2[:, ka:kb, n * HN:(n + 1) * HN]).then_inc(s.w[par], 16)
                        if not (isinstance(b, int) and b == N_LB):
                            for k in h_rows(i):
                                load_h(b + 1, k)

                    up_items(sp, b, up)
                    down_items(b, down)

                blocks(sp, body)

            @block.gpsimd
            def _(pool):
                pool.dma_start(fing[:, :], g.final_g.rearrange("(a n) -> a n", a=1).to_broadcast([P, D_MODEL])).then_inc(s.fing, 16)

                def body(b):
                    nt = width(b) // P
                    wait(pool, s.out, b * (16 * BTT))
                    pool.dma_start(x1[:, 0:nt, :], g.x1_rows(b, width(b))).then_inc(s.x, 16)
                    pool.dma_start(gate[:, :], g.gate2(b)).then_inc(s.x, 16)
                    for t in range(nt):
                        pool.wait_ge(s.ms, b * BTT + (t + 1))
                        pool.tensor_tensor(rs[:, t:t + 1], ms[:, t:t + 1], g.neg_half[:, 0:1], ALU.pow).then_inc(s.rs, 1)
                    for t in range(nt):
                        pool.wait_ge(s.fin, b * BTT + (t + 1))
                        pool.dma_start(g.y_rows(b, t), x1[:, t, :]).then_inc(s.out, 16)

                blocks(pool, body)
                pool.wait_ge(s.out, 16 * NT)

            @block.tensor
            def _(pe):
                def body(b):
                    bt = width(b)
                    nt = bt // P

                    def up(f, par, item, pair):
                        pe.wait_ge(s.w_lo, item + 1)
                        if isinstance(f, int) and f == 0:
                            pe.wait_ge(s.h_lo, b * KC + KC)
                            wait(pe, s.res, b * (2 * BTT))
                        wait(pe, s.glo, b * NF + (f - 1))
                        for j in range(2):
                            for k in range(KC):
                                c = slice((j * KC + k) * P, (j * KC + k + 1) * P)
                                last = split_product(pe, bank[2 * par + j][:, 0:bt], ((whi[:, par, c], wlo[:, par, c]),
                                                     (hhi[:, k, 0:bt], hlo[:, k, 0:bt])), k == 0, k == KC - 1)
                            last.then_inc(s.used if j else s.a, 1)

                    def down(i, n, k0, k1, par, item, pair):
                        pe.wait_ge(s.w_lo, item + 1)
                        pe.wait_ge(s.glo, b * NF + (k1 if n == 0 else NF))
                        last_item = k1 == NF
                        order = [(k, t) for t in range(nt) for k in range(k0, k1)] if last_item else \
                                [(k, t) for k in range(k0, k1) for t in range(nt)]
                        for k, t in order:
                            c = slice((k - k0) * HN, (k - k0 + 1) * HN)
                            q = slice(t * P, (t + 1) * P)
                            last = split_product(pe, bank[4 * (1 - n) + t][:, :], ((ghi[:, k, q], glo[:, k, q]),
                                                 (whi[:, par, c], wlo[:, par, c])), k == 0, k == NF - 1)
                            if k == NF - 1 and t < nt - 1:
                                last.then_inc(s.y, 1)
                        last.then_inc(s.used, 1)

                    up_items(pe, b, up)
                    down_items(b, down)

                blocks(pe, body)

            def weights_high(act, par, item, pair, cols):
                act.wait_ge(s.w[par], pair * 32 + 32)
                wait(act, s.used, item - 1)
                act.activation(whi[:, par, 0:cols], ws[:, par, 0:cols], ACT.Copy).then_inc(s.w_hi, 1)

            def weights_low(dve, par, item, pair, cols):
                dve.wait_ge(s.w_hi, item + 1)
                dve.tensor_tensor(wlo[:, par, 0:cols], ws[:, par, 0:cols], whi[:, par, 0:cols].bitcast(F32), ALU.subtract).then_inc(s.w_lo, 1)

            @block.scalar
            def _(act):
                def h_high(b, k):
                    act.wait_ge([s.h0, s.h1][k % 2], b * (KC // 2 * 16) + (k // 2 + 1) * 16)
                    act.activation(hhi[:, k, 0:width(b)], hs[:, k % 2, 0:width(b)], ACT.Copy).then_inc(s.h_hi, 1)

                for k in range(KC):
                    h_high(0, k)

                def squares(b):
                    for t in range(width(b) // P):
                        act.wait_ge(s.res, b * (2 * BTT) + (width(b) // P + t + 1))
                        wait(act, s.sq, b * BTT + t)
                        act.activation(sil[:, :, :].rearrange("p a n -> p (a n)"), x1[:, t, :], ACT.Square, accum_out=ss[:, t:t + 1]).then_inc(s.sq, 1)

                def silu(b, f, par):
                    act.wait_ge(s.a, b * NF + (f + 1))
                    wait(act, s.glo, b * NF + (f - 1))
                    act.activation(sil[:, par, 0:width(b)], bank[2 * par][:, 0:width(b)], ACT.Silu).then_inc(s.silu, 1)

                def body(b):
                    def up(f, par, item, pair):
                        weights_high(act, par, item, pair, 2 * KC * P)
                        if isinstance(f, int) and f == 0:
                            return
                        if isinstance(f, int) and f == 1 and not (isinstance(b, int) and b == 0):
                            act.wait_ge(s.glo, b * NF)
                            squares(b - 1)
                            act.wait_ge(s.sq, b * BTT)
                        silu(b, f - 1, 1 - par)

                    def down(i, n, k0, k1, par, item, pair):
                        weights_high(act, par, item, pair, (k1 - k0) * HN)
                        if i == 0:
                            silu(b, NF - 1, 1)
                        if not (isinstance(b, int) and b == N_LB):
                            for k in h_rows(i):
                                act.wait_ge(s.used, b * ITEMS + NF)
                                h_high(b + 1, k)

                    up_items(act, b, up)
                    down_items(b, down)

                blocks(act, body)
                squares(N_LB)

            @block.vector
            def _(dve):
                def h_low(b, k):
                    dve.wait_ge(s.h_hi, b * KC + (k + 1))
                    dve.tensor_tensor(hlo[:, k, 0:width(b)], hs[:, k % 2, 0:width(b)], hhi[:, k, 0:width(b)].bitcast(F32), ALU.subtract).then_inc(s.h_lo, 1)

                for k in range(KC):
                    h_low(0, k)

                def residual(b, n):
                    nt = width(b) // P
                    cols = slice(n * HN, (n + 1) * HN)
                    for t in range(nt):
                        done = b * (2 * BTT) + (n * nt + t)
                        if t < nt - 1:
                            dve.wait_ge(s.y, b * (2 * (BTT - 1)) + (n * (nt - 1) + t + 1))
                        else:
                            dve.wait_ge(s.used, b * ITEMS + (NF + (n + 1) * (len(DOWN) // 2)))
                        wait(dve, s.res, done)
                        dve.tensor_tensor(tmp[:, :], bank[4 * (1 - n) + t][:, :], gate[:, cols], ALU.mult).then_inc(s.gt, 1)
                        dve.wait_ge(s.gt, done + 1)
                        dve.tensor_tensor(x1[:, t, cols], x1[:, t, cols], tmp[:, :], ALU.add).then_inc(s.res, 1)

                def final_norm(b):
                    for t in range(width(b) // P):
                        done = b * BTT + t
                        dve.wait_ge(s.sq, done + 1)
                        dve.tensor_scalar(ms[:, t:t + 1], ss[:, t:t + 1], 1.0 / D_MODEL, EPS, ALU.mult, ALU.add).then_inc(s.ms, 1)
                        dve.wait_ge(s.rs, done + 1)
                        dve.scalar_tensor_tensor(x1[:, t, :], x1[:, t, :], rs[:, t:t + 1], fing[:, :], ALU.mult, ALU.mult).then_inc(s.fin, 1)

                def gated(b, f, par):
                    dve.wait_ge(s.silu, b * NF + (f + 1))
                    dve.wait_ge(s.used, b * ITEMS + (f + 1))
                    bt = width(b)
                    dve.tensor_tensor(sil[:, par, 0:bt], sil[:, par, 0:bt], bank[2 * par + 1][:, 0:bt], ALU.mult).then_inc(s.mul, 1)
                    dve.wait_ge(s.mul, b * NF + (f + 1))
                    hi = ghi[:, bass.ds(f, 1), 0:bt].rearrange("p o q -> p (o q)")
                    lo = glo[:, bass.ds(f, 1), 0:bt].rearrange("p o q -> p (o q)")
                    dve.tensor_copy(hi, sil[:, par, 0:bt]).then_inc(s.ghi, 1)
                    dve.wait_ge(s.ghi, b * NF + (f + 1))
                    dve.tensor_tensor(lo, sil[:, par, 0:bt], hi.bitcast(F32), ALU.subtract).then_inc(s.glo, 1)

                def body(b):
                    def up(f, par, item, pair):
                        weights_low(dve, par, item, pair, 2 * KC * P)
                        begin = isinstance(f, int) and not (isinstance(b, int) and b == 0)
                        if begin and f == 0:
                            residual(b - 1, 1)
                        if begin and f == 1:
                            final_norm(b - 1)
                        if not (isinstance(f, int) and f == 0):
                            gated(b, f - 1, 1 - par)

                    def down(i, n, k0, k1, par, item, pair):
                        weights_low(dve, par, item, pair, (k1 - k0) * HN)
                        if i == 0:
                            gated(b, NF - 1, 1)
                        if not (isinstance(b, int) and b == N_LB):
                            for k in h_rows(i):
                                h_low(b + 1, k)
                        if i == len(DOWN) // 2 + 1:
                            dve.wait_ge(s.x, b * 32 + 32)
                            residual(b, 0)

                    up_items(dve, b, up)
                    down_items(b, down)

                dve.wait_ge(s.fing, 16)
                blocks(dve, body)
                residual(N_LB, 1)
                final_norm(N_LB)


def hybrid_block(nc, a, outs, consts):
    with ExitStack() as top:
        g = Names()
        (g.c, g.c_ctx, g.ada_w, g.ada_b, g.norm1_g, g.norm2_g, g.w_in, g.w_gk2, g.b_gk2, g.gla_norm_g, g.q_norm_g, g.k_norm_g,
         g.w_out, g.w_ffn1, g.w_ffn3, g.w_ffn2, g.final_g) = (a[name] for name in _INS[6:])
        g.d_ident, g.d_tri, g.d_ind, g.d_mask, d_rope = consts
        y_prompt, y_sample, new_k, new_v, new_f, new_b = outs
        g.new_k = new_k.rearrange("b l t h d -> (b l t) (h d)")
        g.new_v = new_v.rearrange("b l t h d -> (b l t) (h d)")
        g.new_f, g.new_b = new_f[0, 0], new_b[0, 0]
        g.cache_k = a["cache_k"].rearrange("b l t h d -> (b l t) (h d)")
        g.cache_v = a["cache_v"].rearrange("b l t h d -> (b l t) (h d)")
        g.state_f, g.state_b = a["state_gla_fwd"][0, 0], a["state_gla_bwd"][0, 0]

        def scratch(name, shape, dt=F32):
            return nc.dram_tensor(name, shape, dt, kind="Internal").ap()

        g.mod_d = scratch("mod_d", (2, N_MOD * D_MODEL))
        qT_d = scratch("qT_d", (NT, P, AH * P))
        mix_d = scratch("mix_d", (NT, P, KC * P))
        proj_d = scratch("proj_d", (NT * P, D_GLA))
        qkT_d = scratch("qkT_d", (NT, P, 2 * GH * P))
        x1_d = scratch("x1_d", (NT * P, D_MODEL))
        h2_d = scratch("h2_d", (KC, P, NT * P))

        def tile_of(d):
            return lambda t: d[bass.ds(t, 1)].rearrange("o p n -> (o p) n")

        def rows_of(lat, ctx):
            return lambda t: ctx[(t - N_LAT) * P:(t - N_LAT + 1) * P, :] if cond_of(t) else lat[bass.ds(t * P, P), :]

        g.qT_tile, g.mix_tile, g.qkT_tile = tile_of(qT_d), tile_of(mix_d), tile_of(qkT_d)
        g.proj_tile = lambda t: proj_d[bass.ds(t * P, P), :]
        g.rope_tile = lambda t: d_rope[bass.ds(t * P, P), :]
        g.x1_tile = lambda t: x1_d[bass.ds(t * P, P), :]
        g.x_tile = rows_of(a["x_sample"][0], a["x_prompt"][0])
        g.h2_tile = lambda t: h2_d[:, :, bass.ds(t * P, P)].rearrange("k p q -> p k q")
        g.h2_rows = lambda b, k, n: h2_d[k, :, bass.ds(b * 512, n)]
        g.x1_rows = lambda b, n: x1_d[bass.ds(b * 512, n), :].rearrange("(t p) n -> p t n", p=P)
        y_tile = rows_of(y_sample[0], y_prompt[0])
        g.y_rows = lambda b, t: y_tile(b * 4 + t)

        def gate2(b):
            c = 1 if isinstance(b, int) and b == T_LAT // 512 else 0
            return g.mod_d[c:c + 1, 5 * D_MODEL:6 * D_MODEL].to_broadcast([P, D_MODEL])

        g.gate2 = gate2
        g.ident = top.enter_context(nc.sbuf_tensor("ident", [P, P], F32))
        g.lnp = top.enter_context(nc.sbuf_tensor("lnp", [P, 2, 2, 2, KC], F32))
        g.neg_half = top.enter_context(nc.sbuf_tensor("neg_half", [P, 16], F32))
        modulation(nc, g)
        with ExitStack() as att:
            g.keysT = att.enter_context(nc.sbuf_tensor("keysT", [P, KVH, 2, (N_LAT + 4) * P], F32R))
            g.vals = att.enter_context(nc.sbuf_tensor("vals", [P, (N_LAT + 4) * KVH, 2 * HD], F32R))
            attention_projection(nc, g)
            attention(nc, g)
        gla_projection(nc, g)
        with ExitStack() as gla:
            g.states = gla.enter_context(nc.sbuf_tensor("states", [P, SLOTS, GH, DV], F32))
            g.decay = gla.enter_context(nc.sbuf_tensor("decay", [P, GH, NT * 2], F32))
            gla_states(nc, g)
            gla_outputs(nc, g)
        output_projection(nc, g)
        feed_forward(nc, g)


_INS = ["x_prompt", "x_sample", "cache_k", "cache_v", "state_gla_fwd", "state_gla_bwd", "c", "c_ctx", "ada_w", "ada_b", "norm1_g",
        "norm2_g", "w_in", "w_gk2", "b_gk2", "gla_norm_g", "q_norm_g", "k_norm_g", "w_out", "w_ffn1", "w_ffn3", "w_ffn2", "final_g"]
_OUTS = [(1, T_CTX, D_MODEL), (1, T_LAT, D_MODEL), (1, 1, T_CTX, KVH, HD), (1, 1, T_CTX, KVH, HD), (1, 1, GH, DK, DV), (1, 1, GH, DK, DV)]


def _constants():
    j, i = np.meshgrid(np.arange(P), np.arange(P), indexing="ij")
    same = (i // CH) == (j // CH)
    tri = np.stack([same & (j <= i), same & (j >= i), same & (j > i), same & (j < i)], axis=1).astype(np.float32)
    ind = ((np.arange(P)[:, None] // CH) == np.arange(2)[None, :]).astype(np.float32)
    t = np.arange(T_LAT)
    half = HD // 4
    inv = (np.float32(10000.0) ** (-np.arange(0, 2 * half, 2, dtype=np.float32) / np.float32(2 * half))).astype(np.float32)
    pos = np.stack([t // GRID_W, t % GRID_W], axis=1).astype(np.float32)
    ang = pos[:, :, None] * inv
    c, sn = np.cos(ang), np.sin(ang)
    rope = np.zeros((NT * P, 2, 2, 2, half), np.float32)
    rope[:, 0] = 1.0
    rope[:T_LAT, 0] = c[:, :, None, :]
    rope[:T_LAT, 1, :, 0] = -sn
    rope[:T_LAT, 1, :, 1] = sn
    bits = np.where(tri[:, 0:2] > 0, np.uint32(0xFFFFFFFF), np.uint32(0))
    return [np.eye(P, dtype=np.float32), tri, ind, bits, rope.reshape(NT * P, 2 * HD)]


def lay_out(nc, inputs):
    arrays, args, outs, consts = {}, {}, [], []
    for name in _INS:
        x = np.ascontiguousarray(inputs[name])
        arrays[f"in_{name}_dram"] = x
        args[name] = nc.dram_tensor(f"in_{name}_dram", x.shape, mybir.dt.from_np(x.dtype), kind="ExternalInput").ap()
    for n, x in enumerate(_constants()):
        arrays[f"const_{n}_dram"] = x
        consts.append(nc.dram_tensor(f"const_{n}_dram", x.shape, mybir.dt.from_np(x.dtype), kind="ExternalInput").ap())
    for n, shape in enumerate(_OUTS):
        outs.append(nc.dram_tensor(f"out_{n}_dram", shape, F32, kind="ExternalOutput").ap())
    hybrid_block(nc, args, outs, consts)
    return arrays


def kernel(**inputs):
    import concourse.bacc as _bacc
    from concourse.bass_utils import run_bass_kernel_spmd as _run

    nc = _bacc.Bacc("TRN2", target_bir_lowering=False, num_devices=1)
    arrays = lay_out(nc, inputs)
    r = _run(nc, [arrays], core_ids=[0])
    return tuple(r.results[0][f"out_{n}_dram"] for n in range(len(_OUTS)))
```

```python
from contextlib import ExitStack

import numpy as np

import concourse.bass as bass
from concourse import mybir

F32 = mybir.dt.float32
F32R = mybir.dt.float32r
U32 = mybir.dt.uint32
ALU = mybir.AluOpType
ACT = mybir.ActivationFunctionType
AX = mybir.AxisListType

P = 128
D_MODEL = 1024
KC = D_MODEL // P
T_LAT = 2048
T_CTX = 256
PAST = 256
N_LAT = T_LAT // P
N_CTX = T_CTX // P
NT = N_LAT + N_CTX
GH = 4
DK = 64
DV = 128
LR = 16
AH = 8
KVH = 2
HD = 64
D_GLA = 2 * GH * DK + 2 * GH * DV + 2 * LR
D_ATT = AH * HD + 2 * KVH * HD
D_FF = 2816
NF = D_FF // P
EPS = 1e-6
CH = 64
N_MOD = 6
MOD_FIRST = 2 * D_MODEL // 512
GRID_W = 64
W_STAGES = 4
LAT_SLOTS = T_LAT // CH + 2
CTX_SLOTS = T_CTX // CH + 2
SLOTS = LAT_SLOTS + CTX_SLOTS


def wait(eng, sem, value):
    if not (isinstance(value, int) and value <= 0):
        eng.wait_ge(sem, value)


class Step:

    def __init__(self, half, par, static):
        self.half, self.par, self.static = half, par, static

    def first(self, u):
        return self.static and 2 * self.half + self.par == u

    def at(self, off):
        t = 2 * self.half + self.par - off if self.static else self.half * 2 + (self.par - off)
        if self.static:
            return (t, t // 2, t % 2) if 0 <= t < NT else None
        return t, self.half + (self.par - off) // 2, (self.par - off) % 2


def steps(eng, depth, body):
    first = (depth + 2) // 2
    for u in range(2 * first):
        body(Step(u // 2, u % 2, True))
    with eng.Fori(first, N_LAT // 2) as i:
        for par in range(2):
            body(Step(i, par, False))
    for u in range(N_LAT, NT + depth):
        body(Step(u // 2, u % 2, True))


def cond_of(t):
    return 1 if isinstance(t, int) and t >= N_LAT else 0


def bc(ap, axis, n):
    a = ap.unsqueeze(axis)
    shape = list(a.shape)
    shape[axis] = n
    return a.to_broadcast(shape)


class Names:
    pass


class Phase:

    def __init__(self, nc, stack, name):
        self.nc, self.stack, self.name = nc, stack, name
        self.s = Names()
        self.handles = []
        stack.callback(self.clear)

    def semaphores(self, names):
        new = [self.nc.alloc_semaphore(name=f"{self.name}_{n}") for n in names.split()]
        self.handles += new
        return new

    def clear(self):
        self.nc.clear_and_free_semaphores(self.handles)
        self.nc.all_engine_barrier()

    def sb(self, name, shape, dt=F32):
        return self.stack.enter_context(self.nc.sbuf_tensor(f"{self.name}_{name}", shape, dt))

    def ps(self, name, cols=512):
        return self.stack.enter_context(self.nc.psum_tensor(f"{self.name}_{name}", [P, cols], F32))


def modulation(nc, g):
    NCH = MOD_FIRST
    with ExitStack() as stack:
        ph = Phase(nc, stack, "mod")
        s = ph.s
        (s.rows, s.w0, s.w1, s.silu, s.tr, s.cT, s.acc, s.bias, s.out, s.back, s.mtr, s.mT, s.done) = ph.semaphores(
            "rows w0 w1 silu tr cT acc bias out back mtr mT done")
        s.w = [s.w0, s.w1]
        crow = ph.sb("crow", [2 * KC, P])
        nrow = ph.sb("nrow", [2 * KC, P])
        srow = ph.sb("srow", [2 * KC, P])
        adab = ph.sb("adab", [2, NCH * 512])
        mod = ph.sb("mod", [2, NCH * 512])
        aw = ph.sb("aw", [P, 2, KC, 512])
        cT, nT = g.cT, g.nT
        modr = ph.sb("modr", [4 * KC, P])
        modT = ph.sb("modT", [P, 2, 2, KC])
        p_tr = ph.ps("p_tr")
        p_acc = [ph.ps("p_acc0"), ph.ps("p_acc1")]
        ada_w = g.ada_w.rearrange("l (k p) n -> p (l k) n", p=P)

        with nc.Block() as block:

            @block.sync
            def _(sp):
                sp.dma_start(g.ident[:, :], g.d_ident).then_inc(s.rows, 16)
                sp.dma_start(crow[0:KC, :], g.c.rearrange("a (k p) -> (a k) p", p=P)).then_inc(s.rows, 16)
                sp.dma_start(crow[KC:2 * KC, :], g.c_ctx.rearrange("(k p) -> k p", p=P)).then_inc(s.rows, 16)
                sp.dma_start(nrow[0:KC, :], g.norm1_g.rearrange("l (k p) -> (l k) p", p=P)).then_inc(s.rows, 16)
                sp.dma_start(nrow[KC:2 * KC, :], g.norm2_g.rearrange("l (k p) -> (l k) p", p=P)).then_inc(s.rows, 16)
                for r in range(2):
                    sp.dma_start(adab[r:r + 1, :], g.ada_b[:, 0:NCH * 512]).then_inc(s.rows, 16)
                for n in range(2):
                    sp.dma_start(aw[:, n], ada_w[:, :, n * 512:(n + 1) * 512]).then_inc(s.w[n], 16)
                with sp.Fori(1, NCH // 2) as i:
                    for par in range(2):
                        sp.wait_ge(s.acc, i * 2 + (par - 1))
                        sp.dma_start(aw[:, par], ada_w[:, :, bass.ds(i * 1024 + par * 512, 512)]).then_inc(s.w[par], 16)
                sp.wait_ge(s.bias, NCH)
                sp.dma_start(g.mod_d[:, 0:NCH * 512], mod[:, :]).then_inc(s.out, 16)
                sp.wait_ge(s.out, 16)
                load_shift_scale(sp, g, 0, modr, s.back)

            @block.scalar
            def _(act):
                act.wait_ge(s.rows, 16 * 7)
                act.activation(srow[:, :], crow[:, :], ACT.Silu).then_inc(s.silu, 1)

            @block.tensor
            def _(pe):
                pe.wait_ge(s.silu, 1)
                pe.transpose(p_tr[:, 0:2 * KC], srow[:, :], g.ident[0:2 * KC, 0:2 * KC])
                pe.transpose(p_tr[:, 2 * KC:4 * KC], nrow[:, :], g.ident[0:2 * KC, 0:2 * KC]).then_inc(s.tr, 1)
                pe.wait_ge(s.cT, 1)

                def chunk(n, half, par):
                    pe.wait_ge(s.w[par], (half + 1) * 16)
                    wait(pe, s.bias, n - 1)
                    for k in range(KC):
                        last = pe.matmul(p_acc[par][0:2, :], cT[:, k::KC], aw[:, par, k, :], start=k == 0, stop=k == KC - 1)
                    last.then_inc(s.acc, 1)

                chunk(0, 0, 0)
                chunk(1, 0, 1)
                with pe.Fori(1, NCH // 2) as i:
                    for par in range(2):
                        chunk(i * 2 + par, i, par)
                pe.wait_ge(s.back, 32)
                pe.transpose(p_tr[:, 64:64 + 4 * KC], modr[:, :], g.ident[0:4 * KC, 0:4 * KC]).then_inc(s.mtr, 1)

            @block.vector
            def _(dve):
                dve.memset(g.neg_half[:, :], -0.5)
                dve.wait_ge(s.tr, 1)
                dve.tensor_copy(nT[:, :], p_tr[:, 2 * KC:4 * KC])
                dve.tensor_copy(cT[:, :], p_tr[:, 0:2 * KC]).then_inc(s.cT, 1)
                with dve.Fori(0, NCH // 2) as i:
                    for par in range(2):
                        dve.wait_ge(s.acc, i * 2 + (par + 1))
                        cols = bass.ds(i * 1024 + par * 512, 512)
                        dve.tensor_tensor(mod[:, cols], p_acc[par][0:2, :], adab[:, cols], ALU.add).then_inc(s.bias, 1)
                dve.wait_ge(s.mtr, 1)
                norm_table(dve, g, 0, p_tr[:, 64:64 + 4 * KC], modT, s.mT, s.done)


def load_shift_scale(sp, g, n, rows, sem):
    for c in range(2):
        src = g.mod_d[c:c + 1, 3 * n * D_MODEL:(3 * n + 2) * D_MODEL].rearrange("c (j p) -> (c j) p", p=P)
        sp.dma_start(rows[c * 2 * KC:(c + 1) * 2 * KC, :], src).then_inc(sem, 16)


def norm_table(dve, g, n, p_rows, modT, copied, done):
    dve.tensor_copy(modT[:, :, :, :], p_rows.rearrange("p (c m k) -> p c m k", c=2, m=2)).then_inc(copied, 1)
    dve.wait_ge(copied, 1)
    for c in range(2):
        dve.scalar_tensor_tensor(g.lnp[:, n, c, 0, :], modT[:, c, 1, :], 1.0, g.nT[:, n * KC:(n + 1) * KC], ALU.add, ALU.mult)
        last = dve.tensor_copy(g.lnp[:, n, c, 1, :], modT[:, c, 0, :])
    last.then_inc(done, 1)
    dve.wait_ge(done, 1)


class Front:

    def __init__(self, ph, s, g, norm, used):
        self.s, self.g, self.norm, self.used = s, g, norm, used
        (s.x0, s.x1, s.sq, s.ms, s.rstd, s.xn, s.tr, s.hT, s.hi, s.split, s.kept0, s.kept1) = ph.semaphores(
            "x0 x1 sq ms rstd xn tr hT hi split kept0 kept1")
        self.x = ph.sb("x", [P, 2, D_MODEL])
        self.junk = ph.sb("junk", [P, D_MODEL])
        self.ss = ph.sb("ss", [P, 2, 1])
        self.ms = ph.sb("ms", [P, 2, 1])
        self.rstd = ph.sb("rstd", [P, 2, 1])
        self.hT = ph.sb("hT", [P, 2, KC, P])
        self.hi = ph.sb("hi", [P, 2, KC, P], F32R)
        self.lo = ph.sb("lo", [P, 2, KC, P], F32R)
        self.p_tr = ph.ps("p_tr", 1024)

    def load(self, sp, T):
        t, half, par = T
        wait(sp, self.s.tr, t - 1)
        src = self.g.x_tile(t)
        sp.dma_start(self.x[:, par, :], src).then_inc([self.s.x0, self.s.x1][par], 16)

    def squares(self, act, T):
        t, half, par = T
        act.wait_ge([self.s.x0, self.s.x1][par], (half + 1) * 16)
        wait(act, self.s.sq, t)
        act.activation(self.junk[:, :], self.x[:, par, :], ACT.Square, accum_out=self.ss[:, par, :]).then_inc(self.s.sq, 1)

    def normalise(self, dve, T):
        t, half, par = T
        dve.wait_ge(self.s.sq, t + 1)
        dve.tensor_scalar(self.ms[:, par, :], self.ss[:, par, :], 1.0 / D_MODEL, EPS, ALU.mult, ALU.add).then_inc(self.s.ms, 1)
        dve.wait_ge(self.s.rstd, t + 1)
        dve.tensor_scalar(self.x[:, par, :], self.x[:, par, :], self.rstd[:, par, :], None, ALU.mult).then_inc(self.s.xn, 1)

    def root(self, pool, T):
        t, half, par = T
        pool.wait_ge(self.s.ms, t + 1)
        pool.tensor_tensor(self.rstd[:, par, :], self.ms[:, par, :], self.g.neg_half[:, 0:1], ALU.pow).then_inc(self.s.rstd, 1)

    def transpose(self, pe, T):
        t, half, par = T
        pe.wait_ge(self.s.xn, t + 1)
        wait(pe, self.s.hT, t)
        for k in range(KC):
            last = pe.transpose(self.p_tr[:, k * P:(k + 1) * P], self.x[:, par, k * P:(k + 1) * P], self.g.ident[:, :])
        last.then_inc(self.s.tr, 1)

    def modulate(self, act, T):
        t, half, par = T
        act.wait_ge(self.s.tr, t + 1)
        wait(act, self.s.split, t - 1)
        if not (isinstance(t, int) and t < 2):
            act.wait_ge([self.s.kept0, self.s.kept1][par], half * 16)
        c = cond_of(t)
        for k in range(KC):
            last = act.activation(self.hT[:, par, k, :], self.p_tr[:, k * P:(k + 1) * P], ACT.Identity,
                                  bias=self.g.lnp[:, self.norm, c, 1, k:k + 1], scale=self.g.lnp[:, self.norm, c, 0, k:k + 1])
        last.then_inc(self.s.hT, 1)

    def keep(self, sp, T):
        t, half, par = T
        sp.wait_ge(self.s.hT, t + 1)
        sp.dma_start(self.g.hT_tile(t), self.hT[:, par].rearrange("p k q -> p (k q)")).then_inc([self.s.kept0, self.s.kept1][par], 16)

    def split(self, dve, T):
        t, half, par = T
        dve.wait_ge(self.s.hT, t + 1)
        wait(dve, self.used, t - 1)
        dve.tensor_copy(self.hi[:, par], self.hT[:, par]).then_inc(self.s.hi, 1)
        dve.wait_ge(self.s.hi, t + 1)
        dve.tensor_tensor(self.lo[:, par], self.hT[:, par], self.hi[:, par].bitcast(F32), ALU.subtract).then_inc(self.s.split, 1)


def load_split_weights(ph, s, w_dram, n_k, cols, w_hi, w_lo, stage):
    (s.w0, s.w1, s.w2, s.w3, s.w_hi, s.w_lo) = ph.semaphores("w0 w1 w2 w3 w_hi w_lo")
    arrived = [s.w0, s.w1, s.w2, s.w3]

    def sp_part(sp):
        for k in range(n_k):
            wait(sp, s.w_lo, k - W_STAGES + 1)
            sp.dma_start(stage[:, k % W_STAGES, 0:cols], w_dram[k * P:(k + 1) * P, :]).then_inc(arrived[k % W_STAGES], 16)

    def act_part(act):
        for k in range(n_k):
            act.wait_ge(arrived[k % W_STAGES], 16 * (k // W_STAGES + 1))
            act.activation(w_hi[:, k, :], stage[:, k % W_STAGES, 0:cols], ACT.Copy).then_inc(s.w_hi, 1)

    def dve_part(dve):
        for k in range(n_k):
            dve.wait_ge(s.w_hi, k + 1)
            dve.tensor_tensor(w_lo[:, k, :], stage[:, k % W_STAGES, 0:cols], w_hi[:, k, :].bitcast(F32), ALU.subtract).then_inc(s.w_lo, 1)

    return sp_part, act_part, dve_part


def split_product(pe, out, parts, first, last):
    (ah, al), (bh, bl) = parts
    pe.matmul(out, ah, bh, start=first, stop=False)
    pe.matmul(out, ah, bl, start=False, stop=False)
    return pe.matmul(out, al, bh, start=False, stop=last)


def constant_parts(dve, parts):
    dve.memset(parts[:, :, 3, 1:HD].bitcast(F32), 0.0)
    dve.memset(parts[:, :, 3, 0:1].bitcast(F32), -1.0)


def attention_projection(nc, g):
    NH = AH + KVH
    with ExitStack() as stack:
        ph = Phase(nc, stack, "qkv")
        s = ph.s
        (s.gain, s.gmul, s.rope0, s.rope1, s.mq, s.mkv, s.eq, s.ekv, s.psq, s.ssh, s.msh, s.rsh, s.cs, s.qn, s.m1, s.m2,
         s.rot, s.hq, s.lo_q, s.hk, s.lo_k, s.vhi, s.vlo, s.ptr, s.eptr, s.eptk, s.qout0, s.qout1, s.cache) = ph.semaphores(
            "gain gmul rope0 rope1 mq mkv eq ekv psq ssh msh rsh cs qn m1 m2 rot hq lo_q hk lo_k vhi vlo ptr eptr eptk qout0 qout1 cache")
        fr = Front(ph, s, g, 0, s.mkv)
        w_hi = ph.sb("w_hi", [P, KC, D_ATT], F32R)
        w_lo = ph.sb("w_lo", [P, KC, D_ATT], F32R)
        stage = ph.sb("stage", [P, W_STAGES, D_ATT])
        gsrc = ph.sb("gsrc", [P, 4, HD])
        gain = ph.sb("gain", [P, 2, NH, HD])
        rope = ph.sb("rope", [P, 2, 2, HD])
        qkv = ph.sb("qkv", [P, 2, D_ATT])
        psq = ph.sb("psq", [P, NH * HD])
        ssh = ph.sb("ssh", [P, NH])
        msh = ph.sb("msh", [P, NH])
        rsh = ph.sb("rsh", [P, NH])
        cs = ph.sb("cs", [P, 2, NH, HD])
        qn = ph.sb("qn", [P, NH, HD])
        m1 = ph.sb("m1", [P, NH, HD])
        m2 = ph.sb("m2", [P, NH, HD])
        rot = ph.sb("rot", [P, 2, NH, HD])
        qhl = ph.sb("qhl", [P, AH, 2, HD], F32R)
        khl = ph.sb("khl", [P, KVH, 4, HD], F32R)
        qT = ph.sb("qT", [P, 2, AH, P], F32R)
        p_q = [ph.ps("p_q0"), ph.ps("p_q1")]
        p_kv = ph.ps("p_kv")
        p_t = ph.ps("p_t", 1536)
        w_sp, w_act, w_dve = load_split_weights(ph, s, g.w_in[0, :, D_GLA:D_GLA + D_ATT], KC, D_ATT, w_hi, w_lo, stage)
        NQ = AH * HD

        def key_tile(t):
            return t + 2 if cond_of(t) else t

        with nc.Block() as block:

            @block.sync
            def _(sp):
                q_g, k_g = g.q_norm_g, g.k_norm_g
                half = HD // 4
                with nc.allow_non_contiguous_dma(reason="gains"):
                    for n, gg in enumerate((q_g, k_g)):
                        sp.dma_start(gsrc[:, 2 * n, :], gg.to_broadcast([P, HD])).then_inc(s.gain, 16)
                        for a in range(2):
                            for h in range(2):
                                src = gg[:, (2 * a + 1 - h) * half:(2 * a + 2 - h) * half].to_broadcast([P, half])
                                sp.dma_start(gsrc[:, 2 * n + 1, (2 * a + h) * half:(2 * a + h + 1) * half], src).then_inc(s.gain, 16)

                def step(U):
                    if T := U.at(5):
                        t, hf, par = T
                        sp.wait_ge(s.eptr, t + 1)
                        sp.dma_start(g.qT_tile(t), qT[:, par].rearrange("p h q -> p (h q)").bitcast(F32)).then_inc([s.qout0, s.qout1][par], 16)
                        if cond_of(t):
                            r = (t - N_LAT) * P
                            sp.dma_start(g.new_k[r:r + P, :], rot[:, par, AH:NH, :].rearrange("p h d -> p (h d)")).then_inc(s.cache, 16)
                            sp.dma_start(g.new_v[r:r + P, :], qkv[:, par, NH * HD:D_ATT]).then_inc(s.cache, 16)
                    if T := U.at(0):
                        fr.load(sp, T)
                    if T := U.at(2):
                        fr.keep(sp, T)
                    if T := U.at(2):
                        t, hf, par = T
                        wait(sp, s.cs, t - 1)
                        sp.dma_start(rope[:, par].rearrange("p a d -> p (a d)"), g.rope_tile(t)).then_inc([s.rope0, s.rope1][par], 16)
                    if U.first(1):
                        w_sp(sp)

                steps(sp, 5, step)
                sp.wait_ge(s.qout0, 16 * (NT // 2))
                sp.wait_ge(s.qout1, 16 * (NT // 2))
                sp.wait_ge(s.kept0, 16 * (NT // 2))
                sp.wait_ge(s.kept1, 16 * (NT // 2))
                sp.wait_ge(s.cache, 16 * 2 * N_CTX)

            @block.scalar
            def _(act):

                def step(U):
                    if T := U.at(3):
                        t, hf, par = T
                        act.wait_ge(s.mq, t + 1)
                        wait(act, s.vlo, t - 1)
                        act.activation(qkv[:, par, 0:NQ], p_q[par][:, :], ACT.Copy).then_inc(s.eq, 1)
                        act.wait_ge(s.mkv, t + 1)
                        act.activation(qkv[:, par, NQ:D_ATT], p_kv[:, 0:D_ATT - NQ], ACT.Copy).then_inc(s.ekv, 1)
                        act.wait_ge(s.ekv, t + 1)
                        act.wait_ge(s.eq, t + 1)
                        wait(act, s.ssh, t)
                        act.activation(psq[:, :], qkv[:, par, 0:NH * HD], ACT.Square).then_inc(s.psq, 1)
                    if T := U.at(4):
                        t, hf, par = T
                        act.wait_ge(s.ptr, t + 1)
                        if isinstance(t, int) and t < 2:
                            pass
                        else:
                            act.wait_ge([s.qout0, s.qout1][par], hf * 16)
                        act.activation(qT[:, par], p_t[:, 0:AH * P].rearrange("p (h q) -> p h q", h=AH), ACT.Copy).then_inc(s.eptr, 1)
                        kt = key_tile(t)
                        col = kt * P
                        act.activation(g.keysT[:, :, :, bass.ds(col, P)],
                                       p_t[:, AH * P:(AH + 4) * P].rearrange("p (g a q) -> p g a q", g=KVH, a=2), ACT.Copy).then_inc(s.eptk, 1)
                    if T := U.at(0):
                        fr.squares(act, T)
                    if T := U.at(1):
                        fr.modulate(act, T)
                    if U.first(1):
                        w_act(act)

                steps(act, 4, step)
                act.wait_ge(s.eptk, NT)

            @block.vector
            def _(dve):
                constant_parts(dve, khl)
                dve.wait_ge(s.gain, 16 * 10)
                for n in range(2):
                    dve.tensor_scalar(gain[:, n, 0:AH, :], bc(gsrc[:, n, :], 1, AH), HD ** -0.5, None, ALU.mult)
                    last = dve.tensor_copy(gain[:, n, AH:NH, :], bc(gsrc[:, 2 + n, :], 1, KVH))
                last.then_inc(s.gmul, 1)

                def step(U):
                    if T := U.at(3):
                        t, hf, par = T
                        dve.wait_ge(s.psq, t + 1)
                        dve.tensor_reduce(ssh[:, :], psq[:, :].rearrange("p (h d) -> p h d", d=HD), AX.X, ALU.add).then_inc(s.ssh, 1)
                        dve.wait_ge(s.ssh, t + 1)
                        dve.tensor_scalar(msh[:, :], ssh[:, :], 1.0 / HD, EPS, ALU.mult, ALU.add).then_inc(s.msh, 1)
                        vt = key_tile(t)
                        src = qkv[:, par, NH * HD:D_ATT].rearrange("p (g d) -> p g d", g=KVH)
                        dve.wait_ge(s.ekv, t + 1)
                        v_here = g.vals[:, bass.ds(vt * KVH, KVH), :]
                        dve.tensor_copy(v_here[:, :, 0:HD], src).then_inc(s.vhi, 1)
                        dve.wait_ge(s.rsh, t + 1)
                        dve.tensor_tensor(qn[:, :, :], qkv[:, par, 0:NH * HD].rearrange("p (h d) -> p h d", d=HD),
                                          bc(rsh[:, :], 2, HD), ALU.mult).then_inc(s.qn, 1)
                        dve.wait_ge(s.vhi, t + 1)
                        dve.tensor_tensor(v_here[:, :, HD:2 * HD], src, v_here[:, :, 0:HD].bitcast(F32), ALU.subtract).then_inc(s.vlo, 1)
                        dve.wait_ge(s.qn, t + 1)
                        dve.wait_ge(s.cs, t + 1)
                        dve.tensor_tensor(m1[:, :, :], qn[:, :, :], cs[:, 0], ALU.mult).then_inc(s.m1, 1)
                        dve.wait_ge(s.m1, t + 1)
                        dve.wait_ge(s.m2, t + 1)
                        dve.tensor_tensor(rot[:, par], m1[:, :, :], m2[:, :, :], ALU.add).then_inc(s.rot, 1)
                        dve.wait_ge(s.rot, t + 1)
                        wait(dve, s.ptr, t)
                        dve.tensor_copy(qhl[:, :, 0, :], rot[:, par, 0:AH, :]).then_inc(s.hq, 1)
                        dve.tensor_copy(khl[:, :, 0:2, :], bc(rot[:, par, AH:NH, :], 2, 2)).then_inc(s.hk, 1)
                        dve.wait_ge(s.hq, t + 1)
                        dve.tensor_tensor(qhl[:, :, 1, :], rot[:, par, 0:AH, :], qhl[:, :, 0, :].bitcast(F32), ALU.subtract).then_inc(s.lo_q, 1)
                        dve.wait_ge(s.hk, t + 1)
                        dve.tensor_tensor(khl[:, :, 2, :], rot[:, par, AH:NH, :], khl[:, :, 0, :].bitcast(F32), ALU.subtract).then_inc(s.lo_k, 1)
                    if T := U.at(0):
                        fr.normalise(dve, T)
                    if T := U.at(1):
                        fr.split(dve, T)
                    if U.first(1):
                        w_dve(dve)

                steps(dve, 4, step)

            @block.gpsimd
            def _(pool):
                pool.wait_ge(s.gmul, 1)

                def step(U):
                    if T := U.at(3):
                        t, hf, par = T
                        pool.wait_ge([s.rope0, s.rope1][par], (hf + 1) * 16)
                        wait(pool, s.m1, t)
                        wait(pool, s.m2, t)
                        pool.tensor_tensor(cs[:, 0], gain[:, 0], bc(rope[:, par, 0, :], 1, NH), ALU.mult)
                        pool.tensor_tensor(cs[:, 1], gain[:, 1], bc(rope[:, par, 1, :], 1, NH), ALU.mult).then_inc(s.cs, 1)
                        pool.wait_ge(s.msh, t + 1)
                        pool.tensor_tensor(rsh[:, :], msh[:, :], g.neg_half[:, 0:NH], ALU.pow).then_inc(s.rsh, 1)
                        pool.wait_ge(s.cs, t + 1)
                        pool.wait_ge(s.qn, t + 1)
                        wait(pool, s.rot, t)
                        v5 = [x.rearrange("p h (a e d) -> p (h a) e d", a=2, e=2) for x in (m2[:, :, :], qn[:, :, :], cs[:, 1])]
                        for e in range(2):
                            last = pool.tensor_tensor(v5[0][:, :, e, :], v5[1][:, :, 1 - e, :], v5[2][:, :, e, :], ALU.mult)
                        last.then_inc(s.m2, 1)
                    if T := U.at(0):
                        fr.root(pool, T)

                steps(pool, 4, step)

            @block.tensor
            def _(pe):
                def step(U):
                    if T := U.at(4):
                        t, hf, par = T
                        pe.wait_ge(s.lo_q, t + 1)
                        pe.wait_ge(s.lo_k, t + 1)
                        wait(pe, s.eptr, t)
                        wait(pe, s.eptk, t)
                        for h in range(AH):
                            pe.transpose(p_t[:, h * P:(h + 1) * P], qhl[:, h].rearrange("p a d -> p (a d)").bitcast(F32), g.ident[:, :])
                        for n in range(4):
                            last = pe.transpose(p_t[:, (AH + n) * P:(AH + n + 1) * P],
                                                khl[:, n // 2, 2 * (n % 2):2 * (n % 2) + 2, :].rearrange("p a d -> p (a d)").bitcast(F32),
                                                g.ident[:, :])
                        last.then_inc(s.ptr, 1)
                    if T := U.at(1):
                        fr.transpose(pe, T)
                    if T := U.at(2):
                        t, hf, par = T
                        pe.wait_ge(s.split, t + 1)
                        wait(pe, s.eq, t - 1)
                        for k in range(KC):
                            if isinstance(t, int) and t == 0:
                                pe.wait_ge(s.w_lo, k + 1)
                            last = split_product(pe, p_q[par][:, :], ((fr.hi[:, par, k], fr.lo[:, par, k]),
                                                 (w_hi[:, k, 0:NQ], w_lo[:, k, 0:NQ])), k == 0, k == KC - 1)
                        last.then_inc(s.mq, 1)
                        wait(pe, s.ekv, t)
                        for k in range(KC):
                            last = split_product(pe, p_kv[:, 0:D_ATT - NQ], ((fr.hi[:, par, k], fr.lo[:, par, k]),
                                                 (w_hi[:, k, NQ:D_ATT], w_lo[:, k, NQ:D_ATT])), k == 0, k == KC - 1)
                        last.then_inc(s.mkv, 1)

                steps(pe, 4, step)


def attention(nc, g):
    G4 = AH // KVH
    NKT = (T_LAT + PAST) // P
    NKC = T_CTX // P
    NS = NKT // 2
    ROW = 4 * P
    SLOTS_P = 6
    Q_SLOTS = 4
    FULL = T_LAT // ROW
    N_PIECES = G4 * FULL + G4 // 2
    PLAN = [2, 2, 2, 3, 2, 3, 2, 2, 0]
    CHUNKS = N_MOD * D_MODEL // 512 - MOD_FIRST
    HALF = 256
    CHUNK_STEP = 4
    L_UNITS = 2 * N_LAT
    U_UNITS = 2 * NT
    with ExitStack() as stack:
        ph = Phase(nc, stack, "att")
        s = ph.s
        (s.zero, s.ck, s.cv, s.ckh, s.ckl, s.ctr, s.cte, s.q0, s.q1, s.q2, s.q3, s.piece, s.mx, s.nm, s.turn, s.aux, s.st, s.ex, s.hi, s.lo,
         s.pv, s.acc, s.ls, s.rec, s.lb, s.tsums, s.osb, s.osum, s.oo, s.out0, s.out1, s.aw, s.adab, s.chunk, s.mod, s.mout) = ph.semaphores(
            "zero ck cv ckh ckl ctr cte q0 q1 q2 q3 piece mx nm turn aux st ex hi lo pv acc ls rec lb tsums osb osum oo out0 out1 aw adab chunk mod mout")
        s.q, s.out = [s.q0, s.q1, s.q2, s.q3], [s.out0, s.out1]
        ckr = ph.sb("ckr", [P, 2, KVH, HD])
        cvr = ph.sb("cvr", [P, 2, KVH, HD])
        ckp = ph.sb("ckp", [P, 2, KVH, 4, HD], F32R)
        qa = ph.sb("qa", [P, Q_SLOTS, ROW], F32R)
        qb = ph.sb("qb", [P, Q_SLOTS, ROW], F32R)
        mx = ph.sb("mx", [P, 2, G4, FULL + 1])
        wm = ph.sb("wm", [P, 2, G4, P], F32R)
        prob = ph.sb("prob", [P, SLOTS_P, 2 * ROW])
        thi = ph.sb("thi", [P, SLOTS_P, 2 * ROW], F32R)
        tlo = ph.sb("tlo", [P, SLOTS_P, 2 * ROW], F32R)
        acc = ph.sb("acc", [P, 2, 2 * ROW])
        acc_ctx = ph.sb("acc_ctx", [P, KVH * N_CTX, ROW])
        ones = ph.sb("ones", [P, G4])
        osb = ph.sb("osb", [HD, ROW])
        rec = ph.sb("rec", [P, G4])
        lb = ph.sb("lb", [P, G4, HD])
        osum = ph.sb("osum", [P, 2, P])
        oo = ph.sb("oo", [P, 2, 2 * P])
        aw = ph.sb("aw", [P, KC, 512])
        adab = ph.sb("adab", [2, 512])
        mod = ph.sb("mod", [2, 512])
        ada_w = g.ada_w.rearrange("l (k p) n -> p (l k) n", p=P)
        p_s = [ph.ps("p_s0", 2 * ROW), ph.ps("p_s1", 2 * ROW)]
        p_r = [ph.ps("p_r0"), ph.ps("p_r1")]
        p_o = [ph.ps("p_o0"), ph.ps("p_o1")]

        def unit(n, qt, kv, q, q_round):
            u = Names()
            u.n, u.qt, u.kv, u.q, u.q_round = n, qt, kv, q, q_round
            if isinstance(n, int) and n >= L_UNITS:
                m = n - L_UNITS
                u.nds, u.kt0, u.pieces = NKC // 2, NKT, G4 // 2
                u.g0, u.p0, u.a0 = L_UNITS * NS + m, L_UNITS * N_PIECES + m * u.pieces, L_UNITS * (NS - 1) + m
                u.step_no, u.sums, u.adds = [L_UNITS * NS + m], acc_ctx[:, m, :], 1
            else:
                u.nds, u.kt0, u.pieces = NS, 0, N_PIECES
                u.g0, u.p0, u.a0 = n * NS, n * N_PIECES, n * (NS - 1)
                u.sums, u.adds = acc[:, kv, :], NS - 1
                u.step_no = [kv * NS + j for j in range(NS)]
            return u

        def of(n):
            return unit(n, n // 2, n % 2, n % Q_SLOTS, n // Q_SLOTS)

        def turn_unit(i, m):
            return unit(i * 4 + (2 + m), i * 2 + (1 + m // 2), m % 2, (2 + m) % Q_SLOTS, i + (2 + m) // Q_SLOTS)

        class Walk:

            def __init__(self, e=None, b=None, chunk=None):
                self.chunk = chunk
                self.index, self.fin, self.out, self.store, self.done, self.ring = 1, None, None, None, [None, None, None], [None, None]
                if e is not None:
                    self.index, self.done = 0, [(b, NS - 3), (b, NS - 2), (b, NS - 1)]
                    self.ring = [(s.mx, e.p0 + N_PIECES), (s.aux, e.n + 1)]

            def item(self, sem, count):
                bank, before = self.index % 2, self.ring[0]
                self.index += 1
                self.ring = [self.ring[1], (sem, count)]
                return p_r[bank], before

            def pieces(self, v, i0, n):
                return [(v, i, self.item(s.mx, v.p0 + (i + 1))) for i in range(i0, i0 + n)]

            def step(self, e, j, v, i0, n, turn, load=None):
                S = Names()
                S.now = (e, j) if e is not None else None
                S.load, S.chunk, S.after = load, None, None
                S.low, S.val, S.fin = self.done[1], self.done[0], None
                S.early = self.pieces(v, i0, n) if n and (e is None or e.nds == 1) else []
                S.turn = (v, self.item(s.aux, v.n + 1)) if turn else None
                S.turn_sums = (self.out, self.item(s.oo, self.out.n + 1)) if self.out is not None else None
                if self.fin is not None:
                    S.fin = (self.fin, self.item(s.rec, self.fin.n + 1))
                S.max = self.pieces(v, i0, n) if n and not S.early else []
                S.store = self.store
                self.store, self.out = self.out, self.fin
                self.fin = S.val[0] if S.val is not None and S.val[1] == S.val[0].nds - 1 else None
                self.done = [self.done[1], self.done[2], S.now]
                return S

            def unit_steps(self, e, v, w=None, chunk=None):
                i0 = 0
                for j in range(e.nds):
                    n = 0
                    if v is not None:
                        n = min(PLAN[j], v.pieces - i0) if e.nds > 1 else v.pieces
                    S = self.step(e, j, v, i0, n, v is not None and j == e.nds - 1, w if j == 0 else None)
                    S.chunk, S.after = chunk, self.chunk if j == 3 else None
                    if j == 3:
                        self.chunk = None
                    yield S
                    i0 += n
                if chunk is not None:
                    self.chunk = chunk

        def schedule(eng, step):
            w = Walk()
            step(w.step(None, 0, of(0), 0, N_PIECES, True, of(0)))
            step(w.step(None, 0, None, 0, 0, False, of(1)))
            for n in range(2):
                for S in w.unit_steps(of(n), of(n + 1), of(n + 2), (0, n)):
                    step(S)
            with eng.Fori(0, (N_LAT - 2) // 2) as i:
                w = Walk(turn_unit(i, 0), turn_unit(i, -1), (i, 1))
                for m in range(4):
                    for S in w.unit_steps(turn_unit(i, m), turn_unit(i, m + 1), turn_unit(i, m + 2), (i + 1, m // 2) if m % 2 else None):
                        step(S)
            w = Walk(of(L_UNITS - 2), of(L_UNITS - 3), (CHUNKS - 1, 1))
            for n in range(L_UNITS - 2, U_UNITS):
                for S in w.unit_steps(of(n), *(of(m) if m < U_UNITS else None for m in (n + 1, n + 2))):
                    step(S)
            for _ in range(6):
                step(w.step(None, 0, None, 0, 0, False))

        with nc.Block() as block:

            @block.sync
            def _(sp):
                for t in range(2):
                    sp.dma_start(ckr[:, t].rearrange("p g d -> p (g d)"), g.cache_k[t * P:(t + 1) * P, :]).then_inc(s.ck, 16)
                    sp.dma_start(cvr[:, t].rearrange("p g d -> p (g d)"), g.cache_v[t * P:(t + 1) * P, :]).then_inc(s.cv, 16)

                def load(v):
                    src = g.qT_tile(v.qt)[:, v.kv * ROW:(v.kv + 1) * ROW]
                    sp.dma_start(qa[:, v.q, :].bitcast(F32), src).then_inc(s.q[v.q], 16)
                    sp.dma_start(qb[0:HD, v.q, :].bitcast(F32), src[0:HD, :]).then_inc(s.q[v.q], 16)

                def load_chunk(c):
                    cols = bass.ds(c * 512 + MOD_FIRST * 512, 512)
                    sp.dma_start(aw[:, :, :], ada_w[:, :, cols]).then_inc(s.aw, 16)
                    for r in range(2):
                        sp.dma_start(adab[r:r + 1, :], g.ada_b[:, cols]).then_inc(s.adab, 16)

                load_chunk(0)

                def step(S):
                    if S.load is not None:
                        n = S.load.n
                        wait(sp, s.st, of(n - Q_SLOTS + 1).g0 if isinstance(n, int) and n >= Q_SLOTS else (n - Q_SLOTS + 1) * NS)
                        load(S.load)
                    if S.after is not None and S.after[1] == 1:
                        c = S.after[0]
                        sp.wait_ge(s.mod, c * 2 + 2)
                        sp.dma_start(g.mod_d[:, bass.ds(c * 512 + MOD_FIRST * 512, 512)], mod[:, :]).then_inc(s.mout, 16)
                        if not (isinstance(c, int) and c == CHUNKS - 1):
                            sp.wait_ge(s.mout, c * 16 + 16)
                            load_chunk(c + 1)

                schedule(sp, step)
                sp.wait_ge(s.mout, 16 * CHUNKS)

            @block.gpsimd
            def _(pool):
                def step(S):
                    if S.now:
                        e, j = S.now
                        sl = e.step_no[j] % SLOTS_P
                        pool.wait_ge(s.ex, e.g0 + (j + 1))
                        if e.nds == 1:
                            pool.tensor_tensor(e.sums, prob[:, sl, 0:ROW], prob[:, sl, ROW:2 * ROW], ALU.add).then_inc(s.acc, 1)
                        elif j == 1:
                            wait(pool, s.ls, e.n - 1)
                            pool.tensor_tensor(e.sums, prob[:, e.step_no[0] % SLOTS_P, :], prob[:, sl, :], ALU.add).then_inc(s.acc, 1)
                        elif j > 1:
                            pool.wait_ge(s.acc, e.a0 + (j - 1))
                            pool.tensor_tensor(e.sums, e.sums, prob[:, sl, :], ALU.add).then_inc(s.acc, 1)

                schedule(pool, step)

            @block.tensor
            def _(pe):
                pe.wait_ge(s.ckl, 1)
                for t in range(2):
                    for n in range(4):
                        last = pe.transpose(p_s[0][:, (t * 4 + n) * P:(t * 4 + n + 1) * P],
                                            ckp[:, t, n // 2, 2 * (n % 2):2 * (n % 2) + 2, :].rearrange("p a d -> p (a d)").bitcast(F32),
                                            g.ident[:, :])
                last.then_inc(s.ctr, 1)
                pe.wait_ge(s.cte, 2)

                def piece(v, i, item):
                    bank, before = item
                    if i == 0:
                        pe.wait_ge(s.q[v.q], v.q_round * 32 + 32)
                    if before:
                        pe.wait_ge(*before)
                    if v.nds > 1 and i < G4 * FULL:
                        h, c = i // FULL, i % FULL
                        pe.matmul(bank[:, :], qa[:, v.q, h * P:(h + 1) * P], g.keysT[:, v.kv, 0, c * ROW:(c + 1) * ROW],
                                  start=True, stop=True).then_inc(s.piece, 1)
                    else:
                        h0 = 2 * (i - G4 * FULL if v.nds > 1 else i)
                        k0 = (v.kt0 + 2 * (v.nds - 1)) * P
                        for n in range(2):
                            last = pe.matmul(bank[:, n * 2 * P:(n + 1) * 2 * P], qa[:, v.q, (h0 + n) * P:(h0 + n + 1) * P],
                                             g.keysT[:, v.kv, 0, k0:k0 + 2 * P], start=True, stop=True)
                        last.then_inc(s.piece, 1)

                def turn(v, item):
                    bank, before = item
                    pe.wait_ge(s.nm, v.n + 1)
                    pe.wait_ge(*before)
                    for h in range(G4):
                        last = pe.transpose(bank[:, h * P:(h + 1) * P], wm[:, v.kv, h, :].bitcast(F32), g.ident[:, :])
                    last.then_inc(s.turn, 1)

                def step(S):
                    for v, i, item in S.early:
                        piece(v, i, item)
                    late = S.now and S.now[0].nds > 1
                    if S.turn and not late:
                        turn(*S.turn)
                    pieces = list(S.max)
                    if late and S.now[1] == 0:
                        while pieces:
                            piece(*pieces.pop(0))
                    if S.now:
                        e, j = S.now
                        if j == 0:
                            pe.wait_ge(s.aux, e.n + 1)
                            pe.wait_ge(s.q[e.q], e.q_round * 32 + 32)
                        wait(pe, s.ex, e.g0 + (j - 1))
                        bank = p_s[e.step_no[j] % 2]
                        for i in range(2):
                            kt = slice((e.kt0 + 2 * j + i) * P, (e.kt0 + 2 * j + i + 1) * P)
                            pe.matmul(bank[:, i * ROW:(i + 1) * ROW], g.keysT[:, e.kv, 0, kt], qa[:, e.q, :], start=True, stop=False)
                            last = pe.matmul(bank[:, i * ROW:(i + 1) * ROW], g.keysT[:, e.kv, 1, kt], qb[:, e.q, :], start=False, stop=True)
                        last.then_inc(s.st, 1)
                    if S.turn_sums:
                        b, (bank, before) = S.turn_sums
                        pe.wait_ge(s.lb, b.n + 1)
                        pe.wait_ge(*before)
                        for n in range(2):
                            last = pe.transpose(bank[:, n * P:(n + 1) * P], lb[:, 2 * n:2 * n + 2, :].rearrange("p h d -> p (h d)"), g.ident[:, :])
                        last.then_inc(s.tsums, 1)
                    if S.fin:
                        b, (bank, before) = S.fin
                        pe.wait_ge(s.acc, b.a0 + b.adds)
                        pe.wait_ge(*before)
                        for h in range(G4):
                            sums = [b.sums[:, o + h * P:o + (h + 1) * P] for o in ((0, ROW) if b.nds > 1 else (0,))]
                            for o, keys in enumerate(sums):
                                last = pe.matmul(bank[:, h:h + 1], keys, ones[:, 0:1], start=o == 0, stop=o == len(sums) - 1)
                        last.then_inc(s.ls, 1)
                    if pieces:
                        piece(*pieces.pop(0))
                    if S.val:
                        b, j = S.val
                        pe.wait_ge(s.lo, b.g0 + (j + 1))
                        if j == 0:
                            wait(pe, s.osum, b.n - 1)
                            if S.after is not None:
                                pe.wait_ge(s.mod, S.after[0] * 2 + (S.after[1] + 1))
                        sl = b.step_no[j] % SLOTS_P
                        for i in range(2):
                            v = g.vals[:, (b.kt0 + 2 * j + i) * KVH + b.kv, :]
                            cols = slice(i * ROW, (i + 1) * ROW)
                            pe.matmul(p_o[b.kv][:, :], v, thi[:, sl, cols], start=j == 0 and i == 0, stop=False)
                            last = pe.matmul(p_o[b.kv][:, :], v, tlo[:, sl, cols], start=False, stop=j == b.nds - 1 and i == 1)
                            if i == 1:
                                last.then_inc(s.pv, 1)
                            if pieces:
                                piece(*pieces.pop(0))
                    for p in pieces:
                        piece(*p)
                    if S.turn and late:
                        turn(*S.turn)
                    if S.chunk is not None and CHUNK_STEP <= S.now[1] < CHUNK_STEP + KC // 2:
                        (e, j), (c, half) = S.now, S.chunk
                        if j == CHUNK_STEP:
                            wait(pe, s.osum, e.n)
                            pe.wait_ge(s.aw, c * 16 + 16)
                        for k in range(2 * (j - CHUNK_STEP), 2 * (j - CHUNK_STEP) + 2):
                            last = pe.matmul(p_o[1 - e.kv][0:2, 0:HALF], g.cT[:, k::KC], aw[:, k, half * HALF:(half + 1) * HALF], start=k == 0, stop=k == KC - 1)
                        if j == CHUNK_STEP + KC // 2 - 1:
                            last.then_inc(s.chunk, 1)

                schedule(pe, step)

            @block.scalar
            def _(act):
                act.wait_ge(s.ctr, 1)
                for t in range(2):
                    act.activation(g.keysT[:, :, :, (N_LAT + t) * P:(N_LAT + t + 1) * P],
                                   p_s[0][:, t * 512:(t + 1) * 512].rearrange("p (g a q) -> p g a q", g=KVH, a=2), ACT.Copy).then_inc(s.cte, 1)

                def turn(v, item):
                    bank = item[0]
                    act.wait_ge(s.turn, v.n + 1)
                    wait(act, s.st, v.g0 - (NS if v.nds > 1 else 1))
                    act.activation(qb[HD:P, v.q, :], bank[HD:P, :], ACT.Copy).then_inc(s.aux, 1)

                def step(S):
                    late = S.now and S.now[0].nds > 1
                    if S.turn and not late:
                        turn(*S.turn)
                    if S.fin:
                        b = S.fin[0]
                        act.wait_ge(s.pv, b.g0 + b.nds)
                        wait(act, s.osum, b.n)
                        act.activation(osb[:, :], p_o[b.kv][HD:P, :], ACT.Copy).then_inc(s.osb, 1)
                    if S.store:
                        b = S.store
                        act.wait_ge(s.oo, b.n + 1)
                        act.dma_start(g.mix_tile(b.qt)[:, (4 + 2 * b.kv) * P:(6 + 2 * b.kv) * P], oo[:, b.kv, :]).then_inc(s.out[b.kv], 16)
                    if S.now:
                        e, j = S.now
                        sl = e.step_no[j] % SLOTS_P
                        act.wait_ge(s.st, e.g0 + (j + 1))
                        wait(act, s.lo, e.g0 + (j - SLOTS_P + 1))
                        if j >= SLOTS_P:
                            act.wait_ge(s.acc, e.a0 + max(j - SLOTS_P, 1))
                        elif e.nds > 1:
                            wait(act, s.acc, e.a0 + (j - SLOTS_P + 1))
                        else:
                            act.wait_ge(s.acc, e.a0)
                        act.activation(prob[:, sl, :], p_s[e.step_no[j] % 2][:, :], ACT.Exp).then_inc(s.ex, 1)
                        if S.turn and late:
                            turn(*S.turn)
                        act.wait_ge(s.ex, e.g0 + (j + 1))
                        wait(act, s.pv, e.g0 + (j - SLOTS_P + 1))
                        act.activation(thi[:, sl, :], prob[:, sl, :], ACT.Copy).then_inc(s.hi, 1)
                    if S.fin:
                        b = S.fin[0]
                        act.wait_ge(s.rec, b.n + 1)
                        wait(act, s.tsums, b.n)
                        act.activation(lb[:, :, :], bc(rec[:, :], 2, HD), ACT.Copy).then_inc(s.lb, 1)

                schedule(act, step)
                for kv in range(KVH):
                    act.wait_ge(s.out[kv], 16 * NT)

            @block.vector
            def _(dve):
                dve.memset(ones[:, :], 1.0)
                dve.memset(wm[:, :, :, :].bitcast(F32), 0.0).then_inc(s.zero, 1)
                for t in range(2):
                    constant_parts(dve, ckp[:, t])
                dve.wait_ge(s.cv, 32)
                for t in range(2):
                    v_here = g.vals[:, (N_LAT + t) * KVH:(N_LAT + t + 1) * KVH, :]
                    dve.tensor_copy(v_here[:, :, 0:HD], cvr[:, t]).then_inc(s.ckh, 1)
                dve.wait_ge(s.ck, 32)
                for t in range(2):
                    dve.tensor_copy(ckp[:, t, :, 0:2, :], bc(ckr[:, t], 2, 2)).then_inc(s.ckh, 1)
                dve.wait_ge(s.ckh, 4)
                for t in range(2):
                    v_here = g.vals[:, (N_LAT + t) * KVH:(N_LAT + t + 1) * KVH, :]
                    dve.tensor_tensor(v_here[:, :, HD:2 * HD], cvr[:, t], v_here[:, :, 0:HD].bitcast(F32), ALU.subtract)
                    last = dve.tensor_tensor(ckp[:, t, :, 2, :], ckr[:, t], ckp[:, t, :, 0, :].bitcast(F32), ALU.subtract)
                last.then_inc(s.ckl, 1)
                dve.wait_ge(s.zero, 1)

                def piece(v, i, item):
                    bank = item[0]
                    if i == 0:
                        wait(dve, s.nm, v.n - 1)
                    dve.wait_ge(s.piece, v.p0 + (i + 1))
                    if v.nds > 1 and i < G4 * FULL:
                        h, c = i // FULL, i % FULL
                        dve.tensor_reduce(mx[:, v.kv, h, c:c + 1], bank[:, :], AX.X, ALU.max).then_inc(s.mx, 1)
                    else:
                        h0 = 2 * (i - G4 * FULL if v.nds > 1 else i)
                        dve.tensor_reduce(mx[:, v.kv, h0:h0 + 2, FULL], bank[:, :].rearrange("p (h k) -> p h k", h=2), AX.X, ALU.max).then_inc(s.mx, 1)
                    if i == v.pieces - 1:
                        dve.wait_ge(s.mx, v.p0 + v.pieces)
                        wait(dve, s.turn, v.n - 1)
                        parts = mx[:, v.kv, :, :] if v.nds > 1 else mx[:, v.kv, :, FULL:FULL + 1]
                        dve.tensor_reduce(wm[:, v.kv, :, HD], parts, AX.X, ALU.max).then_inc(s.nm, 1)

                def step(S):
                    for p in S.early:
                        piece(*p)
                    if S.low:
                        b, j = S.low
                        sl = b.step_no[j] % SLOTS_P
                        dve.wait_ge(s.hi, b.g0 + (j + 1))
                        dve.tensor_tensor(tlo[:, sl, :], prob[:, sl, :], thi[:, sl, :].bitcast(F32), ALU.subtract).then_inc(s.lo, 1)
                    if S.turn_sums:
                        b, (bank, _) = S.turn_sums
                        dve.wait_ge(s.osum, b.n + 1)
                        dve.wait_ge(s.tsums, b.n + 1)
                        if not (isinstance(b.qt, int) and b.qt == 0):
                            dve.wait_ge(s.out[b.kv], b.qt * 16)
                        dve.tensor_tensor(oo[:, b.kv, :], osum[:, :, :].rearrange("p n q -> p (n q)"), bank[:, 0:2 * P], ALU.mult).then_inc(s.oo, 1)
                    if S.fin:
                        b, (bank, _) = S.fin
                        dve.wait_ge(s.osb, b.n + 1)
                        wait(dve, s.oo, b.n)
                        ov = p_o[b.kv][0:HD, :].rearrange("p (n e q) -> p n e q", e=2, q=P)
                        sv = osb[:, :].rearrange("p (n e q) -> p n e q", e=2, q=P)
                        for e in range(2):
                            last = dve.tensor_tensor(osum[e * HD:(e + 1) * HD, :, :], ov[:, :, e, :], sv[:, :, e, :], ALU.add)
                        last.then_inc(s.osum, 1)
                        dve.wait_ge(s.ls, b.n + 1)
                        wait(dve, s.lb, b.n)
                        dve.reciprocal(rec[:, :], bank[:, 0:G4]).then_inc(s.rec, 1)
                    for p in S.max:
                        piece(*p)
                    if S.chunk is not None and S.now[1] == CHUNK_STEP + KC // 2:
                        e, (c, half) = S.now[0], S.chunk
                        cols = slice(half * HALF, (half + 1) * HALF)
                        dve.wait_ge(s.chunk, c * 2 + (half + 1))
                        dve.wait_ge(s.adab, c * 32 + 32)
                        dve.tensor_tensor(mod[:, cols], p_o[1 - e.kv][0:2, 0:HALF], adab[:, cols], ALU.add).then_inc(s.mod, 1)

                schedule(dve, step)


def gla_projection(nc, g):
    NB = 4
    BW = D_GLA // NB
    with ExitStack() as stack:
        ph = Phase(nc, stack, "gp")
        s = ph.s
        (s.b0, s.b1, s.b2, s.b3, s.e0, s.e1, s.e2, s.e3, s.o0, s.o1, s.h0, s.h1, s.hi, s.split) = ph.semaphores(
            "b0 b1 b2 b3 e0 e1 e2 e3 o0 o1 h0 h1 hi split")
        b, e, o = [s.b0, s.b1, s.b2, s.b3], [s.e0, s.e1, s.e2, s.e3], [s.o0, s.o1]
        h = ph.sb("h", [P, 2, KC, P])
        hi = ph.sb("hi", [P, 2, KC, P], F32R)
        lo = ph.sb("lo", [P, 2, KC, P], F32R)
        w_hi = ph.sb("w_hi", [P, KC, D_GLA], F32R)
        w_lo = ph.sb("w_lo", [P, KC, D_GLA], F32R)
        stage = ph.sb("stage", [P, W_STAGES, D_GLA])
        out = ph.sb("out", [P, 2, D_GLA])
        p_b = [ph.ps(f"p_b{j}") for j in range(NB)]
        w_sp, w_act, w_dve = load_split_weights(ph, s, g.w_in[0, :, 0:D_GLA], KC, D_GLA, w_hi, w_lo, stage)

        def evacuate(eng, copy, T, banks):
            t, hf, par = T
            for j in banks:
                eng.wait_ge(b[j], t + 1)
                if not (isinstance(t, int) and t < 2):
                    eng.wait_ge(o[par], hf * 16)
                copy(out[:, par, j * BW:(j + 1) * BW], p_b[j][:, 0:BW]).then_inc(e[j], 1)

        with nc.Block() as block:

            @block.sync
            def _(sp):

                def step(U):
                    if T := U.at(2):
                        t, hf, par = T
                        for j in range(NB):
                            sp.wait_ge(e[j], t + 1)
                        sp.dma_start(g.proj_tile(t), out[:, par, :]).then_inc(o[par], 16)
                    if T := U.at(0):
                        t, hf, par = T
                        wait(sp, s.split, t - 1)
                        sp.dma_start(h[:, par].rearrange("p k q -> p (k q)"), g.hT_tile(t)).then_inc([s.h0, s.h1][par], 16)
                    if U.first(0):
                        w_sp(sp)

                steps(sp, 2, step)
                for par in range(2):
                    sp.wait_ge(o[par], 16 * (NT // 2))

            @block.scalar
            def _(act):

                def step(U):
                    if T := U.at(0):
                        t, hf, par = T
                        act.wait_ge([s.h0, s.h1][par], (hf + 1) * 16)
                        wait(act, b[NB - 1], t - 1)
                        act.activation(hi[:, par], h[:, par], ACT.Copy).then_inc(s.hi, 1)
                    if T := U.at(1):
                        evacuate(act, lambda a, c: act.activation(a, c, ACT.Copy), T, (0, 2))
                    if U.first(0):
                        w_act(act)

                steps(act, 2, step)

            @block.vector
            def _(dve):

                def step(U):
                    if T := U.at(0):
                        t, hf, par = T
                        dve.wait_ge(s.hi, t + 1)
                        dve.tensor_tensor(lo[:, par], h[:, par], hi[:, par].bitcast(F32), ALU.subtract).then_inc(s.split, 1)
                    if T := U.at(1):
                        evacuate(dve, dve.tensor_copy, T, (1, 3))
                    if U.first(0):
                        w_dve(dve)

                steps(dve, 2, step)

            @block.tensor
            def _(pe):
                def step(U):
                    if T := U.at(1):
                        t, hf, par = T
                        pe.wait_ge(s.split, t + 1)
                        for j in range(NB):
                            wait(pe, e[j], t)
                            for k in range(KC):
                                if isinstance(t, int) and t == 0 and j == 0:
                                    pe.wait_ge(s.w_lo, k + 1)
                                last = split_product(pe, p_b[j][:, 0:BW], ((hi[:, par, k], lo[:, par, k]),
                                                     (w_hi[:, k, j * BW:(j + 1) * BW], w_lo[:, k, j * BW:(j + 1) * BW])),
                                                     k == 0, k == KC - 1)
                            last.then_inc(b[j], 1)

                steps(pe, 2, step)


def slot_of(chunk, ctx):
    return LAT_SLOTS + 1 + chunk if ctx else chunk + 1


def gla_states(nc, g):
    NG = 2 * GH * DK
    with ExitStack() as stack:
        ph = Phase(nc, stack, "gs")
        s = ph.s
        (s.const, s.wgz, s.lr0, s.lr1, s.in0, s.in1, s.v0, s.v1, s.lrp, s.lrT, s.gk, s.ab, s.ex1, s.ln, s.mn, s.gate, s.cum, s.dec,
         s.e1, s.e2, s.e3, s.edec, s.qs, s.qt, s.kt, s.ke, s.tq, s.tk, s.u, s.etq, s.etk, s.scan, s.ub, s.out0, s.out1,
         s.init, s.z, s.fin) = ph.semaphores(
            "const wgz lr0 lr1 in0 in1 v0 v1 lrp lrT gk ab ex1 ln mn gate cum dec e1 e2 e3 edec qs qt kt ke tq tk u etq etk scan ub out0 out1 init z fin")
        s.low, s.inp, s.vin, s.out = [s.lr0, s.lr1], [s.in0, s.in1], [s.v0, s.v1], [s.out0, s.out1]
        tri = ph.sb("tri", [P, 4, P])
        ind = ph.sb("ind", [P, 2])
        wg = ph.sb("wg", [2 * LR + 1, GH, 2, DK])
        lrT = ph.sb("lrT", [2 * LR + 1, P])
        qk = ph.sb("qk", [P, 2, 2 * GH * DK])
        lr = ph.sb("lr", [P, 2, 2 * LR])
        vin = ph.sb("vin", [P, 2, GH * DV])
        ab = ph.sb("ab", [P, NG])
        mn = ph.sb("mn", [P, NG])
        gate = ph.sb("gate", [P, 2, GH, 2, DK])
        e1 = ph.sb("e1", [P, GH, 2, DK])
        e2 = ph.sb("e2", [P, GH, 2, DK])
        e3 = ph.sb("e3", [P, GH, 2, DK])
        qs = ph.sb("qs", [P, GH, DK])
        qt = ph.sb("qt", [P, GH, 2, DK])
        kt = ph.sb("kt", [P, GH, 2, DK])
        ke = ph.sb("ke", [P, GH, 2, DK])
        qkT = ph.sb("qkT", [P, 2, GH, 2, P])
        p_a = ph.ps("p_a")
        p_g = ph.ps("p_g")
        p_inc = ph.ps("p_inc")
        p_exc = ph.ps("p_exc")
        p_q = ph.ps("p_q")
        p_k = ph.ps("p_k")
        p_u = [ph.ps("p_u0"), ph.ps("p_u1")]
        V0 = 2 * GH * DK
        LR0 = D_GLA - 2 * LR

        with nc.Block() as block:

            @block.sync
            def _(sp):
                sp.dma_start(tri[:, :, :], g.d_tri).then_inc(s.const, 16)
                sp.dma_start(ind[:, :], g.d_ind).then_inc(s.const, 16)
                sp.wait_ge(s.wgz, 1)
                for r in range(2):
                    sp.dma_start(wg[r * LR:(r + 1) * LR, :, r, :], g.w_gk2[0, r].rearrange("l (h d) -> l h d", h=GH)).then_inc(s.const, 16)
                    sp.dma_start(wg[2 * LR:2 * LR + 1, :, r, :], g.b_gk2[:, r, :].rearrange("l (h d) -> l h d", h=GH)).then_inc(s.const, 16)
                sp.wait_ge(s.z, 1)
                sp.dma_start(g.states[0:DK, slot_of(0, False)], g.state_f.rearrange("h k v -> k h v")).then_inc(s.init, 16)
                sp.dma_start(g.states[DK:P, slot_of(T_LAT // CH - 1, False)], g.state_b.rearrange("h k v -> k h v")).then_inc(s.init, 16)

                def step(U):
                    if T := U.at(0):
                        t, hf, par = T
                        wait(sp, s.lrp, t - 1)
                        sp.dma_start(lr[:, par, :], g.proj_tile(t)[:, LR0:D_GLA]).then_inc(s.low[par], 16)
                    if T := U.at(3):
                        t, hf, par = T
                        wait(sp, s.u, t - 1)
                        sp.dma_start(vin[:, par, :], g.proj_tile(t)[:, V0:V0 + GH * DV]).then_inc(s.vin[par], 16)
                    if T := U.at(5):
                        t, hf, par = T
                        sp.wait_ge(s.etq, t + 1)
                        sp.wait_ge(s.etk, t + 1)
                        sp.dma_start(g.qkT_tile(t), qkT[:, par].rearrange("p h a q -> p (h a q)")).then_inc(s.out[par], 16)

                steps(sp, 5, step)
                sp.wait_ge(s.out0, 16 * (NT // 2))
                sp.wait_ge(s.out1, 16 * (NT // 2))
                sp.wait_ge(s.scan, 2 * GH * NT)
                sp.dma_start(g.new_f.rearrange("h k v -> k h v"), g.states[0:DK, slot_of(T_CTX // CH, True)]).then_inc(s.fin, 16)
                sp.wait_ge(s.fin, 16)

            @block.gpsimd
            def _(pool):
                pool.memset(wg[:, :, :, :], 0.0).then_inc(s.wgz, 1)

                def step(U):
                    if T := U.at(3):
                        t, hf, par = T
                        pool.wait_ge(s.inp[par], (hf + 1) * 16)
                        pool.wait_ge(s.e3, t + 1)
                        wait(pool, s.u, t)
                        pool.tensor_tensor(ke[:, :, :, :], bc(qk[:, par, GH * DK:V0].rearrange("p (h d) -> p h d", h=GH), 2, 2),
                                           e3[:, :, :, :], ALU.mult).then_inc(s.ke, 1)

                steps(pool, 5, step)

            @block.tensor
            def _(pe):
                pe.wait_ge(s.const, 16 * 6)

                def step(U):
                    if T := U.at(3):
                        t, hf, par = T
                        pe.wait_ge(s.gate, t + 1)
                        wait(pe, s.e3, t)
                        for r in range(2):
                            pe.matmul(p_inc[:, :].rearrange("p (h r d) -> p h r d", h=GH, r=2)[:, :, r, :], tri[:, r, :], gate[:, par, :, r, :],
                                      start=r == 0, stop=True, skip_group_check=True)
                        for r in range(2):
                            last = pe.matmul(p_exc[:, :].rearrange("p (h r d) -> p h r d", h=GH, r=2)[:, :, r, :], tri[:, 2 + r, :],
                                             gate[:, par, :, r, :], start=r == 0, stop=True, skip_group_check=True)
                        last.then_inc(s.cum, 1)
                    if T := U.at(2):
                        t, hf, par = T
                        pe.wait_ge(s.lrT, t + 1)
                        wait(pe, s.mn, t)
                        pe.matmul(p_g[:, :], lrT[:, :], wg[:, :, :, :].rearrange("l h r d -> l (h r d)"), start=True, stop=True).then_inc(s.gk, 1)
                    if T := U.at(3):
                        t, hf, par = T
                        wait(pe, s.edec, t)
                        for h in range(GH):
                            last = pe.matmul(p_a[:, 256 + 2 * h:258 + 2 * h], gate[:, par, h].rearrange("p r d -> p (r d)"), ind[:, :], start=True, stop=True)
                        last.then_inc(s.dec, 1)
                    if T := U.at(4):
                        t, hf, par = T
                        pe.wait_ge(s.qt, t + 1)
                        wait(pe, s.etq, t)
                        for h in range(GH):
                            last = pe.transpose(p_q[:, h * P:(h + 1) * P], qt[:, h].rearrange("p r d -> p (r d)"), g.ident[:, :])
                        last.then_inc(s.tq, 1)
                        pe.wait_ge(s.kt, t + 1)
                        wait(pe, s.etk, t)
                        for h in range(GH):
                            last = pe.transpose(p_k[:, h * P:(h + 1) * P], kt[:, h].rearrange("p r d -> p (r d)"), g.ident[:, :])
                        last.then_inc(s.tk, 1)
                        pe.wait_ge(s.ke, t + 1)
                        pe.wait_ge(s.vin[par], (hf + 1) * 16)
                        wait(pe, s.ub, t)
                        wait(pe, s.scan, 2 * GH * t)
                        for c in range(2):
                            rows = slice(c * CH, (c + 1) * CH)
                            for h in range(GH):
                                last = pe.matmul(p_u[c][:, h * DV:(h + 1) * DV], ke[rows, h].rearrange("p r d -> p (r d)"),
                                                 vin[rows, par, h * DV:(h + 1) * DV], start=True, stop=True)
                        last.then_inc(s.u, 1)
                    if T := U.at(1):
                        t, hf, par = T
                        pe.wait_ge(s.low[par], (hf + 1) * 16)
                        wait(pe, s.edec, t - 1)
                        wait(pe, s.lrT, t)
                        pe.transpose(p_a[0:2 * LR, 0:P], lr[:, par, :], g.ident[:, :]).then_inc(s.lrp, 1)

                steps(pe, 5, step)

            @block.scalar
            def _(act):
                def step(U):
                    if T := U.at(2):
                        t, hf, par = T
                        wait(act, s.kt, t - 1)
                        wait(act, s.ke, t - 1)
                        act.dma_start(qk[:, par, :], g.proj_tile(t)[:, 0:V0]).then_inc(s.inp[par], 16)
                    if T := U.at(5):
                        t, hf, par = T
                        ctx = cond_of(t)
                        chunk = 2 * (t - N_LAT) if ctx else 2 * t
                        act.wait_ge(s.scan, 2 * GH * (t + 1))
                        act.wait_ge(s.u, t + 1)
                        for c in range(2):
                            idx = slot_of(chunk + c - 1, ctx)
                            last = act.activation(g.states[DK:P, bass.ds(idx, 1)].rearrange("p o h v -> p (o h) v"),
                                                  p_u[c][DK:P, :].rearrange("p (h v) -> p h v", h=GH), ACT.Copy)
                        last.then_inc(s.ub, 1)
                    if T := U.at(2):
                        t, hf, par = T
                        act.wait_ge(s.gk, t + 1)
                        wait(act, s.gate, t)
                        act.activation(ab[:, :], p_g[:, :], ACT.Abs).then_inc(s.ab, 1)
                        act.wait_ge(s.ab, t + 1)
                        act.activation(ab[:, :], ab[:, :], ACT.Exp, scale=-1.0).then_inc(s.ex1, 1)
                        act.wait_ge(s.ex1, t + 1)
                        act.activation(ab[:, :], ab[:, :], ACT.Ln, bias=1.0).then_inc(s.ln, 1)
                    if T := U.at(3):
                        t, hf, par = T
                        act.wait_ge(s.dec, t + 1)
                        act.activation(g.decay[:, :, bass.ds(2 * t, 2)], p_a[:, 256:256 + 2 * GH].rearrange("p (h c) -> p h c", c=2),
                                       ACT.Exp, scale=1.0 / 16).then_inc(s.edec, 1)
                        act.wait_ge(s.cum, t + 1)
                        wait(act, s.kt, t)
                        wait(act, s.ke, t)
                        r3 = lambda p: p[:, :].rearrange("p (h r d) -> p h r d", h=GH, r=2)
                        act.activation(e1[:, :, :, :], r3(p_inc), ACT.Exp, scale=1.0 / 16).then_inc(s.e1, 1)
                        act.activation(e2[:, :, :, :], r3(p_inc), ACT.Exp, scale=-1.0 / 16).then_inc(s.e2, 1)
                        act.activation(e3[:, :, :, :], r3(p_exc), ACT.Exp, scale=1.0 / 16).then_inc(s.e3, 1)
                    if T := U.at(4):
                        t, hf, par = T
                        act.wait_ge(s.tq, t + 1)
                        if not (isinstance(t, int) and t < 2):
                            act.wait_ge(s.out[par], hf * 16)
                        act.activation(qkT[:, par, :, 0, :], p_q[:, :].rearrange("p (h q) -> p h q", h=GH), ACT.Copy).then_inc(s.etq, 1)
                        act.wait_ge(s.tk, t + 1)
                        act.activation(qkT[:, par, :, 1, :], p_k[:, :].rearrange("p (h q) -> p h q", h=GH), ACT.Copy).then_inc(s.etk, 1)

                steps(act, 5, step)

            @block.vector
            def _(dve):
                last_state = slot_of(T_CTX // CH - 1, True)
                dve.memset(g.states[0:DK, slot_of(0, True)], 0.0)
                dve.memset(g.states[DK:P, last_state], 0.0)
                dve.memset(lrT[2 * LR:2 * LR + 1, :], 1.0).then_inc(s.z, 1)
                dve.wait_ge(s.z, 1)
                dve.wait_ge(s.init, 32)

                def step(U):
                    if T := U.at(5):
                        t, hf, par = T
                        ctx = cond_of(t)
                        chunk = 2 * (t - N_LAT) if ctx else 2 * t
                        dve.wait_ge(s.u, t + 1)
                        dve.wait_ge(s.edec, t + 1)
                        for c in range(2):
                            if c:
                                dve.wait_ge(s.scan, 2 * GH * t + GH)
                            else:
                                wait(dve, s.scan, 2 * GH * t)
                            for h in range(GH):
                                idx = slot_of(chunk + c, ctx)
                                state = lambda i: g.states[0:DK, bass.ds(i, 1), h, :].rearrange("p o v -> p (o v)")
                                dve.scalar_tensor_tensor(state(idx + 1), state(idx), g.decay[0:DK, h, bass.ds(2 * t + c, 1)],
                                                         p_u[c][0:DK, h * DV:(h + 1) * DV], ALU.mult, ALU.add).then_inc(s.scan, 1)
                    if T := U.at(2):
                        t, hf, par = T
                        dve.wait_ge(s.ln, t + 1)
                        dve.tensor_scalar(mn[:, :], p_g[:, :], 0.0, None, ALU.min).then_inc(s.mn, 1)
                        dve.wait_ge(s.mn, t + 1)
                        dve.tensor_tensor(gate[:, par].rearrange("p h r d -> p (h r d)"), mn[:, :], ab[:, :], ALU.subtract).then_inc(s.gate, 1)
                    if T := U.at(3):
                        t, hf, par = T
                        dve.wait_ge(s.inp[par], (hf + 1) * 16)
                        dve.tensor_scalar(qs[:, :, :], qk[:, par, 0:GH * DK].rearrange("p (h d) -> p h d", h=GH), DK ** -0.5, None,
                                          ALU.mult).then_inc(s.qs, 1)
                        dve.wait_ge(s.qs, t + 1)
                        dve.wait_ge(s.e1, t + 1)
                        wait(dve, s.tq, t)
                        dve.tensor_tensor(qt[:, :, :, :], bc(qs[:, :, :], 2, 2), e1[:, :, :, :], ALU.mult).then_inc(s.qt, 1)
                        dve.wait_ge(s.e2, t + 1)
                        wait(dve, s.tk, t)
                        dve.tensor_tensor(kt[:, :, :, :], bc(qk[:, par, GH * DK:V0].rearrange("p (h d) -> p h d", h=GH), 2, 2),
                                          e2[:, :, :, :], ALU.mult).then_inc(s.kt, 1)
                    if T := U.at(1):
                        t, hf, par = T
                        dve.wait_ge(s.lrp, t + 1)
                        wait(dve, s.gk, t)
                        dve.tensor_copy(lrT[0:2 * LR, :], p_a[0:2 * LR, 0:P]).then_inc(s.lrT, 1)

                steps(dve, 5, step)
                dve.wait_ge(s.ub, NT)


def gla_outputs(nc, g):
    with ExitStack() as stack:
        ph = Phase(nc, stack, "go")
        s = ph.s
        (s.const, s.z0, s.qk0, s.qk1, s.vo0, s.vo1, s.af, s.abk, s.mf, s.mb, s.o, s.sq, s.ss, s.ms, s.rs, s.on, s.sg,
         s.gg, s.mix, s.tr, s.et, s.st0, s.st1, s.scan, s.fin) = ph.semaphores(
            "const z0 qk0 qk1 vo0 vo1 af abk mf mb o sq ss ms rs on sg gg mix tr et st0 st1 scan fin")
        s.qk, s.vo, s.st = [s.qk0, s.qk1], [s.vo0, s.vo1], [s.st0, s.st1]
        qp = ph.sb("qp", [P, 2, GH, 4, CH])
        kT = ph.sb("kT", [P, 2, GH, P])
        vo = ph.sb("vo", [P, 2, 2 * GH * DV])
        mask = ph.sb("mask", [P, 2, P], U32)
        af = ph.sb("af", [P, 2, GH, P])
        ab = ph.sb("ab", [P, 2, GH, P])
        gg_ = ph.sb("gg_", [P, DV])
        sq = ph.sb("sq", [P, GH, DV])
        ss = ph.sb("ss", [P, GH])
        ms = ph.sb("ms", [P, GH])
        rs = ph.sb("rs", [P, GH])
        on = ph.sb("on", [P, GH, DV])
        sg = ph.sb("sg", [P, GH, DV])
        gg = ph.sb("gg", [P, GH, DV])
        mix = ph.sb("mix", [P, GH, DV])
        mT = ph.sb("mT", [P, 2, GH * P])
        p_f = ph.ps("p_f")
        p_b = ph.ps("p_b")
        p_o = [ph.ps("p_o0"), ph.ps("p_o1")]
        p_m = ph.ps("p_m")
        V0 = 2 * GH * DK

        def tile_at(t):
            if isinstance(t, int):
                return N_LAT - 1 - t if t < N_LAT else N_LAT + NT - 1 - t
            return t * -1 + (N_LAT - 1)

        def scans_behind(t):
            return t * 2 + 1 if cond_of(t) == 0 else t * 2

        with nc.Block() as block:

            @block.sync
            def _(sp):
                sp.dma_start(mask[:, :, :], g.d_mask).then_inc(s.const, 16)
                sp.dma_start(gg_[:, :], g.gla_norm_g.to_broadcast([P, DV])).then_inc(s.const, 16)
                sp.wait_ge(s.z0, 1)

                def step(U):
                    if T := U.at(4):
                        t, hf, par = T
                        sp.wait_ge(s.et, t + 1)
                        sp.dma_start(g.mix_tile(tile_at(t))[:, 0:GH * P], mT[:, par, :]).then_inc(s.st[par], 16)
                    if T := U.at(0):
                        t, hf, par = T
                        wait(sp, s.o, t - 1)
                        src = g.qkT_tile(tile_at(t)).rearrange("p (h a c q) -> p h a c q", h=GH, a=2, c=2)
                        for c in range(2):
                            sp.dma_start(qp[:, par, :, 3 * c, :], src[:, :, 0, c, :]).then_inc(s.qk[par], 16)
                        sp.dma_start(kT[:, par], g.qkT_tile(tile_at(t)).rearrange("p (h a q) -> p h a q", h=GH, a=2)[:, :, 1, :]).then_inc(s.qk[par], 16)
                        wait(sp, s.sg, t - 1)
                        sp.dma_start(vo[:, par, :], g.proj_tile(tile_at(t))[:, V0:V0 + 2 * GH * DV]).then_inc(s.vo[par], 16)

                steps(sp, 4, step)
                for par in range(2):
                    sp.wait_ge(s.st[par], 16 * (NT // 2))
                sp.wait_ge(s.scan, GH * (scans_behind(NT - 1) + 1))
                sp.dma_start(g.new_b.rearrange("h k v -> k h v"), g.states[DK:P, slot_of(-1, True)]).then_inc(s.fin, 16)
                sp.wait_ge(s.fin, 16)

            @block.gpsimd
            def _(pool):
                pool.wait_ge(s.const, 32)

                def step(U):
                    if T := U.at(2):
                        t, hf, par = T
                        pool.wait_ge(s.ms, t + 1)
                        pool.tensor_tensor(rs[:, :], ms[:, :], g.neg_half[:, 0:GH], ALU.pow).then_inc(s.rs, 1)
                    if T := U.at(1):
                        t, hf, par = T
                        pool.wait_ge(s.sg, t + 1)
                        wait(pool, s.mix, t)
                        pool.tensor_tensor(gg[:, :, :], sg[:, :, :], bc(gg_[:, :], 1, GH), ALU.mult).then_inc(s.gg, 1)

                steps(pool, 4, step)

            @block.tensor
            def _(pe):
                def step(U):
                    if T := U.at(1):
                        t, hf, par = T
                        pe.wait_ge(s.qk[par], (hf + 1) * 48)
                        wait(pe, s.mf, t)
                        for r, (bank, done, free) in enumerate(((p_f, s.af, s.mf), (p_b, s.abk, s.mb))):
                            wait(pe, free, t)
                            rows = slice(r * DK, (r + 1) * DK)
                            for h in range(GH):
                                last = pe.matmul(bank[:, h * P:(h + 1) * P], kT[rows, par, h, :], qp[rows, par, h, 0:4:3, :], start=True, stop=True)
                            last.then_inc(done, 1)
                    if T := U.at(3):
                        t, hf, par = T
                        pe.wait_ge(s.mix, t + 1)
                        wait(pe, s.et, t)
                        for h in range(GH):
                            last = pe.transpose(p_m[:, h * P:(h + 1) * P], mix[:, h, :], g.ident[:, :])
                        last.then_inc(s.tr, 1)
                    if T := U.at(1):
                        t, hf, par = T
                        pe.wait_ge(s.mf, t + 1)
                        pe.wait_ge(s.mb, t + 1)
                        pe.wait_ge(s.vo[par], (hf + 1) * 16)
                        wait(pe, s.on, t - 1)
                        pe.wait_ge(s.scan, GH * scans_behind(t))
                        ctx = cond_of(t)
                        chunk = 2 * (tile_at(t) - N_LAT) if ctx else 2 * tile_at(t)
                        for h in range(GH):
                            out = p_o[par][:, h * DV:(h + 1) * DV]
                            v = vo[:, par, h * DV:(h + 1) * DV]
                            pe.matmul(out, af[:, par, h, :], v, start=True, stop=False)
                            pe.matmul(out, ab[:, par, h, :], v, start=False, stop=False)
                            for c in range(2):
                                last = pe.matmul(out, qp[:, par, h, 2 * c:2 * c + 2, :].rearrange("p a q -> p (a q)"),
                                                 g.states[:, bass.ds(slot_of(chunk + c, ctx), 1), h, :].rearrange("p o v -> p (o v)"),
                                                 start=False, stop=c == 1)
                        last.then_inc(s.o, 1)

                steps(pe, 4, step)

            @block.scalar
            def _(act):
                def step(U):
                    if T := U.at(2):
                        t, hf, par = T
                        act.wait_ge(s.o, t + 1)
                        wait(act, s.ss, t)
                        act.activation(sq[:, :, :].rearrange("p h v -> p (h v)"), p_o[par][:, :], ACT.Square).then_inc(s.sq, 1)
                    if T := U.at(1):
                        t, hf, par = T
                        act.wait_ge(s.vo[par], (hf + 1) * 16)
                        wait(act, s.gg, t)
                        act.activation(sg[:, :, :].rearrange("p h v -> p (h v)"), vo[:, par, GH * DV:2 * GH * DV], ACT.Silu).then_inc(s.sg, 1)
                    if T := U.at(3):
                        t, hf, par = T
                        act.wait_ge(s.tr, t + 1)
                        if not (isinstance(t, int) and t < 2):
                            act.wait_ge(s.st[par], hf * 16)
                        act.activation(mT[:, par, :], p_m[:, :], ACT.Copy).then_inc(s.et, 1)

                steps(act, 4, step)

            @block.vector
            def _(dve):
                dve.memset(qp[:, :, :, 1:3, :], 0.0).then_inc(s.z0, 1)
                dve.wait_ge(s.const, 32)

                def backwards(chunk, ctx, before):
                    wait(dve, s.scan, before * GH)
                    idx = slot_of(chunk, ctx)
                    at = (T_LAT // CH if ctx else 0) + chunk
                    for h in range(GH):
                        state = lambda i: g.states[DK:P, bass.ds(i, 1), h, :].rearrange("p o v -> p (o v)")
                        dve.scalar_tensor_tensor(state(idx - 1), state(idx), g.decay[DK:P, h, bass.ds(at, 1)],
                                                 state(idx - 1), ALU.mult, ALU.add).then_inc(s.scan, 1)

                def step(U):
                    if T := U.at(1):
                        t, hf, par = T
                        for r, (bank, done, to, got) in enumerate(((p_f, s.mf, af, s.af), (p_b, s.mb, ab, s.abk))):
                            dve.wait_ge(got, t + 1)
                            wait(dve, s.o, t - 1)
                            dve.tensor_tensor(to[:, par].bitcast(U32), bank[:, :].rearrange("p (h q) -> p h q", h=GH).bitcast(U32),
                                              bc(mask[:, r, :], 1, GH), ALU.bitwise_and).then_inc(done, 1)
                    if T := U.at(2):
                        t, hf, par = T
                        dve.wait_ge(s.sq, t + 1)
                        dve.tensor_reduce(ss[:, :], sq[:, :, :], AX.X, ALU.add).then_inc(s.ss, 1)
                        dve.wait_ge(s.ss, t + 1)
                        dve.tensor_scalar(ms[:, :], ss[:, :], 1.0 / DV, EPS, ALU.mult, ALU.add).then_inc(s.ms, 1)
                        dve.wait_ge(s.rs, t + 1)
                        dve.tensor_tensor(on[:, :, :], p_o[par][:, :].rearrange("p (h v) -> p h v", h=GH), bc(rs[:, :], 2, DV),
                                          ALU.mult).then_inc(s.on, 1)
                        dve.wait_ge(s.on, t + 1)
                        dve.wait_ge(s.gg, t + 1)
                        wait(dve, s.tr, t)
                        dve.tensor_tensor(mix[:, :, :], on[:, :, :], gg[:, :, :], ALU.mult).then_inc(s.mix, 1)
                    if T := U.at(0):
                        t, hf, par = T
                        ctx = cond_of(t)
                        chunk = 2 * (tile_at(t) - N_LAT) if ctx else 2 * tile_at(t)
                        behind = scans_behind(t)
                        if not (isinstance(t, int) and t in (0, N_LAT)):
                            backwards(chunk + 2, ctx, behind - 2)
                        backwards(chunk + 1, ctx, behind - 1)

                steps(dve, 4, step)
                backwards(0, True, scans_behind(NT - 1))
                dve.wait_ge(s.scan, GH * (scans_behind(NT - 1) + 1))


def output_projection(nc, g):
    with ExitStack() as stack:
        ph = Phase(nc, stack, "op")
        s = ph.s
        (s.gates, s.m0, s.m1, s.x0, s.x1, s.mhi, s.mlo, s.y0, s.y1, s.g0, s.g1, s.r, s.xs0, s.xs1, s.sq, s.ms, s.rstd,
         s.xn, s.tr, s.hT, s.hs0, s.hs1, s.rows, s.mtr, s.mT, s.table) = ph.semaphores(
            "gates m0 m1 x0 x1 mhi mlo y0 y1 g0 g1 r xs0 xs1 sq ms rstd xn tr hT hs0 hs1 rows mtr mT table")
        s.m, s.x, s.y, s.gt, s.xs, s.hs = [s.m0, s.m1], [s.x0, s.x1], [s.y0, s.y1], [s.g0, s.g1], [s.xs0, s.xs1], [s.hs0, s.hs1]
        w_hi = ph.sb("w_hi", [P, KC, D_MODEL], F32R)
        w_lo = ph.sb("w_lo", [P, KC, D_MODEL], F32R)
        stage = ph.sb("stage", [P, W_STAGES, D_MODEL])
        gate = ph.sb("gate", [P, 2, D_MODEL])
        m = ph.sb("m", [P, 2, KC, P])
        mhi = ph.sb("mhi", [P, 2, KC, P], F32R)
        mlo = ph.sb("mlo", [P, 2, KC, P], F32R)
        x = ph.sb("x", [P, 2, D_MODEL])
        y = ph.sb("y", [P, D_MODEL])
        x1 = ph.sb("x1", [P, 2, D_MODEL])
        xn = ph.sb("xn", [P, D_MODEL])
        junk = ph.sb("junk", [P, D_MODEL])
        ss = ph.sb("ss", [P, 1])
        ms = ph.sb("ms", [P, 1])
        rstd = ph.sb("rstd", [P, 1])
        hT = ph.sb("hT", [P, 2, KC, P])
        modr = ph.sb("modr", [4 * KC, P])
        modT = ph.sb("modT", [P, 2, 2, KC])
        p_y = [[ph.ps(f"p_y{a}{b}") for b in range(2)] for a in range(2)]
        p_t = ph.ps("p_t", 1024)
        w_sp, w_act, w_dve = load_split_weights(ph, s, g.w_out[0], KC, D_MODEL, w_hi, w_lo, stage)

        with nc.Block() as block:

            @block.sync
            def _(sp):
                load_shift_scale(sp, g, 1, modr, s.rows)
                for c in range(2):
                    sp.dma_start(gate[:, c, :], g.mod_d[c:c + 1, 2 * D_MODEL:3 * D_MODEL].to_broadcast([P, D_MODEL])).then_inc(s.gates, 16)

                def step(U):
                    if T := U.at(0):
                        t, hf, par = T
                        wait(sp, s.mlo, t - 1)
                        sp.dma_start(m[:, par].rearrange("p k q -> p (k q)"), g.mix_tile(t)).then_inc(s.m[par], 16)
                        wait(sp, s.r, t - 1)
                        sp.dma_start(x[:, par, :], g.x_tile(t)).then_inc(s.x[par], 16)
                    if T := U.at(3):
                        t, hf, par = T
                        sp.wait_ge(s.r, t + 1)
                        sp.dma_start(g.x1_tile(t), x1[:, par, :]).then_inc(s.xs[par], 16)
                    if U.first(1):
                        w_sp(sp)

                steps(sp, 4, step)
                for par in range(2):
                    sp.wait_ge(s.xs[par], 16 * (NT // 2))

            @block.gpsimd
            def _(pool):
                def step(U):
                    if T := U.at(2):
                        t, hf, par = T
                        pool.wait_ge(s.ms, t + 1)
                        pool.tensor_tensor(rstd[:, :], ms[:, :], g.neg_half[:, 0:1], ALU.pow).then_inc(s.rstd, 1)
                    if T := U.at(4):
                        t, hf, par = T
                        pool.wait_ge(s.hT, t + 1)
                        pool.dma_start(g.h2_tile(t), hT[:, par]).then_inc(s.hs[par], 16)

                steps(pool, 4, step)
                for par in range(2):
                    pool.wait_ge(s.hs[par], 16 * (NT // 2))

            @block.tensor
            def _(pe):
                pe.wait_ge(s.rows, 32)
                pe.transpose(p_t[:, 0:4 * KC], modr[:, :], g.ident[0:4 * KC, 0:4 * KC]).then_inc(s.mtr, 1)

                def step(U):
                    if T := U.at(1):
                        t, hf, par = T
                        pe.wait_ge(s.mlo, t + 1)
                        for n in range(2):
                            wait(pe, s.gt[n], t - 1)
                            for k in range(KC):
                                if isinstance(t, int) and t == 0 and n == 0:
                                    pe.wait_ge(s.w_lo, k + 1)
                                last = split_product(pe, p_y[par][n][:, :], ((mhi[:, par, k], mlo[:, par, k]),
                                                     (w_hi[:, k, n * 512:(n + 1) * 512], w_lo[:, k, n * 512:(n + 1) * 512])),
                                                     k == 0, k == KC - 1)
                            last.then_inc(s.y[n], 1)
                    if T := U.at(3):
                        t, hf, par = T
                        if isinstance(t, int) and t == 0:
                            pe.wait_ge(s.table, 1)
                        pe.wait_ge(s.xn, t + 1)
                        wait(pe, s.hT, t)
                        for k in range(KC):
                            last = pe.transpose(p_t[:, k * P:(k + 1) * P], xn[:, k * P:(k + 1) * P], g.ident[:, :])
                        last.then_inc(s.tr, 1)

                steps(pe, 4, step)

            @block.scalar
            def _(act):

                def step(U):
                    if T := U.at(0):
                        t, hf, par = T
                        act.wait_ge(s.m[par], (hf + 1) * 16)
                        wait(act, s.y[1], t - 1)
                        act.activation(mhi[:, par], m[:, par], ACT.Copy).then_inc(s.mhi, 1)
                    if T := U.at(2):
                        t, hf, par = T
                        act.wait_ge(s.r, t + 1)
                        wait(act, s.ms, t)
                        act.activation(junk[:, :], x1[:, par, :], ACT.Square, accum_out=ss[:, :]).then_inc(s.sq, 1)
                    if T := U.at(3):
                        t, hf, par = T
                        if isinstance(t, int) and t == 0:
                            act.wait_ge(s.table, 1)
                        act.wait_ge(s.tr, t + 1)
                        if not (isinstance(t, int) and t < 2):
                            act.wait_ge(s.hs[par], hf * 16)
                        c = cond_of(t)
                        for k in range(KC):
                            last = act.activation(hT[:, par, k, :], p_t[:, k * P:(k + 1) * P], ACT.Identity,
                                                  bias=g.lnp[:, 1, c, 1, k:k + 1], scale=g.lnp[:, 1, c, 0, k:k + 1])
                        last.then_inc(s.hT, 1)
                    if U.first(1):
                        w_act(act)

                steps(act, 4, step)

            @block.vector
            def _(dve):
                dve.wait_ge(s.mtr, 1)
                norm_table(dve, g, 1, p_t[:, 0:4 * KC], modT, s.mT, s.table)
                dve.wait_ge(s.gates, 32)

                def step(U):
                    if T := U.at(0):
                        t, hf, par = T
                        dve.wait_ge(s.mhi, t + 1)
                        dve.tensor_tensor(mlo[:, par], m[:, par], mhi[:, par].bitcast(F32), ALU.subtract).then_inc(s.mlo, 1)
                    if T := U.at(2):
                        t, hf, par = T
                        c = cond_of(t)
                        for n in range(2):
                            dve.wait_ge(s.y[n], t + 1)
                            cols = slice(n * 512, (n + 1) * 512)
                            dve.tensor_tensor(y[:, cols], p_y[par][n][:, :], gate[:, c, cols], ALU.mult).then_inc(s.gt[n], 1)
                        dve.wait_ge(s.gt[0], t + 1)
                        dve.wait_ge(s.gt[1], t + 1)
                        dve.wait_ge(s.x[par], (hf + 1) * 16)
                        if not (isinstance(t, int) and t < 2):
                            dve.wait_ge(s.xs[par], hf * 16)
                        dve.tensor_tensor(x1[:, par, :], y[:, :], x[:, par, :], ALU.add).then_inc(s.r, 1)
                        dve.wait_ge(s.sq, t + 1)
                        dve.tensor_scalar(ms[:, :], ss[:, :], 1.0 / D_MODEL, EPS, ALU.mult, ALU.add).then_inc(s.ms, 1)
                        dve.wait_ge(s.rstd, t + 1)
                        wait(dve, s.tr, t)
                        dve.tensor_scalar(xn[:, :], x1[:, par, :], rstd[:, :], None, ALU.mult).then_inc(s.xn, 1)
                    if U.first(1):
                        w_dve(dve)

                steps(dve, 4, step)


def feed_forward(nc, g):
    BT = 512
    BTT = BT // P
    HN = 512
    KG = 4
    DOWN = [(n, k, min(k + KG, NF)) for n in range(2) for k in range(0, NF, KG)]
    ITEMS = NF + len(DOWN)
    N_LB = T_LAT // BT
    with ExitStack() as stack:
        ph = Phase(nc, stack, "ff")
        s = ph.s
        (s.w0, s.w1, s.w_hi, s.w_lo, s.h0, s.h1, s.h_hi, s.h_lo, s.fing, s.x, s.a, s.used, s.silu, s.mul, s.ghi, s.glo,
         s.y, s.gt, s.res, s.sq, s.ms, s.rs, s.fin, s.out) = ph.semaphores(
            "w0 w1 w_hi w_lo h0 h1 h_hi h_lo fing x a used silu mul ghi glo y gt res sq ms rs fin out")
        s.w = [s.w0, s.w1]
        ws = ph.sb("ws", [P, 2, 2 * KC * P])
        whi = ph.sb("whi", [P, 2, 2 * KC * P], F32R)
        wlo = ph.sb("wlo", [P, 2, 2 * KC * P], F32R)
        hs = ph.sb("hs", [P, 2, BT])
        hhi = ph.sb("hhi", [P, KC, BT], F32R)
        hlo = ph.sb("hlo", [P, KC, BT], F32R)
        ghi = ph.sb("ghi", [P, NF, BT], F32R)
        glo = ph.sb("glo", [P, NF, BT], F32R)
        sil = ph.sb("sil", [P, 2, BT])
        tmp = ph.sb("tmp", [P, HN])
        x1 = ph.sb("x1", [P, BTT, D_MODEL])
        gate = ph.sb("gate", [P, D_MODEL])
        fing = ph.sb("fing", [P, D_MODEL])
        ss = ph.sb("ss", [P, BTT])
        ms = ph.sb("ms", [P, BTT])
        rs = ph.sb("rs", [P, BTT])
        bank = [ph.ps(f"p{j}") for j in range(8)]
        w13 = [w[0].rearrange("(k p) n -> p k n", p=P) for w in (g.w_ffn1, g.w_ffn3)]
        w2 = g.w_ffn2[0].rearrange("(k p) n -> p k n", p=P)

        def width(b):
            return T_CTX if isinstance(b, int) and b == N_LB else BT

        def blocks(eng, body):
            body(0)
            with eng.Fori(1, N_LB - 1) as b:
                body(b)
            body(N_LB - 1)
            body(N_LB)

        def up_items(eng, b, body):
            for par in range(2):
                body(par, par, b * ITEMS + par, b * (ITEMS // 2))
            with eng.Fori(1, NF // 2) as i:
                for par in range(2):
                    body(i * 2 + par, par, b * ITEMS + i * 2 + par, b * (ITEMS // 2) + i)

        def down_items(b, body):
            for i, (n, k0, k1) in enumerate(DOWN):
                body(i, n, k0, k1, i % 2, b * ITEMS + (NF + i), b * (ITEMS // 2) + (NF + i) // 2)

        def h_source(b, k):
            return x1[:, k // 2, k % 2 * BT:(k % 2 + 1) * BT] if isinstance(b, int) and b == 0 else hs[:, k % 2, 0:width(b)]

        def h_rows(i):
            return range(2 * (i - 1), 2 * i) if 1 <= i <= KC // 2 else ()

        with nc.Block() as block:

            @block.sync
            def _(sp):
                def load_h(b, k):
                    if isinstance(b, int) and b == 0:
                        sp.dma_start(x1[:, k // 2, k % 2 * BT:(k % 2 + 1) * BT], g.h2_rows(b, k, BT)).then_inc([s.h0, s.h1][k % 2], 16)
                        return
                    wait(sp, s.h_lo, b * KC + (k - 1))
                    sp.dma_start(hs[:, k % 2, 0:width(b)], g.h2_rows(b, k, width(b))).then_inc([s.h0, s.h1][k % 2], 16)

                def body(b):
                    def up(f, par, item, pair):
                        wait(sp, s.w_lo, item - 1)
                        for j in range(2):
                            sp.dma_start(ws[:, par, j * KC * P:(j + 1) * KC * P].rearrange("p (k n) -> p k n", k=KC),
                                         w13[j][:, :, bass.ds(f * P, P)]).then_inc(s.w[par], 16)
                        if isinstance(b, int) and b == 0 and isinstance(f, int) and f == 0:
                            for k in range(KC):
                                load_h(0, k)

                    def down(i, n, k0, k1, par, item, pair):
                        wait(sp, s.w_lo, item - 1)
                        mid = (k0 + k1) // 2
                        for ka, kb in ((k0, mid), (mid, k1)):
                            sp.dma_start(ws[:, par, (ka - k0) * HN:(kb - k0) * HN].rearrange("p (k n) -> p k n", n=HN),
                                         w2[:, ka:kb, n * HN:(n + 1) * HN]).then_inc(s.w[par], 16)
                        if not (isinstance(b, int) and b == N_LB):
                            for k in h_rows(i):
                                load_h(b + 1, k)

                    up_items(sp, b, up)
                    down_items(b, down)

                blocks(sp, body)

            @block.gpsimd
            def _(pool):
                pool.dma_start(fing[:, :], g.final_g.rearrange("(a n) -> a n", a=1).to_broadcast([P, D_MODEL])).then_inc(s.fing, 16)

                def body(b):
                    nt = width(b) // P
                    wait(pool, s.out, b * (16 * BTT))
                    if isinstance(b, int) and b == 0:
                        pool.wait_ge(s.h_lo, KC)
                    pool.dma_start(x1[:, 0:nt, :], g.x1_rows(b, width(b))).then_inc(s.x, 16)
                    pool.dma_start(gate[:, :], g.gate2(b)).then_inc(s.x, 16)
                    for t in range(nt):
                        pool.wait_ge(s.ms, b * BTT + (t + 1))
                        pool.tensor_tensor(rs[:, t:t + 1], ms[:, t:t + 1], g.neg_half[:, 0:1], ALU.pow).then_inc(s.rs, 1)
                    for t in range(nt):
                        pool.wait_ge(s.fin, b * BTT + (t + 1))
                        pool.dma_start(g.y_rows(b, t), x1[:, t, :]).then_inc(s.out, 16)

                blocks(pool, body)
                pool.wait_ge(s.out, 16 * NT)

            @block.tensor
            def _(pe):
                def body(b):
                    bt = width(b)
                    nt = bt // P

                    def up(f, par, item, pair):
                        pe.wait_ge(s.w_lo, item + 1)
                        if isinstance(f, int) and f == 0:
                            if not (isinstance(b, int) and b == 0):
                                pe.wait_ge(s.h_lo, b * KC + KC)
                        if isinstance(f, int) and f < 2:
                            wait(pe, s.res, b * (2 * BTT) - (2 - 2 * f))
                        wait(pe, s.glo, b * NF + (f - 1))
                        for j in range(2):
                            for k in range(KC):
                                if isinstance(b, int) and b == 0 and isinstance(f, int) and f == 0 and j == 0:
                                    pe.wait_ge(s.h_lo, k + 1)
                                c = slice((j * KC + k) * P, (j * KC + k + 1) * P)
                                last = split_product(pe, bank[2 * par + j][:, 0:bt], ((whi[:, par, c], wlo[:, par, c]),
                                                     (hhi[:, k, 0:bt], hlo[:, k, 0:bt])), k == 0, k == KC - 1)
                            last.then_inc(s.used if j else s.a, 1)

                    def down(i, n, k0, k1, par, item, pair):
                        pe.wait_ge(s.w_lo, item + 1)
                        pe.wait_ge(s.glo, b * NF + (k1 if n == 0 else NF))
                        last_item = k1 == NF
                        order = [(k, t) for t in range(nt) for k in range(k0, k1)] if last_item else \
                                [(k, t) for k in range(k0, k1) for t in range(nt)]
                        for k, t in order:
                            c = slice((k - k0) * HN, (k - k0 + 1) * HN)
                            q = slice(t * P, (t + 1) * P)
                            last = split_product(pe, bank[4 * (1 - n) + t][:, :], ((ghi[:, k, q], glo[:, k, q]),
                                                 (whi[:, par, c], wlo[:, par, c])), k == 0, k == NF - 1)
                            if k == NF - 1 and t < nt - 1:
                                last.then_inc(s.y, 1)
                        last.then_inc(s.used, 1)

                    up_items(pe, b, up)
                    down_items(b, down)

                blocks(pe, body)

            def weights_high(act, par, item, pair, cols):
                act.wait_ge(s.w[par], pair * 32 + 32)
                wait(act, s.used, item - 1)
                act.activation(whi[:, par, 0:cols], ws[:, par, 0:cols], ACT.Copy).then_inc(s.w_hi, 1)

            def weights_low(dve, par, item, pair, cols):
                dve.wait_ge(s.w_hi, item + 1)
                dve.tensor_tensor(wlo[:, par, 0:cols], ws[:, par, 0:cols], whi[:, par, 0:cols].bitcast(F32), ALU.subtract).then_inc(s.w_lo, 1)

            @block.scalar
            def _(act):
                def h_high(b, k):
                    act.wait_ge([s.h0, s.h1][k % 2], b * (KC // 2 * 16) + (KC // 2 if isinstance(b, int) and b == 0 else k // 2 + 1) * 16)
                    act.activation(hhi[:, k, 0:width(b)], h_source(b, k), ACT.Copy).then_inc(s.h_hi, 1)

                def squares(b):
                    for t in range(width(b) // P):
                        act.wait_ge(s.res, b * (2 * BTT) + (width(b) // P + t + 1))
                        wait(act, s.sq, b * BTT + t)
                        act.activation(sil[:, :, :].rearrange("p a n -> p (a n)"), x1[:, t, :], ACT.Square, accum_out=ss[:, t:t + 1]).then_inc(s.sq, 1)

                def silu(b, f, par):
                    act.wait_ge(s.a, b * NF + (f + 1))
                    wait(act, s.glo, b * NF + (f - 1))
                    act.activation(sil[:, par, 0:width(b)], bank[2 * par][:, 0:width(b)], ACT.Silu).then_inc(s.silu, 1)

                def body(b):
                    def up(f, par, item, pair):
                        weights_high(act, par, item, pair, 2 * KC * P)
                        if isinstance(b, int) and b == 0 and isinstance(f, int) and f == 0:
                            for k in range(KC):
                                h_high(0, k)
                        if isinstance(f, int) and f == 0:
                            return
                        if isinstance(f, int) and f == 1 and not (isinstance(b, int) and b == 0):
                            act.wait_ge(s.glo, b * NF)
                            squares(b - 1)
                            act.wait_ge(s.sq, b * BTT)
                        silu(b, f - 1, 1 - par)

                    def down(i, n, k0, k1, par, item, pair):
                        weights_high(act, par, item, pair, (k1 - k0) * HN)
                        if i == 0:
                            silu(b, NF - 1, 1)
                        if not (isinstance(b, int) and b == N_LB):
                            for k in h_rows(i):
                                act.wait_ge(s.used, b * ITEMS + NF)
                                h_high(b + 1, k)

                    up_items(act, b, up)
                    down_items(b, down)

                blocks(act, body)
                squares(N_LB)

            @block.vector
            def _(dve):
                def h_low(b, k):
                    dve.wait_ge(s.h_hi, b * KC + (k + 1))
                    dve.tensor_tensor(hlo[:, k, 0:width(b)], h_source(b, k), hhi[:, k, 0:width(b)].bitcast(F32), ALU.subtract).then_inc(s.h_lo, 1)

                def residual(b, n):
                    nt = width(b) // P
                    cols = slice(n * HN, (n + 1) * HN)
                    for t in range(nt):
                        done = b * (2 * BTT) + (n * nt + t)
                        if t < nt - 1:
                            dve.wait_ge(s.y, b * (2 * (BTT - 1)) + (n * (nt - 1) + t + 1))
                        else:
                            dve.wait_ge(s.used, b * ITEMS + (NF + (n + 1) * (len(DOWN) // 2)))
                        wait(dve, s.res, done)
                        dve.tensor_tensor(tmp[:, :], bank[4 * (1 - n) + t][:, :], gate[:, cols], ALU.mult).then_inc(s.gt, 1)
                        dve.wait_ge(s.gt, done + 1)
                        dve.tensor_tensor(x1[:, t, cols], x1[:, t, cols], tmp[:, :], ALU.add).then_inc(s.res, 1)

                def final_norm(b):
                    for t in range(width(b) // P):
                        done = b * BTT + t
                        dve.wait_ge(s.sq, done + 1)
                        dve.tensor_scalar(ms[:, t:t + 1], ss[:, t:t + 1], 1.0 / D_MODEL, EPS, ALU.mult, ALU.add).then_inc(s.ms, 1)
                        dve.wait_ge(s.rs, done + 1)
                        dve.scalar_tensor_tensor(x1[:, t, :], x1[:, t, :], rs[:, t:t + 1], fing[:, :], ALU.mult, ALU.mult).then_inc(s.fin, 1)

                def gated(b, f, par):
                    dve.wait_ge(s.silu, b * NF + (f + 1))
                    dve.wait_ge(s.used, b * ITEMS + (f + 1))
                    bt = width(b)
                    dve.tensor_tensor(sil[:, par, 0:bt], sil[:, par, 0:bt], bank[2 * par + 1][:, 0:bt], ALU.mult).then_inc(s.mul, 1)
                    dve.wait_ge(s.mul, b * NF + (f + 1))
                    hi = ghi[:, bass.ds(f, 1), 0:bt].rearrange("p o q -> p (o q)")
                    lo = glo[:, bass.ds(f, 1), 0:bt].rearrange("p o q -> p (o q)")
                    dve.tensor_copy(hi, sil[:, par, 0:bt]).then_inc(s.ghi, 1)
                    dve.wait_ge(s.ghi, b * NF + (f + 1))
                    dve.tensor_tensor(lo, sil[:, par, 0:bt], hi.bitcast(F32), ALU.subtract).then_inc(s.glo, 1)

                def body(b):
                    def up(f, par, item, pair):
                        weights_low(dve, par, item, pair, 2 * KC * P)
                        if isinstance(b, int) and b == 0 and isinstance(f, int) and f == 0:
                            for k in range(KC):
                                h_low(0, k)
                        begin = isinstance(f, int) and not (isinstance(b, int) and b == 0)
                        if begin and f == 0:
                            residual(b - 1, 1)
                        if begin and f == 1:
                            final_norm(b - 1)
                        if not (isinstance(f, int) and f == 0):
                            gated(b, f - 1, 1 - par)

                    def down(i, n, k0, k1, par, item, pair):
                        weights_low(dve, par, item, pair, (k1 - k0) * HN)
                        if i == 0:
                            gated(b, NF - 1, 1)
                        if not (isinstance(b, int) and b == N_LB):
                            for k in h_rows(i):
                                h_low(b + 1, k)
                        if i == len(DOWN) // 2 + 1:
                            dve.wait_ge(s.x, b * 32 + 32)
                            residual(b, 0)

                    up_items(dve, b, up)
                    down_items(b, down)

                dve.wait_ge(s.fing, 16)
                blocks(dve, body)
                residual(N_LB, 1)
                final_norm(N_LB)


def hybrid_block(nc, a, outs, consts):
    with ExitStack() as top:
        g = Names()
        (g.c, g.c_ctx, g.ada_w, g.ada_b, g.norm1_g, g.norm2_g, g.w_in, g.w_gk2, g.b_gk2, g.gla_norm_g, g.q_norm_g, g.k_norm_g,
         g.w_out, g.w_ffn1, g.w_ffn3, g.w_ffn2, g.final_g) = (a[name] for name in _INS[6:])
        g.d_ident, g.d_tri, g.d_ind, g.d_mask, d_rope = consts
        y_prompt, y_sample, new_k, new_v, new_f, new_b = outs
        g.new_k = new_k.rearrange("b l t h d -> (b l t) (h d)")
        g.new_v = new_v.rearrange("b l t h d -> (b l t) (h d)")
        g.new_f, g.new_b = new_f[0, 0], new_b[0, 0]
        g.cache_k = a["cache_k"].rearrange("b l t h d -> (b l t) (h d)")
        g.cache_v = a["cache_v"].rearrange("b l t h d -> (b l t) (h d)")
        g.state_f, g.state_b = a["state_gla_fwd"][0, 0], a["state_gla_bwd"][0, 0]

        def scratch(name, shape, dt=F32):
            return nc.dram_tensor(name, shape, dt, kind="Internal").ap()

        g.mod_d = scratch("mod_d", (2, N_MOD * D_MODEL))
        qT_d = scratch("qT_d", (NT, P, AH * P))
        mix_d = scratch("mix_d", (NT, P, KC * P))
        proj_d = scratch("proj_d", (NT * P, D_GLA))
        qkT_d = scratch("qkT_d", (NT, P, 2 * GH * P))
        x1_d = scratch("x1_d", (NT * P, D_MODEL))
        h2_d = scratch("h2_d", (KC, P, NT * P))

        def tile_of(d):
            return lambda t: d[bass.ds(t, 1)].rearrange("o p n -> (o p) n")

        def rows_of(lat, ctx):
            return lambda t: ctx[(t - N_LAT) * P:(t - N_LAT + 1) * P, :] if cond_of(t) else lat[bass.ds(t * P, P), :]

        g.qT_tile, g.mix_tile, g.qkT_tile = tile_of(qT_d), tile_of(mix_d), tile_of(qkT_d)
        g.hT_tile = tile_of(scratch("hT_d", (NT, P, KC * P)))
        g.proj_tile = lambda t: proj_d[bass.ds(t * P, P), :]
        g.rope_tile = lambda t: d_rope[bass.ds(t * P, P), :]
        g.x1_tile = lambda t: x1_d[bass.ds(t * P, P), :]
        g.x_tile = rows_of(a["x_sample"][0], a["x_prompt"][0])
        g.h2_tile = lambda t: h2_d[:, :, bass.ds(t * P, P)].rearrange("k p q -> p k q")
        g.h2_rows = lambda b, k, n: h2_d[k, :, bass.ds(b * 512, n)]
        g.x1_rows = lambda b, n: x1_d[bass.ds(b * 512, n), :].rearrange("(t p) n -> p t n", p=P)
        y_tile = rows_of(y_sample[0], y_prompt[0])
        g.y_rows = lambda b, t: y_tile(b * 4 + t)

        def gate2(b):
            c = 1 if isinstance(b, int) and b == T_LAT // 512 else 0
            return g.mod_d[c:c + 1, 5 * D_MODEL:6 * D_MODEL].to_broadcast([P, D_MODEL])

        g.gate2 = gate2
        g.ident = top.enter_context(nc.sbuf_tensor("ident", [P, P], F32))
        g.lnp = top.enter_context(nc.sbuf_tensor("lnp", [P, 2, 2, 2, KC], F32))
        g.neg_half = top.enter_context(nc.sbuf_tensor("neg_half", [P, 16], F32))
        g.cT = top.enter_context(nc.sbuf_tensor("cT", [P, 2 * KC], F32))
        g.nT = top.enter_context(nc.sbuf_tensor("nT", [P, 2 * KC], F32))
        modulation(nc, g)
        with ExitStack() as att:
            g.keysT = att.enter_context(nc.sbuf_tensor("keysT", [P, KVH, 2, (N_LAT + 4) * P], F32R))
            g.vals = att.enter_context(nc.sbuf_tensor("vals", [P, (N_LAT + 4) * KVH, 2 * HD], F32R))
            attention_projection(nc, g)
            attention(nc, g)
        gla_projection(nc, g)
        with ExitStack() as gla:
            g.states = gla.enter_context(nc.sbuf_tensor("states", [P, SLOTS, GH, DV], F32))
            g.decay = gla.enter_context(nc.sbuf_tensor("decay", [P, GH, NT * 2], F32))
            gla_states(nc, g)
            gla_outputs(nc, g)
        output_projection(nc, g)
        feed_forward(nc, g)


_INS = ["x_prompt", "x_sample", "cache_k", "cache_v", "state_gla_fwd", "state_gla_bwd", "c", "c_ctx", "ada_w", "ada_b", "norm1_g",
        "norm2_g", "w_in", "w_gk2", "b_gk2", "gla_norm_g", "q_norm_g", "k_norm_g", "w_out", "w_ffn1", "w_ffn3", "w_ffn2", "final_g"]
_OUTS = [(1, T_CTX, D_MODEL), (1, T_LAT, D_MODEL), (1, 1, T_CTX, KVH, HD), (1, 1, T_CTX, KVH, HD), (1, 1, GH, DK, DV), (1, 1, GH, DK, DV)]


def _constants():
    j, i = np.meshgrid(np.arange(P), np.arange(P), indexing="ij")
    same = (i // CH) == (j // CH)
    tri = np.stack([same & (j <= i), same & (j >= i), same & (j > i), same & (j < i)], axis=1).astype(np.float32)
    ind = ((np.arange(P)[:, None] // CH) == np.arange(2)[None, :]).astype(np.float32)
    t = np.arange(T_LAT)
    half = HD // 4
    inv = (np.float32(10000.0) ** (-np.arange(0, 2 * half, 2, dtype=np.float32) / np.float32(2 * half))).astype(np.float32)
    pos = np.stack([t // GRID_W, t % GRID_W], axis=1).astype(np.float32)
    ang = pos[:, :, None] * inv
    c, sn = np.cos(ang), np.sin(ang)
    rope = np.zeros((NT * P, 2, 2, 2, half), np.float32)
    rope[:, 0] = 1.0
    rope[:T_LAT, 0] = c[:, :, None, :]
    rope[:T_LAT, 1, :, 0] = -sn
    rope[:T_LAT, 1, :, 1] = sn
    bits = np.where(tri[:, 0:2] > 0, np.uint32(0xFFFFFFFF), np.uint32(0))
    return [np.eye(P, dtype=np.float32), tri, ind, bits, rope.reshape(NT * P, 2 * HD)]


def lay_out(nc, inputs):
    arrays, args, outs, consts = {}, {}, [], []
    for name in _INS:
        x = np.ascontiguousarray(inputs[name])
        arrays[f"in_{name}_dram"] = x
        args[name] = nc.dram_tensor(f"in_{name}_dram", x.shape, mybir.dt.from_np(x.dtype), kind="ExternalInput").ap()
    for n, x in enumerate(_constants()):
        arrays[f"const_{n}_dram"] = x
        consts.append(nc.dram_tensor(f"const_{n}_dram", x.shape, mybir.dt.from_np(x.dtype), kind="ExternalInput").ap())
    for n, shape in enumerate(_OUTS):
        outs.append(nc.dram_tensor(f"out_{n}_dram", shape, F32, kind="ExternalOutput").ap())
    hybrid_block(nc, args, outs, consts)
    return arrays


def kernel(**inputs):
    import concourse.bacc as _bacc
    from concourse.bass_utils import run_bass_kernel_spmd as _run

    nc = _bacc.Bacc("TRN2", target_bir_lowering=False, num_devices=1)
    arrays = lay_out(nc, inputs)
    r = _run(nc, [arrays], core_ids=[0])
    return tuple(r.results[0][f"out_{n}_dram"] for n in range(len(_OUTS)))
```
